# Optimizing a Trainium2 kernel written in Bass

```python
import math
import jax
import jax.numpy as jnp
from jax import lax
import numpy as np
import jax, jax.numpy as jnp

D_MODEL = 2048
BATCH = 1
SEQ = 256
DEPTH = 1

MEM_LEN = 256
RMS_EPS = 1e-6
DN_HEAD_DIM = 128
DN_WIDTH = D_MODEL // 2
DN_HEADS = DN_WIDTH // DN_HEAD_DIM
DN_CONV = 4
DN_CHUNK = 64
RW_HEAD_DIM = 64
RW_WIDTH = D_MODEL - DN_WIDTH
RW_HEADS = RW_WIDTH // RW_HEAD_DIM
RW_DECAY_LORA = 64
RW_AAA_LORA = 64
RW_GATE_LORA = 128
RW_GN_EPS = 64e-5
DN_COLS = 4 * DN_WIDTH + 2 * DN_HEADS
RW_COLS = 3 * RW_WIDTH + RW_DECAY_LORA + RW_AAA_LORA + RW_GATE_LORA
IN_COLS = DN_COLS + RW_COLS
XA_HEADS = 4
XA_HEAD_DIM = 128
XA_WIDTH = XA_HEADS * XA_HEAD_DIM
FFN_HIDDEN = 4 * D_MODEL


def rmsnorm(x, w):
    xf = x.astype(jnp.float32)
    y = xf * lax.rsqrt(jnp.mean(xf * xf, axis=-1, keepdims=True) + RMS_EPS)
    return (y * w.astype(jnp.float32)).astype(x.dtype)

def l2norm(x):
    return x * lax.rsqrt(jnp.sum(x * x, axis=-1, keepdims=True) + 1e-6)

def causal_depthwise_conv(x, w):
    k = w.shape[0]
    return lax.conv_general_dilated(
        x, w[:, None, :].astype(x.dtype), window_strides=(1,), padding=[(k - 1, 0)],
        dimension_numbers=('NWC', 'WIO', 'NWC'), feature_group_count=x.shape[-1])

def token_shift(p):
    return jnp.pad(p, ((0, 0), (1, 0), (0, 0)))[:, :-1]

def chunked_gated_delta_rule(q, k, v, g, beta):
    b, s, h, dk = q.shape
    dv = v.shape[-1]
    c = DN_CHUNK
    n = s // c

    def chunks(t):
        return t.reshape(b, n, c, h, -1).transpose(0, 3, 1, 2, 4)

    q = chunks(q) * (dk ** -0.5)
    k = chunks(k)
    v = chunks(v)
    g = g.reshape(b, n, c, h).transpose(0, 3, 1, 2)
    beta = beta.reshape(b, n, c, h).transpose(0, 3, 1, 2)
    gc = jnp.cumsum(g, axis=-1)
    idx = jnp.arange(c)
    causal = idx[:, None] >= idx[None, :]
    strict = idx[:, None] > idx[None, :]
    decay = jnp.exp(jnp.where(causal, gc[..., :, None] - gc[..., None, :], -jnp.inf))
    kb = k * beta[..., None]
    a_strict = jnp.where(strict, jnp.einsum('bhncd,bhnmd->bhncm', kb, k) * decay, 0.0)
    lower = a_strict + jnp.eye(c, dtype=q.dtype)
    rhs = jnp.concatenate([v * beta[..., None], kb * jnp.exp(gc)[..., None]], axis=-1)
    sol = lax.linalg.triangular_solve(lower, rhs, left_side=True, lower=True)
    u, w = sol[..., :dv], sol[..., dv:]
    attn = jnp.einsum('bhncd,bhnmd->bhncm', q, k) * decay
    qg = q * jnp.exp(gc)[..., None]
    g_last = gc[..., -1]
    kd = k * jnp.exp(g_last[..., None] - gc)[..., None]
    xs = tuple(jnp.moveaxis(t, 2, 0) for t in (u, w, qg, attn, kd, g_last))

    def step(state, xs_n):
        u_n, w_n, qg_n, attn_n, kd_n, gl_n = xs_n
        v_new = u_n - jnp.einsum('bhcd,bhde->bhce', w_n, state)
        o_n = jnp.einsum('bhcd,bhde->bhce', qg_n, state) + jnp.einsum('bhcm,bhme->bhce', attn_n, v_new)
        state = state * jnp.exp(gl_n)[..., None, None] + jnp.einsum('bhcd,bhce->bhde', kd_n, v_new)
        return state, o_n

    s0 = jnp.zeros((b, h, dk, dv), q.dtype)
    _, o = lax.scan(step, s0, xs)
    return o.transpose(1, 0, 3, 2, 4).reshape(b, s, h, dv)

def wkv7_scan(r, w, k, v, kk, a):
    b, s, h, nd = r.shape
    xs = tuple(jnp.swapaxes(t, 0, 1) for t in (r, w, k, v, kk, a))

    def step(state, xs_t):
        r_t, w_t, k_t, v_t, kk_t, a_t = xs_t
        sa = jnp.einsum('bhvk,bhk->bhv', state, -kk_t)
        state = (state * w_t[:, :, None, :] + sa[..., None] * (kk_t * a_t)[:, :, None, :]
                 + v_t[..., None] * k_t[:, :, None, :])
        return state, jnp.einsum('bhvk,bhk->bhv', state, r_t)

    s0 = jnp.zeros((b, h, nd, nd), r.dtype)
    _, y = lax.scan(step, s0, xs)
    return jnp.swapaxes(y, 0, 1)

def deltanet_group(p, conv_w, a_log, dt_bias, norm_w):
    p = p.astype(jnp.float32)
    b, s, _ = p.shape
    qkv, z, ga, gb = jnp.split(p, [3 * DN_WIDTH, 4 * DN_WIDTH, 4 * DN_WIDTH + DN_HEADS], axis=-1)
    qkv = jax.nn.silu(causal_depthwise_conv(qkv, conv_w))
    q, k, v = (t.reshape(b, s, DN_HEADS, DN_HEAD_DIM) for t in jnp.split(qkv, 3, axis=-1))
    q = l2norm(q)
    k = l2norm(k)
    beta = jax.nn.sigmoid(gb)
    g = -jnp.exp(a_log) * jax.nn.softplus(ga + dt_bias)
    o = chunked_gated_delta_rule(q, k, v, g, beta)
    o = rmsnorm(o, norm_w) * jax.nn.silu(z.reshape(b, s, DN_HEADS, DN_HEAD_DIM))
    return o.reshape(b, s, DN_WIDTH)

def rwkv7_group(p, mu, w0, w2, a0, a2, g2, k_k, k_a, r_k, ln_w, ln_b):
    p = p.astype(jnp.float32)
    b, s, _ = p.shape
    p = p + (token_shift(p) - p) * mu
    pr, pk, pv, pw, pa, pg = jnp.split(
        p, [RW_WIDTH, 2 * RW_WIDTH, 3 * RW_WIDTH, 3 * RW_WIDTH + RW_DECAY_LORA,
            3 * RW_WIDTH + RW_DECAY_LORA + RW_AAA_LORA], axis=-1)

    def heads(t):
        return t.reshape(b, s, RW_HEADS, RW_HEAD_DIM)

    log_w = -jax.nn.softplus(-(w0 + jnp.tanh(pw) @ w2)) - 0.5
    decay = jnp.exp(-jnp.exp(log_w))
    a = jax.nn.sigmoid(a0 + pa @ a2)
    gate = jax.nn.sigmoid(pg) @ g2
    kk = heads(pk * k_k)
    kk = kk / jnp.maximum(jnp.sqrt(jnp.sum(kk * kk, axis=-1, keepdims=True)), 1e-12)
    k = pk * (1.0 + (a - 1.0) * k_a)
    r_h, k_h, v_h = heads(pr), heads(k), heads(pv)
    y = wkv7_scan(r_h, heads(decay), k_h, v_h, kk, heads(a))
    mean = jnp.mean(y, axis=-1, keepdims=True)
    var = jnp.mean(jnp.square(y - mean), axis=-1, keepdims=True)
    y = ((y - mean) * lax.rsqrt(var + RW_GN_EPS)).reshape(b, s, RW_WIDTH) * ln_w + ln_b
    bonus = jnp.sum(r_h * k_h * r_k, axis=-1, keepdims=True) * v_h
    return (y + bonus.reshape(b, s, RW_WIDTH)) * gate

def memory_cross_attention(hn, mn, wq, wk, wv, wo):
    b, s, _ = hn.shape
    m = mn.shape[1]
    q = (hn @ wq).reshape(b, s, XA_HEADS, XA_HEAD_DIM)
    k = (mn @ wk).reshape(b, m, XA_HEADS, XA_HEAD_DIM)
    v = (mn @ wv).reshape(b, m, XA_HEADS, XA_HEAD_DIM)
    scores = jnp.einsum('bshd,bmhd->bhsm', q, k).astype(jnp.float32) * (XA_HEAD_DIM ** -0.5)
    probs = jax.nn.softmax(scores, axis=-1).astype(v.dtype)
    o = jnp.einsum('bhsm,bmhd->bshd', probs, v).reshape(b, s, XA_WIDTH)
    return o @ wo

def squared_relu_mlp(u, w1, w2):
    return jnp.square(jax.nn.relu(u @ w1)) @ w2

def first_inputs(seed: int = 0) -> dict:
    key = jax.random.key(seed)
    ks = jax.random.split(key, 32)
    L = DEPTH
    D = D_MODEL

    def normal(i, shape, scale):
        return jax.random.normal(ks[i], shape, jnp.float32) * scale

    def uniform(i, shape, lo, hi):
        return jax.random.uniform(ks[i], shape, jnp.float32, lo, hi)

    dt = jnp.exp(uniform(6, (L, DN_HEADS), math.log(1e-3), math.log(1e-1)))
    return {
        'x': normal(0, (BATCH, SEQ, D), 1.0),
        'mem': normal(1, (BATCH, MEM_LEN, D), 1.0),
        'mix_norm_w': 1.0 + normal(2, (L, D), 0.02),
        'w_in': normal(3, (L, D, IN_COLS), D ** -0.5),
        'dn_conv_w': normal(4, (L, DN_CONV, 3 * DN_WIDTH), DN_CONV ** -0.5),
        'dn_a_log': jnp.log(uniform(5, (L, DN_HEADS), 1.0, 16.0)),
        'dn_dt_bias': dt + jnp.log(-jnp.expm1(-dt)),
        'dn_norm_w': 1.0 + normal(7, (L, DN_HEAD_DIM), 0.02),
        'rw_mu': uniform(8, (L, RW_COLS), 0.0, 1.0),
        'rw_w0': uniform(9, (L, RW_WIDTH), -6.0, 1.0),
        'rw_w2': normal(10, (L, RW_DECAY_LORA, RW_WIDTH), 0.1 * RW_DECAY_LORA ** -0.5),
        'rw_a0': normal(11, (L, RW_WIDTH), 0.1),
        'rw_a2': normal(12, (L, RW_AAA_LORA, RW_WIDTH), 0.1 * RW_AAA_LORA ** -0.5),
        'rw_g2': normal(13, (L, RW_GATE_LORA, RW_WIDTH), RW_GATE_LORA ** -0.5),
        'rw_k_k': 0.85 + normal(14, (L, RW_WIDTH), 0.02),
        'rw_k_a': 1.0 + normal(15, (L, RW_WIDTH), 0.02),
        'rw_r_k': normal(16, (L, RW_HEADS, RW_HEAD_DIM), 0.1),
        'rw_ln_w': 1.0 + normal(17, (L, RW_WIDTH), 0.02),
        'rw_ln_b': normal(18, (L, RW_WIDTH), 0.02),
        'w_out': normal(19, (L, D, D), D ** -0.5),
        'xa_norm_w': 1.0 + normal(20, (L, D), 0.02),
        'mem_norm_w': 1.0 + normal(21, (L, D), 0.02),
        'xa_wq': normal(22, (L, D, XA_WIDTH), D ** -0.5),
        'xa_wk': normal(23, (L, D, XA_WIDTH), D ** -0.5),
        'xa_wv': normal(24, (L, D, XA_WIDTH), D ** -0.5),
        'xa_wo': normal(25, (L, XA_WIDTH, D), XA_WIDTH ** -0.5),
        'ffn_norm_w': 1.0 + normal(26, (L, D), 0.02),
        'ffn_w1': normal(27, (L, D, FFN_HIDDEN), D ** -0.5),
        'ffn_w2': normal(28, (L, FFN_HIDDEN, D), FFN_HIDDEN ** -0.5),
        'final_norm_w': 1.0 + normal(29, (D,), 0.02),
    }

def first_block(x, mem, mix_norm_w, w_in, dn_conv_w, dn_a_log, dn_dt_bias, dn_norm_w, rw_mu, rw_w0,
              rw_w2, rw_a0, rw_a2, rw_g2, rw_k_k, rw_k_a, rw_r_k, rw_ln_w, rw_ln_b, w_out,
              xa_norm_w, mem_norm_w, xa_wq, xa_wk, xa_wv, xa_wo, ffn_norm_w, ffn_w1, ffn_w2,
              final_norm_w):
    h = x
    for l in range(DEPTH):
        u = rmsnorm(h, mix_norm_w[l])
        p = u @ w_in[l]
        o_dn = deltanet_group(p[..., :DN_COLS], dn_conv_w[l], dn_a_log[l], dn_dt_bias[l], dn_norm_w[l])
        o_rw = rwkv7_group(p[..., DN_COLS:], rw_mu[l], rw_w0[l], rw_w2[l], rw_a0[l], rw_a2[l], rw_g2[l],
                           rw_k_k[l], rw_k_a[l], rw_r_k[l], rw_ln_w[l], rw_ln_b[l])
        h = h + jnp.concatenate([o_dn, o_rw], axis=-1).astype(h.dtype) @ w_out[l]
        h = h + memory_cross_attention(rmsnorm(h, xa_norm_w[l]), rmsnorm(mem, mem_norm_w[l]),
                                       xa_wq[l], xa_wk[l], xa_wv[l], xa_wo[l])
        h = h + squared_relu_mlp(rmsnorm(h, ffn_norm_w[l]), ffn_w1[l], ffn_w2[l])
    return rmsnorm(h, final_norm_w)


GROUP_WIDTH = 128
HEAD_DIM = 128
D_GMLP = D_MODEL // 4
D_SB = D_MODEL // 4
D_MIX = D_GMLP + D_SB
N_GMLP_GROUPS = D_GMLP // GROUP_WIDTH
N_SB_HEADS = D_SB // HEAD_DIM
N_MIX_GROUPS = D_MIX // GROUP_WIDTH
D_IN = 2 * D_GMLP + 3 * D_SB
SPLIT_POINTS = (D_GMLP, 2 * D_GMLP, 2 * D_GMLP + D_SB, 2 * D_GMLP + 2 * D_SB)
CHUNK = 128
Q_BLOCK = 128
N_GROUPS = 4
EXPERTS_PER_GROUP = 8
N_EXPERTS = N_GROUPS * EXPERTS_PER_GROUP
TOP_K = 2
D_EXPERT = D_MODEL // 8
EXPERT_BLOCK = 128
N_MOD = 6
EPS = 1e-6


def rms_norm(x, g):
    xf = x.astype(jnp.float32)
    y = xf * lax.rsqrt(jnp.mean(xf * xf, axis=-1, keepdims=True) + EPS)
    return (y * g.astype(jnp.float32)).astype(x.dtype)

def chunked_spatial_gating(u, v, norm_g, ws, bs):
    B, S, _ = u.shape
    u = jax.nn.gelu(u, approximate=False)
    v = jax.nn.gelu(v, approximate=False).reshape(B, S // CHUNK, CHUNK, N_GMLP_GROUPS, GROUP_WIDTH)
    v = rms_norm(v, norm_g.reshape(N_GMLP_GROUPS, GROUP_WIDTH))
    w = ws * jnp.tril(jnp.ones((CHUNK, CHUNK), ws.dtype))
    s = jnp.einsum('gtp,bcpgk->bctgk', w, v) + bs.T[:, :, None]
    return u * s.reshape(B, S, D_GMLP)

def stick_breaking_attention(q, k, v):
    B, S, H, dh = q.shape
    nq = S // Q_BLOCK
    scale = HEAD_DIM ** -0.5
    qf = q.astype(jnp.float32).transpose(0, 2, 1, 3)
    kf = k.astype(jnp.float32).transpose(0, 2, 1, 3)
    vt = v.transpose(0, 2, 1, 3)
    idx = jnp.arange(Q_BLOCK, dtype=jnp.int32)
    after_in_block = (idx[:, None] > idx[None, :]).astype(jnp.float32)
    outs = []
    for n in range(nq):
        nk = n + 1
        kl = nk * Q_BLOCK
        qb = qf[:, :, n * Q_BLOCK:kl]
        z = jnp.einsum('bhqd,bhkd->bhqk', qb, kf[:, :, :kl]) * scale
        q_pos = n * Q_BLOCK + idx
        causal = jnp.arange(kl, dtype=jnp.int32)[None, :] < q_pos[:, None]
        log_fail = jnp.where(causal, jax.nn.log_sigmoid(-z), 0.0).reshape(B, H, Q_BLOCK, nk, Q_BLOCK)
        within = jnp.einsum('bhqni,ij->bhqnj', log_fail, after_in_block)
        blk = jnp.sum(log_fail, axis=-1)
        later = lax.cumsum(blk, axis=3, reverse=True) - blk
        log_a = jax.nn.log_sigmoid(z) + (within + later[..., None]).reshape(B, H, Q_BLOCK, kl)
        a = jnp.where(causal, jnp.exp(log_a), 0.0)
        outs.append(jnp.einsum('bhqk,bhkd->bhqd', a.astype(vt.dtype), vt[:, :, :kl]))
    o = jnp.concatenate(outs, axis=2)
    return o.transpose(0, 2, 1, 3).reshape(B, S, H * dh)

def hierarchical_moe(h, w_group, b_group, w_route, b_route, w_gate, w_up, w_down):
    n, d = h.shape
    hf = h.astype(jnp.float32)
    g_logits = hf @ w_group.astype(jnp.float32) + b_group.astype(jnp.float32)
    g_prob = jax.nn.softmax(g_logits, axis=-1)
    g_idx = jnp.argmax(g_logits, axis=-1).astype(jnp.int32)
    p_group = jnp.take_along_axis(g_prob, g_idx[:, None], axis=-1)
    e_logits = (hf @ w_route.astype(jnp.float32) + b_route.astype(jnp.float32)).reshape(n, N_GROUPS, EXPERTS_PER_GROUP)
    e_logits = jnp.take_along_axis(e_logits, g_idx[:, None, None], axis=1)[:, 0]
    top_val, top_idx = lax.top_k(e_logits, TOP_K)
    weights = jax.nn.softmax(top_val, axis=-1) * p_group
    expert_id = g_idx[:, None] * EXPERTS_PER_GROUP + top_idx.astype(jnp.int32)

    a = n * TOP_K
    flat_e = expert_id.reshape(a)
    flat_tok = jnp.repeat(jnp.arange(n, dtype=jnp.int32), TOP_K)
    order = jnp.argsort(flat_e)
    sorted_e = flat_e[order]
    counts = jnp.bincount(flat_e, length=N_EXPERTS).astype(jnp.int32)
    start = jnp.cumsum(counts) - counts
    padded = (counts + EXPERT_BLOCK - 1) // EXPERT_BLOCK * EXPERT_BLOCK
    pend = jnp.cumsum(padded)
    pstart = pend - padded
    rank = jnp.arange(a, dtype=jnp.int32) - start[sorted_e]
    slot = jnp.zeros((a,), jnp.int32).at[order].set((pstart[sorted_e] + rank).astype(jnp.int32))
    n_blocks = (a + EXPERT_BLOCK - 1) // EXPERT_BLOCK + N_EXPERTS
    capacity = n_blocks * EXPERT_BLOCK
    slot_tok = jnp.full((capacity,), n, jnp.int32).at[slot].set(flat_tok)
    block_e = jnp.minimum(
        jnp.searchsorted(pend, jnp.arange(n_blocks, dtype=jnp.int32) * EXPERT_BLOCK, side='right'),
        N_EXPERTS - 1).astype(jnp.int32)
    h_pad = jnp.concatenate([h, jnp.zeros((1, d), h.dtype)], axis=0)
    xs = h_pad[slot_tok].reshape(n_blocks, EXPERT_BLOCK, d)

    def expert_block(args):
        xb, e = args
        act = jax.nn.silu(xb @ w_gate[e]) * (xb @ w_up[e])
        return act @ w_down[e]

    ys = lax.map(expert_block, (xs, block_e)).reshape(capacity, d)
    picked = ys[slot].reshape(n, TOP_K, d)
    return jnp.einsum('nkd,nk->nd', picked, weights.astype(picked.dtype))

def second_inputs(seed: int = 0) -> dict:
    key = jax.random.key(seed)
    ks = jax.random.split(key, 22)
    f32 = jnp.float32
    L, D = DEPTH, D_MODEL

    def nrm(k, shape, s):
        return jax.random.normal(k, shape, f32) * s

    return {
        "x": nrm(ks[0], (BATCH, SEQ, D), 1.0),
        "c": nrm(ks[1], (BATCH, D), 1.0),
        "w_mod": nrm(ks[2], (D, N_MOD * D), 0.5 * D ** -0.5),
        "b_mod": nrm(ks[3], (N_MOD * D,), 0.02),
        "mod_layer": nrm(ks[4], (L, N_MOD * D), 0.1),
        "norm1_g": 1.0 + nrm(ks[5], (L, D), 0.02),
        "w_in": nrm(ks[6], (L, D, D_IN), D ** -0.5),
        "gm_norm_g": 1.0 + nrm(ks[7], (L, D_GMLP), 0.02),
        "gm_ws": nrm(ks[8], (L, N_GMLP_GROUPS, CHUNK, CHUNK), CHUNK ** -0.5),
        "gm_bs": 1.0 + nrm(ks[9], (L, N_GMLP_GROUPS, CHUNK), 0.1),
        "q_norm_g": 1.0 + nrm(ks[10], (L, HEAD_DIM), 0.02),
        "k_norm_g": 1.0 + nrm(ks[11], (L, HEAD_DIM), 0.02),
        "out_norm_g": 1.0 + nrm(ks[12], (L, D_MIX), 0.02),
        "w_out": nrm(ks[13], (L, D_MIX, D), D_MIX ** -0.5),
        "norm2_g": 1.0 + nrm(ks[14], (L, D), 0.02),
        "w_group": nrm(ks[15], (L, D, N_GROUPS), D ** -0.5),
        "b_group": nrm(ks[16], (L, N_GROUPS), 0.01),
        "w_route": nrm(ks[17], (L, D, N_EXPERTS), D ** -0.5),
        "b_route": nrm(ks[18], (L, N_EXPERTS), 0.01),
        "w_gate": nrm(ks[19], (L, N_EXPERTS, D, D_EXPERT), D ** -0.5),
        "w_up": nrm(ks[20], (L, N_EXPERTS, D, D_EXPERT), D ** -0.5),
        "w_down": nrm(ks[21], (L, N_EXPERTS, D_EXPERT, D), D_EXPERT ** -0.5),
    }

def second_block(x, c, w_mod, b_mod, mod_layer, norm1_g, w_in, gm_norm_g, gm_ws, gm_bs,
              q_norm_g, k_norm_g, out_norm_g, w_out, norm2_g, w_group, b_group,
              w_route, b_route, w_gate, w_up, w_down):
    B, S, D = x.shape
    mod_shared = jax.nn.silu(c) @ w_mod + b_mod
    for l in range(DEPTH):
        mod = (mod_shared + mod_layer[l])[:, None, :]
        shift1, scale1, gate1, shift2, scale2, gate2 = jnp.split(mod, N_MOD, axis=-1)

        h = rms_norm(x, norm1_g[l]) * (1.0 + scale1) + shift1
        proj = h @ w_in[l]
        u_a, v_a, q, k, v = jnp.split(proj, SPLIT_POINTS, axis=-1)
        y_a = chunked_spatial_gating(u_a, v_a, gm_norm_g[l], gm_ws[l], gm_bs[l])
        q = rms_norm(q.reshape(B, S, N_SB_HEADS, HEAD_DIM), q_norm_g[l])
        k = rms_norm(k.reshape(B, S, N_SB_HEADS, HEAD_DIM), k_norm_g[l])
        v = v.reshape(B, S, N_SB_HEADS, HEAD_DIM)
        y_b = stick_breaking_attention(q, k, v)
        y = jnp.concatenate([y_a, y_b], axis=-1).reshape(B, S, N_MIX_GROUPS, GROUP_WIDTH)
        y = rms_norm(y, out_norm_g[l].reshape(N_MIX_GROUPS, GROUP_WIDTH)).reshape(B, S, D_MIX)
        x = x + gate1 * (y @ w_out[l])

        h = rms_norm(x, norm2_g[l]) * (1.0 + scale2) + shift2
        m = hierarchical_moe(h.reshape(B * S, D), w_group[l], b_group[l], w_route[l], b_route[l],
                             w_gate[l], w_up[l], w_down[l]).reshape(B, S, D)
        x = x + gate2 * m
    return x


def setup_inputs(seed=0):
    out = dict(first_inputs(seed))
    for name, value in second_inputs(seed + 1).items():
        if name != "x":
            out[name + "_2"] = value
    return out


def reference(
    x, mem, mix_norm_w, w_in, dn_conv_w, dn_a_log, dn_dt_bias, dn_norm_w, rw_mu, rw_w0, rw_w2,
    rw_a0, rw_a2, rw_g2, rw_k_k, rw_k_a, rw_r_k, rw_ln_w, rw_ln_b, w_out, xa_norm_w, mem_norm_w,
    xa_wq, xa_wk, xa_wv, xa_wo, ffn_norm_w, ffn_w1, ffn_w2, final_norm_w, c_2, w_mod_2, b_mod_2,
    mod_layer_2, norm1_g_2, w_in_2, gm_norm_g_2, gm_ws_2, gm_bs_2, q_norm_g_2, k_norm_g_2,
    out_norm_g_2, w_out_2, norm2_g_2, w_group_2, b_group_2, w_route_2, b_route_2, w_gate_2,
    w_up_2, w_down_2,
):
    x = first_block(
        x, mem, mix_norm_w, w_in, dn_conv_w, dn_a_log, dn_dt_bias, dn_norm_w, rw_mu, rw_w0,
        rw_w2, rw_a0, rw_a2, rw_g2, rw_k_k, rw_k_a, rw_r_k, rw_ln_w, rw_ln_b, w_out, xa_norm_w,
        mem_norm_w, xa_wq, xa_wk, xa_wv, xa_wo, ffn_norm_w, ffn_w1, ffn_w2, final_norm_w,
    )
    return second_block(
        x, c_2, w_mod_2, b_mod_2, mod_layer_2, norm1_g_2, w_in_2, gm_norm_g_2, gm_ws_2, gm_bs_2,
        q_norm_g_2, k_norm_g_2, out_norm_g_2, w_out_2, norm2_g_2, w_group_2, b_group_2,
        w_route_2, b_route_2, w_gate_2, w_up_2, w_down_2,
    )


_drawn_inputs = setup_inputs


def setup_inputs(seed=0):
    import zlib

    import numpy as np

    out = dict(_drawn_inputs(seed))
    spreads = {}
    factors = {'dn_norm_w': 4.649,
     'rw_w2': 8.0,
     'rw_a2': 3.218,
     'rw_k_k': 5.137,
     'rw_k_a': 4.595,
     'rw_ln_w': 5.496,
     'rw_ln_b': 6.326,
     'xa_norm_w': 8.0,
     'mem_norm_w': 8.0,
     'ffn_norm_w': 2.835,
     'norm1_g_2': 6.053,
     'gm_norm_g_2': 8.0,
     'gm_bs_2': 4.02,
     'q_norm_g_2': 8.0,
     'k_norm_g_2': 8.0,
     'out_norm_g_2': 5.765,
     'norm2_g_2': 4.299,
     'b_group_2': 8.0,
     'b_route_2': 8.0}
    for name, (base, spread) in spreads.items():
        noise = np.random.default_rng([zlib.crc32(name.encode()), seed]).standard_normal(out[name].shape)
        drawn = base * np.exp(spread * noise) if base else spread * noise
        out[name] = jnp.asarray(drawn.astype(out[name].dtype))
    for name, factor in factors.items():
        out[name] = (out[name] * factor).astype(out[name].dtype)
    return out
```

```python
from contextlib import ExitStack

import numpy as np

import concourse.bass as bass
from concourse import mybir

F32 = mybir.dt.float32
F32R = mybir.dt.float32r
ALU = mybir.AluOpType
ACT = mybir.ActivationFunctionType
AX = mybir.AxisListType

P = 128
D = 2048
T = 256
TT = T // P
KC = D // P
UNIT_KC = 8
COLS = 512
UNIT = UNIT_KC * COLS
SLOTS = 4
EPS = 1e-6
HALF_E = float(np.exp(-0.5))

DN_HEADS, DN_DIM = 8, 128
DN_TILES = 24
RW_HEADS, RW_DIM = 16, 64
RW_TILES = 8
RW_GN_EPS = 64e-5
XA_HEADS = 4
FFN_QUARTERS = 4
SB_HEADS = 4
GMLP_GROUPS = 4
MIX_GROUPS = 8
GROUPS, PER_GROUP = 4, 8
EXPERTS = GROUPS * PER_GROUP
D_EXPERT = 256
MOD_COLS = 6 * D

STREAM, _at = {}, 0
for _name, _units in (("dn", 16), ("rw", 12), ("lora", 1), ("w_out", 8), ("xk", 2), ("xv", 2), ("xq", 2),
                      ("xo", 2), ("ffn", 16 * FFN_QUARTERS), ("w_in_2", 10), ("w_out_2", 4), ("moe", 3 * EXPERTS)):
    STREAM[_name] = (_at, _units)
    _at += _units
UNITS = _at

COL, _at = {}, 0
for _name, _n in (("mix_norm", 16), ("conv", 4 * DN_TILES), ("dn_norm", 1), ("mu", 26), ("a0", 8), ("k_k", 8),
                  ("k_a", 8), ("r_k", 8), ("ln_w", 8), ("ln_b", 8), ("xa_norm", 16), ("mem_norm", 16), ("ffn_norm", 16),
                  ("norm1", 16), ("norm2", 16), ("out_norm", 8), ("q_norm", 1), ("k_norm", 1), ("gm_bs", 4), ("c", 16),
                  ("dn_gate", 2 * DN_HEADS)):
    COL[_name] = (_at, _n)
    _at += _n
N_COLS = _at

CONST, _at = {}, 0
for _name, _n in (("ident", P), ("ones", P), ("tri_le", P), ("tri_gt", P), ("levels", 7 * P), ("strict_incl", 2 * P),
                  ("head_ones", P), ("g_incl", P), ("g_excl", P), ("g_pre", 1),
                  ("g_post", 1), ("before", TT * T), ("index", PER_GROUP)):
    CONST[_name] = (_at, _n)
    _at += _n
N_CONST = _at


class Kit:

    def __init__(self, stream):
        self.stream = stream
        self.norm_uses = self.inv_uses = self.turns = self.dve_at = 0
        self.ft = self.tt = self.act_n = self.pe_n = 0


class Steps:

    def __init__(self, eng, sem):
        self.eng, self.sem, self.n, self.turn, self.per = eng, sem, 0, None, 0

    def step(self, ins):
        ins.then_inc(self.sem, 1)
        self.n += 1

    def value(self):
        return self.n if self.turn is None else self.turn * self.per + self.n

    def settle(self):
        self.eng.wait_ge(self.sem, self.value())

    def loop(self, turn, per):
        self.turn, self.per, self.start = turn, per, self.n

    def end(self, trips):
        assert self.n - self.start == self.per
        self.n, self.turn = self.start + trips * self.per, None


def load_unit(k, sp, unit, slot):
    src = k.stream[unit] if isinstance(unit, int) else k.stream[bass.ds(unit, 1)].rearrange("a p n -> (a p) n")
    sp.dma_start(k.ring[:, slot].rearrange("p k n -> p (k n)"), src).then_inc(k.loaded[slot], 16)


def col(k, name, n=0):
    at, count = COL[name]
    assert n < count
    return k.cols[:, at + n:at + n + 1]


def cols_of(k, name):
    at, count = COL[name]
    return k.cols[:, at:at + count]


def const(k, name):
    at, n = CONST[name]
    return k.consts[:, at:at + n]


def bank(k, b):
    return k.psum[:, b, :]


def features(a):
    return a[:].rearrange("p t n -> p (t n)").rearrange("p (c t) -> p c t", t=T)


def norm_turn(nc, k, src, dst, scale, bias=None, sync=None, await_src=None):
    u = k.norm_uses
    k.norm_uses += 1
    with nc.Block(no_gpsimd_drain=True) as block:
        if sync is not None:
            @block.sync
            def _(sp):
                sync(sp)

        @block.scalar
        def _(act):
            for t in range(TT):
                if await_src is not None:
                    act.wait_ge(await_src[t], 16)
                act.activation(dst[:, 8 * t:8 * t + 8, :].rearrange("p a b -> p (a b)"), src[:, t, :], ACT.Square,
                               accum_out=k.ssq[:, t:t + 1]).then_inc(k.norm_ssq, 1)
            act.wait_ge(k.norm_ssq, 2 * u + 2)
            if await_src is not None:
                act.wait_ge(k.consts_in, 32)
            act.activation(k.rms[:, 0:TT], k.ssq[:, 0:TT], ACT.Sqrt, bias=k.eps[:, 0:1], scale=1.0 / D)\
               .then_inc(k.norm_rms, 1)
            for b in range(0, 8, 2):
                act.wait_ge(k.norm_mm, 8 * u + b + 1)
                for c in (2 * b, 2 * b + 1):
                    act.activation(dst[:, c, :], bank(k, b)[:, (c % 2) * T:(c % 2) * T + T], ACT.Identity,
                                   scale=scale(c), bias=0.0 if bias is None else bias(c))

        @block.vector
        def _(dve):
            dve.wait_ge(k.norm_rms, u + 1)
            dve.reciprocal(k.rstd[:, 0:TT], k.rms[:, 0:TT]).then_inc(k.norm_diag, 1)
            dve.wait_ge(k.norm_diag, 3 * u + 1)
            for t in range(TT):
                dve.tensor_scalar(k.diag[:, t, :], const(k, "ident"), k.rstd[:, t:t + 1], None, ALU.mult)\
                   .then_inc(k.norm_diag, 1)
            for b in range(1, 8, 2):
                dve.wait_ge(k.norm_mm, 8 * u + b + 1)
                for c in (2 * b, 2 * b + 1):
                    ps = bank(k, b)[:, (c % 2) * T:(c % 2) * T + T]
                    if bias is None:
                        dve.tensor_scalar(dst[:, c, :], ps, scale(c), None, ALU.mult)
                    else:
                        dve.tensor_scalar(dst[:, c, :], ps, scale(c), bias(c), ALU.mult, ALU.add)

        @block.tensor
        def _(pe):
            pe.wait_ge(k.norm_diag, 3 * u + 3)
            for c in range(KC):
                for t in range(TT):
                    mm = pe.matmul(bank(k, c // 2)[:, (c % 2) * T + t * P:(c % 2) * T + (t + 1) * P],
                                   src[:, t, c * P:(c + 1) * P], k.diag[:, t, :], start=True, stop=True)
                if c % 2:
                    mm.then_inc(k.norm_mm, 1)


def feature_group(k, pe, unit, rhs, tile, tiles=4, width=COLS, turn=None, rounds=0, per_turn=0):
    def at(value):
        return value if turn is None else turn * per_turn + value
    for half in range(2):
        pe.wait_ge(k.loaded[(unit + half) % SLOTS], (16 * ((unit + half) // SLOTS + 1)) if turn is None
                   else turn * (16 * rounds) + 16 * ((unit + half) // SLOTS + 1))
    for m in range(tiles):
        pe.wait_ge(k.ft_free, at(tile + m + 1))
        for c in range(KC):
            w = k.ring[:, (unit + c // UNIT_KC) % SLOTS, c % UNIT_KC, m * P:(m + 1) * P]
            mm = pe.matmul(bank(k, m)[:, 0:T], w, rhs[:, c, :], start=(c == 0), stop=(c == KC - 1))
        mm.then_inc(k.ft_done, 1)


def token_group(k, pe, units, lhs, chunks, tile, where=0, turn=None, rounds=0, per_turn=0, wait=True):
    def at(value):
        return value if turn is None else turn * per_turn + value
    if wait:
        for u in sorted({u for u, _, _ in units}):
            pe.wait_ge(k.loaded[u % SLOTS], (16 * (u // SLOTS + 1)) if turn is None
                       else turn * (16 * rounds) + 16 * (u // SLOTS + 1))
    for t in range(TT):
        pe.wait_ge(k.tt_free, at(tile + t + 1))
    for n, (u, row, at_col) in enumerate(units):
        flat = k.ring[:, u % SLOTS].rearrange("p k n -> p (k n)")
        w = flat[:, row * COLS + at_col:row * COLS + at_col + COLS]
        for t in range(TT):
            mm = pe.matmul(bank(k, 4 + (tile + t) % 4), lhs[:, chunks[n], t * P:(t + 1) * P], w,
                           start=(n == 0), stop=(n == len(units) - 1))
            if n == len(units) - 1:
                mm.then_inc(k.tt_done, 1)


def load_next(k, sp, unit, sem, value):
    if unit + SLOTS < STREAM["moe"][0]:
        sp.wait_ge(sem, value)
        load_unit(k, sp, unit + SLOTS, unit % SLOTS)


def invert(nc, k, X):
    u = k.inv_uses
    k.inv_uses += 1
    LEVELS = 7
    per = 2 * (LEVELS - 1)
    levels = const(k, "levels").rearrange("p (l n) -> p l n", l=LEVELS)
    ident = const(k, "ident")
    U, W, M, PR = k.inv_u, k.inv_w, k.inv_m, k.inv_p

    def mats(b):
        return bank(k, b).rearrange("p (h n) -> p h n", h=4)

    def four(g):
        return slice(4 * g, 4 * g + 4)

    def rep(a):
        return a.unsqueeze(1).broadcast_to([P, 4, P])

    with nc.Block(no_gpsimd_drain=True) as block:
        @block.vector
        def _(dve):
            s = k.dve_steps
            s.eng = dve
            for g in range(2):
                s.step(dve.tensor_tensor(W[:, four(g), :], X[:, four(g), 0, :], rep(levels[:, 0, :]), ALU.mult))
                s.settle()
                s.step(dve.tensor_tensor(U[:, four(g), :], rep(ident), W[:, four(g), :], ALU.subtract))
                s.settle()
                dve.tensor_tensor(M[:, four(g), :], X[:, four(g), 0, :], rep(levels[:, 1, :]), ALU.mult)\
                   .then_inc(k.inv_masked, 1)
            for level in range(1, LEVELS):
                for g in range(2):
                    n = 2 * (level - 1) + g
                    dve.wait_ge(k.inv_second, u * per + n + 1)
                    if level < LEVELS - 1:
                        s.step(dve.tensor_tensor(W[:, four(g), :], W[:, four(g), :], mats(4 + g), ALU.subtract))
                        s.step(dve.tensor_tensor(M[:, four(g), :], X[:, four(g), 0, :], rep(levels[:, level + 1, :]),
                                                 ALU.mult))
                    s.settle()
                    dve.tensor_tensor(U[:, four(g), :], U[:, four(g), :], mats(6 + g), ALU.subtract)\
                       .then_inc(k.inv_masked, 1)
            s.settle()

        @block.tensor
        def _(pe):
            for g in range(2):
                pe.wait_ge(k.inv_masked, u * (per + 2) + g + 1)
                for h in range(4):
                    mm = pe.transpose(mats(g)[:, h, :], U[:, 4 * g + h, :], ident)
                mm.then_inc(k.inv_first, 1)
            for level in range(1, LEVELS):
                for g in range(2):
                    n = 2 * (level - 1) + g
                    pe.wait_ge(k.inv_masked, u * (per + 2) + n + 1)
                    pe.wait_ge(k.inv_taken, u * (per + 2) + n + 1)
                    for h in range(4):
                        mm = pe.matmul(mats(g)[:, h, :], M[:, 4 * g + h, :], W[:, 4 * g + h, :], start=True, stop=True)
                    mm.then_inc(k.inv_first, 1)
                for g in range(2):
                    n = 2 * (level - 1) + g
                    pe.wait_ge(k.inv_taken, u * (per + 2) + n + 3)
                    for h in range(4):
                        if level < LEVELS - 1:
                            pe.matmul(mats(4 + g)[:, h, :], U[:, 4 * g + h, :], PR[:, 4 * g + h, :],
                                      start=True, stop=True)
                    for h in range(4):
                        mm = pe.matmul(mats(6 + g)[:, h, :], PR[:, 4 * g + h, :], U[:, 4 * g + h, :],
                                       start=True, stop=True)
                    mm.then_inc(k.inv_second, 1)

        @block.scalar
        def _(act):
            for n in range(per + 2):
                g = n % 2
                act.wait_ge(k.inv_first, u * (per + 2) + n + 1)
                act.activation((W if n < 2 else PR)[:, four(g), :], mats(g), ACT.Copy).then_inc(k.inv_taken, 1)


def deltanet_project(nc, k, u, qkvz):
    first, _ = STREAM["dn"]
    f0 = k.ft
    with nc.Block(no_gpsimd_drain=True) as block:
        @block.sync
        def _(sp):
            with sp.Fori(0, 3) as i:
                for j in range(4):
                    sp.wait_ge(k.ft_done, i * 8 + f0 + 4 * (j // 2 + 1))
                    load_unit(k, sp, i * 4 + first + SLOTS + j, (first + j) % SLOTS)
            for j in range(12, 16):
                load_next(k, sp, first + j, k.ft_done, f0 + 4 * (j // 2 + 1))

        @block.tensor
        def _(pe):
            with pe.Fori(0, 3) as i:
                for g in range(2):
                    feature_group(k, pe, first + 2 * g, u, f0 + 4 * g, turn=i, rounds=1, per_turn=8)
            for g in range(6, 8):
                feature_group(k, pe, first + 2 * g, u, f0 + 4 * g)

        @block.vector
        def _(dve):
            s = k.dve_steps
            s.eng = dve
            with dve.Fori(0, 3) as i:
                s.loop(i, 8 * 4)
                for m in range(8):
                    dve.wait_ge(k.ft_done, i * 8 + f0 + m + 1)
                    ps = bank(k, m % 4)
                    at = COL["conv"][0] + 4 * m

                    def tap(n):
                        return k.cols[:, bass.ds(i * 32 + at + n, 1)]

                    def out(lag):
                        return qkvz[:, bass.ds(i * 8 + m, 1), lag:T].rearrange("p a t -> p (a t)")
                    s.step(dve.tensor_scalar(out(0), ps[:, 0:T], tap(3), None, ALU.mult))
                    for lag in (1, 2, 3):
                        s.settle()
                        s.step(dve.scalar_tensor_tensor(out(lag), ps[:, 0:T - lag], tap(3 - lag), out(lag),
                                                        ALU.mult, ALU.add))
            s.end(3)

        @block.scalar
        def _(act):
            d0 = k.dve_at
            with act.Fori(0, 3) as i:
                for m in range(8):
                    act.wait_ge(k.dve_sem, i * 32 + d0 + 4 * (m + 1))
                    y = qkvz[:, bass.ds(i * 8 + m, 1), :].rearrange("p a t -> p (a t)")
                    act.activation(y, y, ACT.Silu).then_inc(k.ft_free, 1)
            for m in range(24, 32):
                act.wait_ge(k.ft_done, f0 + m + 1)
                act.activation(qkvz[:, m, :], bank(k, m % 4)[:, 0:T], ACT.Silu).then_inc(k.ft_free, 1)
    k.dve_at = k.dve_steps.n
    k.ft += 32


def deltanet_prepare(nc, k, u, qkvz, w_gate, q_tm, k_tm, v_tm, kb_tm, KQ, kT):
    s = k.dve_steps
    grids = [(q_tm, 0), (k_tm, 8), (v_tm, 16)]
    with nc.Block(no_gpsimd_drain=True) as block:
        @block.tensor
        def _(pe):
            n = 0
            for t in range(TT):
                for _, at in grids:
                    for g in range(2):
                        if n >= 6:
                            pe.wait_ge(k.turn_taken, k.turns + n - 5)
                        for h in range(4):
                            mm = pe.transpose(bank(k, n % 6)[:, h * P:(h + 1) * P],
                                              qkvz[:, at + 4 * g + h, t * P:(t + 1) * P], const(k, "ident"))
                        mm.then_inc(k.turned, 1)
                        n += 1
            for t in range(TT):
                for c in range(KC):
                    mm = pe.matmul(bank(k, 6 + t)[:, 0:16], u[:, c, t * P:(t + 1) * P], w_gate[:, c, :],
                                   start=(c == 0), stop=(c == KC - 1))
                mm.then_inc(k.gates_ready, 1)

        @block.scalar
        def _(act):
            n = 0
            for t in range(TT):
                for dst, _ in grids:
                    for g in range(2):
                        act.wait_ge(k.turned, k.turns + n + 1)
                        act.activation(dst[:, t, 4 * g:4 * g + 4, :], bank(k, n % 6).rearrange("p (h n) -> p h n", h=4),
                                       ACT.Copy).then_inc(k.turn_taken, 1)
                        n += 1

        @block.vector
        def _(dve):
            s.eng = dve
            dve.wait_ge(k.gates_ready, 2)
            for t in range(TT):
                s.step(dve.tensor_copy(k.beta[:, t, :], bank(k, 6 + t)[:, 8:16]))
                s.step(dve.tensor_tensor(k.g[:, t, :], bank(k, 6 + t)[:, 0:8],
                                         k.cols[:, COL["dn_gate"][0] + 8:COL["dn_gate"][0] + 16], ALU.add))
            s.settle()
            s.step(dve.tensor_scalar(k.sp_pos[:], k.g[:], 0.0, None, ALU.max))
            s.settle()
            s.step(dve.scalar_tensor_tensor(k.g[:], k.sp_pos[:], -2.0, k.g[:], ALU.mult, ALU.add))
            s.settle()
    k.turns += 12
    with nc.Block(no_gpsimd_drain=True) as block:
        @block.scalar
        def _(act):
            act.activation(k.beta[:], k.beta[:], ACT.Sigmoid).then_inc(k.act_sem, 1)
            act.activation(k.g[:], k.g[:], ACT.Exp).then_inc(k.act_sem, 1)
            act.activation(k.a_exp[:], k.cols[:, COL["dn_gate"][0]:COL["dn_gate"][0] + 8], ACT.Exp).then_inc(k.act_sem, 1)
            act.wait_ge(k.act_sem, k.act_n + 3)
            act.activation(k.g[:], k.g[:], ACT.Ln, bias=k.one[:, 0:1])

        @block.vector
        def _(dve):
            s.eng = dve
            for n, src in enumerate((q_tm, k_tm)):
                s.step(dve.tensor_tensor(k.scratch8[:], src[:].rearrange("p t h d -> p (t h d)"),
                                         src[:].rearrange("p t h d -> p (t h d)"), ALU.mult))
                s.settle()
                s.step(dve.tensor_reduce(k.qk_ssq[:, n], k.scratch8[:].rearrange("p (t h d) -> p t h d", t=2, h=8),
                                         AX.X, ALU.add))
                s.settle()
    k.act_n += 3
    with nc.Block(no_gpsimd_drain=True) as block:
        @block.scalar
        def _(act):
            act.activation(k.qk_ssq[:], k.qk_ssq[:], ACT.Sqrt, bias=k.eps[:, 0:1])

        @block.vector
        def _(dve):
            s.eng = dve
            s.step(dve.tensor_tensor(k.g[:], k.g[:], k.sp_pos[:], ALU.add))
            s.settle()
            s.step(dve.scalar_tensor_tensor(k.g[:], k.g[:], -1.0, k.a_exp[:].unsqueeze(1).broadcast_to([P, TT, 8]),
                                            ALU.mult, ALU.mult))
            s.settle()
    with nc.Block(no_gpsimd_drain=True) as block:
        @block.vector
        def _(dve):
            s.eng = dve
            s.step(dve.reciprocal(k.qk_ssq[:], k.qk_ssq[:]))
            s.settle()
            s.step(dve.tensor_scalar(k.qk_ssq[:, 0], k.qk_ssq[:, 0], DN_DIM ** -0.5, None, ALU.mult))
            s.settle()

            def over(a):
                return a.unsqueeze(3).broadcast_to([P, TT, 8, P])
            s.step(dve.tensor_tensor(q_tm[:], q_tm[:], over(k.qk_ssq[:, 0]), ALU.mult))
            s.step(dve.tensor_tensor(k_tm[:], k_tm[:], over(k.qk_ssq[:, 1]), ALU.mult))
            s.settle()
            s.step(dve.tensor_tensor(kb_tm[:], k_tm[:], over(k.beta[:]), ALU.mult))
            s.step(dve.tensor_scalar(qkvz[:, 24:32, :], qkvz[:, 24:32, :], col(k, "dn_norm"), None, ALU.mult))
            s.settle()
    jobs = [(k_tm, t, g, kT[:, 4 * g:4 * g + 4, t, :]) for t in range(TT) for g in range(2)]
    jobs += [(kb_tm, t, g, KQ[:, 4 * g:4 * g + 4, t, 0, :]) for t in range(TT) for g in range(2)]
    jobs += [(q_tm, t, g, KQ[:, 4 * g:4 * g + 4, t, 1, :]) for t in range(TT) for g in range(2)]
    turn_blocks(nc, k, [([src[:, t, 4 * g + h, :] for h in range(4)], dst) for src, t, g, dst in jobs])


def turn_blocks(nc, k, jobs):
    n0 = k.turns
    with nc.Block(no_gpsimd_drain=True) as block:
        @block.tensor
        def _(pe):
            for n, (pieces, _) in enumerate(jobs):
                if n >= 8:
                    pe.wait_ge(k.turn_taken, n0 + n - 7)
                for h, piece in enumerate(pieces):
                    mm = pe.transpose(bank(k, n % 8)[:, h * P:(h + 1) * P], piece, const(k, "ident"))
                mm.then_inc(k.turned, 1)

        @block.scalar
        def _(act):
            for n, (pieces, dst) in enumerate(jobs):
                if n % 2 == 0 or n >= 0:
                    act.wait_ge(k.turned, n0 + n + 1)
                    act.activation(dst, bank(k, n % 8)[:, 0:len(pieces) * P].rearrange("p (h n) -> p h n", n=P),
                                   ACT.Copy).then_inc(k.turn_taken, 1)
    k.turns += len(jobs)


def deltanet_tile(nc, k, t, v_tm, k_tm, KQ, kT, X, dec, dec_rhs, state, zs, out):
    s = k.dve_steps
    le, gt = const(k, "tri_le"), const(k, "tri_gt")
    with nc.Block(no_gpsimd_drain=True) as block:
        @block.vector
        def _(dve):
            s.eng = dve
            s.step(dve.tensor_tensor(dec_rhs[:], le.unsqueeze(1).broadcast_to([P, 8, P]),
                                     k.g[:, t, :].unsqueeze(2).broadcast_to([P, 8, P]), ALU.mult))
            s.settle()

        @block.tensor
        def _(pe):
            pe.matmul(bank(k, 7)[:, 0:8], le, k.g[:, t, :], start=True, stop=True)
            pe.matmul(bank(k, 7)[:, 8:16], gt, k.g[:, t, :], start=True, stop=True)
            for h in range(6):
                pe.matmul(bank(k, h // 2)[:, (h % 2) * T:(h % 2) * T + T], kT[:, h, t, :],
                          KQ[:, h, t].rearrange("p a n -> p (a n)"), start=True, stop=True)
            for h in range(6, 8):
                pe.matmul(bank(k, h // 2)[:, (h % 2) * T:(h % 2) * T + T], kT[:, h, t, :],
                          KQ[:, h, t].rearrange("p a n -> p (a n)"), start=True, stop=True)
    with nc.Block(no_gpsimd_drain=True) as block:
        @block.tensor
        def _(pe):
            for b in range(2):
                pe.matmul(bank(k, 4 + b), gt, dec_rhs[:, 4 * b:4 * b + 4, :].rearrange("p h n -> p (h n)"),
                          start=True, stop=True).then_inc(k.pe_sem, 1)

        @block.scalar
        def _(act):
            act.activation(k.egc[:], bank(k, 7)[:, 0:16], ACT.Exp)
            for b in range(2):
                act.wait_ge(k.pe_sem, k.pe_n + b + 1)
                act.activation(dec[:, 4 * b:4 * b + 4, :].rearrange("p h n -> p (h n)"), bank(k, 4 + b), ACT.Exp)

        @block.vector
        def _(dve):
            s.eng = dve
            mask = const(k, "strict_incl")
            for b in range(4):
                s.step(dve.tensor_tensor(X[:, 2 * b:2 * b + 2].rearrange("p h a n -> p h (a n)"),
                                         bank(k, b).rearrange("p (h n) -> p h n", h=2),
                                         mask.unsqueeze(1).broadcast_to([P, 2, 2 * P]), ALU.mult))
            s.settle()
    k.pe_n += 2
    with nc.Block(no_gpsimd_drain=True) as block:
        @block.vector
        def _(dve):
            s.eng = dve
            for a in range(2):
                s.step(dve.tensor_tensor(X[:, :, a, :], X[:, :, a, :], dec[:], ALU.mult))
            s.settle()
    invert(nc, k, X)
    R, V, O = k.inv_w, k.inv_m, k.inv_p

    def over(a):
        return a.unsqueeze(2).broadcast_to([P, 8, P])

    def product(lhs, rhs, b0):
        def _(pe):
            for h in range(8):
                pe.matmul(bank(k, b0 + h // 4)[:, (h % 4) * P:(h % 4 + 1) * P], lhs(h), rhs[:, h, :],
                          start=True, stop=True)
        return _
    two = [k.psum[:, b:b + 2, :].rearrange("p b (h n) -> p (b h) n", n=P) for b in (0, 2, 4, 6)]
    if t:
        with nc.Block(no_gpsimd_drain=True) as block:
            block.tensor(product(lambda h: kT[:, h, t, :], state, 0))
    with nc.Block(no_gpsimd_drain=True) as block:
        @block.vector
        def _(dve):
            s.eng = dve
            if t:
                s.step(dve.tensor_tensor(R[:], two[0], over(k.egc[:, 0:8]), ALU.mult))
                s.settle()
                s.step(dve.tensor_tensor(R[:], v_tm[:, t], R[:], ALU.subtract))
                s.settle()
            s.step(dve.tensor_tensor(R[:], R[:] if t else v_tm[:, t], over(k.beta[:, t, :]), ALU.mult))
            if not t:
                s.step(dve.tensor_tensor(k_tm[:, 0], k_tm[:, 0], over(k.egc[:, 8:16]), ALU.mult))
            s.settle()
    with nc.Block(no_gpsimd_drain=True) as block:
        block.tensor(product(lambda h: k.inv_u[:, h, :], R, 2))
    with nc.Block(no_gpsimd_drain=True) as block:
        @block.scalar
        def _(act):
            act.activation(V[:], two[1], ACT.Copy)
    with nc.Block(no_gpsimd_drain=True) as block:
        @block.tensor
        def _(pe):
            product(lambda h: X[:, h, 1, :], V, 4)(pe)
            if t:
                product(lambda h: KQ[:, h, t, 1, :], state, 6)(pe)
            else:
                product(lambda h: k_tm[:, 0, h, :], V, 6)(pe)
    with nc.Block(no_gpsimd_drain=True) as block:
        if not t:
            @block.scalar
            def _(act):
                act.activation(state[:], two[3], ACT.Copy)

        @block.vector
        def _(dve):
            s.eng = dve
            if t:
                s.step(dve.tensor_tensor(O[:], two[3], over(k.egc[:, 0:8]), ALU.mult))
                s.settle()
                s.step(dve.tensor_tensor(O[:], O[:], two[2], ALU.add))
            else:
                s.step(dve.tensor_copy(O[:], two[2]))
            s.settle()
            s.step(dve.tensor_tensor(R[:], O[:], O[:], ALU.mult))
            s.settle()
            s.step(dve.tensor_reduce(k.o_ssq[:], R[:], AX.X, ALU.add))
            s.settle()
    with nc.Block(no_gpsimd_drain=True) as block:
        @block.scalar
        def _(act):
            act.activation(k.o_ssq[:], k.o_ssq[:], ACT.Sqrt, bias=k.eps[:, 0:1], scale=1.0 / DN_DIM)
    with nc.Block(no_gpsimd_drain=True) as block:
        @block.vector
        def _(dve):
            s.eng = dve
            s.step(dve.reciprocal(k.o_ssq[:], k.o_ssq[:]))
            s.settle()
            s.step(dve.tensor_tensor(O[:], O[:], over(k.o_ssq[:]), ALU.mult))
            s.settle()
    with nc.Block(no_gpsimd_drain=True) as block:
        @block.tensor
        def _(pe):
            for h in range(8):
                pe.transpose(bank(k, h // 4)[:, (h % 4) * P:(h % 4 + 1) * P], O[:, h, :], const(k, "ident"))
    with nc.Block(no_gpsimd_drain=True) as block:
        @block.vector
        def _(dve):
            s.eng = dve
            s.step(dve.tensor_tensor(out[:, 0:8, t * P:(t + 1) * P], two[0], zs[:, :, t * P:(t + 1) * P], ALU.mult))
            s.settle()


def rwkv_project(nc, k, u, mix):
    first, _ = STREAM["rw"]
    lora, _ = STREAM["lora"]
    f0 = k.ft
    s = k.dve_steps
    with nc.Block(no_gpsimd_drain=True) as block:
        @block.sync
        def _(sp):
            with sp.Fori(0, 3) as i:
                for j in range(4):
                    sp.wait_ge(k.ft_done, i * 8 + f0 + 4 * (j // 2 + 1))
                    load_unit(k, sp, i * 4 + first + SLOTS + j, (first + j) % SLOTS)
            load_next(k, sp, lora, k.ft_done, f0 + 26)

        @block.tensor
        def _(pe):
            with pe.Fori(0, 3) as i:
                for g in range(2):
                    feature_group(k, pe, first + 2 * g, u, f0 + 4 * g, turn=i, rounds=1, per_turn=8)
            pe.wait_ge(k.loaded[lora % SLOTS], 16 * (lora // SLOTS + 1))
            w = k.ring[:, lora % SLOTS].rearrange("p k n -> p (k n)").rearrange("p (k n) -> p k n", n=2 * P)
            for m in range(2):
                pe.wait_ge(k.ft_free, f0 + 24 + m + 1)
                for c in range(KC):
                    mm = pe.matmul(bank(k, m)[:, 0:T], w[:, c, m * P:(m + 1) * P], u[:, c, :],
                                   start=(c == 0), stop=(c == KC - 1))
                mm.then_inc(k.ft_done, 1)

        @block.vector
        def _(dve):
            s.eng = dve
            s.step(dve.tensor_scalar(k.one_less_mu[:], cols_of(k, "mu"), -1.0, 1.0, ALU.mult, ALU.add))
            s.step(dve.tensor_scalar(k.one_less_ka[:], cols_of(k, "k_a"), -1.0, 1.0, ALU.mult, ALU.add))
            s.settle()

            def shift(ps, less, mu, now, later):
                s.step(dve.tensor_scalar(now, ps[:, 0:T], less, None, ALU.mult))
                s.settle()
                dve.scalar_tensor_tensor(later, ps[:, 0:T - 1], mu, later, ALU.mult, ALU.add).then_inc(k.ft_free, 1)
            with dve.Fori(0, 3) as i:
                s.loop(i, 8)
                for m in range(8):
                    dve.wait_ge(k.ft_done, i * 8 + f0 + m + 1)
                    shift(bank(k, m % 4), k.one_less_mu[:, bass.ds(i * 8 + m, 1)],
                          k.cols[:, bass.ds(i * 8 + (COL["mu"][0] + m), 1)],
                          mix[:, bass.ds(i * 8 + m, 1), :].rearrange("p a t -> p (a t)"),
                          mix[:, bass.ds(i * 8 + m, 1), 1:T].rearrange("p a t -> p (a t)"))
            s.end(3)
            for m in range(2):
                dve.wait_ge(k.ft_done, f0 + 24 + m + 1)
                shift(bank(k, m), k.one_less_mu[:, 24 + m:25 + m], col(k, "mu", 24 + m), mix[:, 24 + m, :],
                      mix[:, 24 + m, 1:T])
    k.ft += 26


def rwkv_prepare(nc, k, mix, lora, AR, sig, neg, a, gate, kk, scratch, out):
    s = k.dve_steps
    r, kv, v = mix[:, 0:8, :], mix[:, 8:16, :], mix[:, 16:24, :]
    th = k.tanh
    with nc.Block(no_gpsimd_drain=True) as block:
        @block.sync
        def _(sp):
            sp.wait_ge(k.small_in, 32)

        @block.scalar
        def _(act):
            act.activation(th[0:64, :], mix[0:64, 24, :], ACT.Tanh)
            act.activation(mix[:, 25, :], mix[:, 25, :], ACT.Sigmoid)

        @block.vector
        def _(dve):
            s.eng = dve
            s.step(dve.memset(th[64:65, :], 1.0))
            for c in range(8):
                s.step(dve.tensor_scalar(kk[:, c, :], kv[:, c, :], col(k, "k_k", c), None, ALU.mult))
            s.settle()
            s.step(dve.tensor_tensor(scratch[:], kk[:], kk[:], ALU.mult))
            s.settle()
    with nc.Block(no_gpsimd_drain=True) as block:
        @block.tensor
        def _(pe):
            for t in range(TT):
                for n in range(2):
                    pe.matmul(bank(k, 2 * t + n), th[0:65, t * P:(t + 1) * P], lora[0:65, 0, n * 512:(n + 1) * 512],
                              start=True, stop=True)
            for c in range(8):
                pe.matmul(bank(k, 4 + c // 2)[:, (c % 2) * T:(c % 2) * T + T], lora[64:128, 1, c * P:(c + 1) * P],
                          mix[64:128, 24, :], start=True, stop=True)
    with nc.Block(no_gpsimd_drain=True) as block:
        @block.scalar
        def _(act):
            act.activation(sig[:].rearrange("p t n -> p (t n)"),
                           k.psum[:, 0:4, :].rearrange("p b n -> p (b n)"), ACT.Sigmoid).then_inc(k.act_sem, 1)
            for c in range(8):
                act.activation(a[:, c, :], bank(k, 4 + c // 2)[:, (c % 2) * T:(c % 2) * T + T], ACT.Sigmoid,
                               bias=col(k, "a0", c))

        @block.tensor
        def _(pe):
            pe.wait_ge(k.act_sem, k.act_n + 1)
            for c in range(8):
                pe.matmul(bank(k, c // 2)[:, (c % 2) * T:(c % 2) * T + T], lora[:, 2, c * P:(c + 1) * P], mix[:, 25, :],
                          start=True, stop=True)
    k.act_n += 1
    with nc.Block(no_gpsimd_drain=True) as block:
        @block.tensor
        def _(pe):
            for b in range(4):
                pe.matmul(bank(k, 4 + b), const(k, "head_ones"),
                          scratch[:, 2 * b:2 * b + 2, :].rearrange("p c t -> p (c t)"), start=True, stop=True)

        @block.vector
        def _(dve):
            s.eng = dve
            s.step(dve.tensor_copy(gate[:].rearrange("p c t -> p (c t)"),
                                   k.psum[:, 0:4, :].rearrange("p b n -> p (b n)")))
            for c in range(8):
                s.step(dve.tensor_scalar(out[:, c, :], a[:, c, :], col(k, "k_a", c), k.one_less_ka[:, c:c + 1],
                                         ALU.mult, ALU.add))
            s.settle()
            s.step(dve.tensor_tensor(kv, kv, out, ALU.mult))
            s.settle()
    with nc.Block(no_gpsimd_drain=True) as block:
        @block.scalar
        def _(act):
            act.activation(scratch[:].rearrange("p c t -> p (c t)"), k.psum[:, 4:8, :].rearrange("p b n -> p (b n)"),
                           ACT.Sqrt)
    with nc.Block(no_gpsimd_drain=True) as block:
        @block.vector
        def _(dve):
            s.eng = dve
            s.step(dve.tensor_scalar(scratch[:], scratch[:], 1e-12, None, ALU.max))
            s.settle()
            s.step(dve.reciprocal(scratch[:], scratch[:]))
            s.settle()
            s.step(dve.tensor_tensor(kk[:], kk[:], scratch[:], ALU.mult))
            s.settle()
            s.step(dve.tensor_tensor(a[:], a[:], kk[:], ALU.mult))
            for c in range(8):
                s.step(dve.scalar_tensor_tensor(scratch[:, c, :], r[:, c, :], col(k, "r_k", c), kv[:, c, :],
                                                ALU.mult, ALU.mult))
            s.settle()

        @block.tensor
        def _(pe):
            for c in range(8):
                for t in range(TT):
                    pe.matmul(bank(k, c)[:, t * T:(t + 1) * T], sig[:, t, c * P:(c + 1) * P],
                              k.consts[:, CONST["g_incl"][0]:CONST["g_incl"][0] + T], start=True, stop=True)
    with nc.Block(no_gpsimd_drain=True) as block:
        @block.scalar
        def _(act):
            for c in range(8):
                ps = bank(k, c).rearrange("p (t a n) -> p t a n", t=TT, a=2)
                act.activation(AR[:, c, :, 0, :], ps[:, :, 1, :], ACT.Exp, scale=-HALF_E)
                act.activation(AR[:, c, :, 1, :], ps[:, :, 0, :], ACT.Exp, scale=-HALF_E)
                act.activation(neg[:, c, :].rearrange("p (t n) -> p t n", t=TT), ps[:, :, 0, :], ACT.Exp, scale=HALF_E)
    with nc.Block(no_gpsimd_drain=True) as block:
        @block.tensor
        def _(pe):
            for b in range(4):
                pe.matmul(bank(k, b), const(k, "head_ones"),
                          scratch[:, 2 * b:2 * b + 2, :].rearrange("p c t -> p (c t)"), start=True, stop=True)
            for c in range(8):
                pe.matmul(bank(k, 4)[:, c:c + 1], sig[:, 0, c * P:(c + 1) * P], const(k, "g_post"),
                          start=True, stop=False)
                pe.matmul(bank(k, 4)[:, c:c + 1], sig[:, 1, c * P:(c + 1) * P], const(k, "g_pre"),
                          start=False, stop=True)

        @block.vector
        def _(dve):
            s.eng = dve
            def cut(x):
                return x.rearrange("p c (t n) -> p c t n", t=TT)
            for t in range(TT):
                s.step(dve.tensor_tensor(AR[:, :, t, 0, :], AR[:, :, t, 0, :], cut(kk)[:, :, t, :], ALU.mult))
                s.step(dve.tensor_tensor(AR[:, :, t, 1, :], AR[:, :, t, 1, :], cut(r)[:, :, t, :], ALU.mult))
            s.step(dve.tensor_tensor(a[:], a[:], neg[:], ALU.mult))
            s.step(dve.tensor_tensor(kv, kv, neg[:], ALU.mult))
            s.settle()
    with nc.Block(no_gpsimd_drain=True) as block:
        @block.scalar
        def _(act):
            act.activation(k.carry[:], bank(k, 4)[:, 0:8], ACT.Exp, scale=-HALF_E)

        @block.vector
        def _(dve):
            s.eng = dve
            for b in range(4):
                s.step(dve.tensor_tensor(out[:, 2 * b:2 * b + 2, :].rearrange("p c t -> p (c t)"), bank(k, b),
                                         v[:, 2 * b:2 * b + 2, :].rearrange("p c t -> p (c t)"), ALU.mult))
            s.settle()
            for c in range(8):
                s.step(dve.scalar_tensor_tensor(out[:, c, :], out[:, c, :], col(k, "ln_b", c), gate[:, c, :],
                                                ALU.add, ALU.mult))
            s.settle()
            for c in range(8):
                s.step(dve.tensor_scalar(gate[:, c, :], gate[:, c, :], col(k, "ln_w", c), None, ALU.mult))
            s.settle()


def rwkv_batch(nc, k, t, half, X, Y, AR, B, K, v_tm, b_tm, k_tm, R, U, y, tmp, state, gate, out):
    s = k.dve_steps
    c0 = 4 * half

    def rows(h):
        return slice(RW_DIM * (h % 2), RW_DIM * (h % 2) + RW_DIM)
    ts = slice(t * P, (t + 1) * P)
    if not t:
        turn_blocks(nc, k, [([B[:, c0 + c, ts] for c in range(4)], b_tm.rearrange("p (h n) -> p h n", n=P)),
                            ([K[:, c0 + c, ts] for c in range(4)], k_tm.rearrange("p (h n) -> p h n", n=P))])
    with nc.Block(no_gpsimd_drain=True) as block:
        @block.tensor
        def _(pe):
            for n, src in enumerate((B, K)):
                for h in range(8):
                    pe.matmul(bank(k, 4 * n + 2 * (h // 4) + h % 2)[:, (h // 2 % 2) * T:(h // 2 % 2) * T + T],
                              src[rows(h), c0 + h // 2, ts],
                              AR[rows(h), c0 + h // 2, t].rearrange("p a n -> p (a n)"), start=True, stop=True)
    with nc.Block(no_gpsimd_drain=True) as block:
        @block.vector
        def _(dve):
            s.eng = dve
            mask = const(k, "strict_incl").unsqueeze(1).broadcast_to([P, 2, 2 * P])
            for n, dst in enumerate((X, Y)):
                for b in range(4):
                    h = 4 * (b // 2) + b % 2
                    s.step(dve.tensor_tensor(dst[:, h:h + 3:2].rearrange("p h a n -> p h (a n)"),
                                             bank(k, 4 * n + b).rearrange("p (h n) -> p h n", h=2), mask, ALU.mult))
            s.settle()
    invert(nc, k, X)
    with nc.Block(no_gpsimd_drain=True) as block:
        @block.tensor
        def _(pe):
            for h in range(8):
                ps = bank(k, 5 * (h % 2))[:, (h // 2) * RW_DIM:(h // 2 + 1) * RW_DIM]
                pe.matmul(ps, Y[:, h, 0, :], v_tm[:, t, (8 * half + h) * RW_DIM:(8 * half + h + 1) * RW_DIM],
                          start=True, stop=not t)
                if t:
                    pe.matmul(ps, AR[rows(h), c0 + h // 2, t, 0, :], state[rows(h), c0 + h // 2, :],
                              start=False, stop=True)
    with nc.Block(no_gpsimd_drain=True) as block:
        @block.scalar
        def _(act):
            for b in range(2):
                act.activation(R.rearrange("p (h b n) -> p h b n", b=2, n=RW_DIM)[:, :, b, :],
                               bank(k, 5 * b)[:, 0:4 * RW_DIM].rearrange("p (h n) -> p h n", n=RW_DIM),
                               ACT.Copy, scale=-1.0)
    with nc.Block(no_gpsimd_drain=True) as block:
        @block.tensor
        def _(pe):
            for h in range(8):
                pe.matmul(bank(k, 1)[:, h * RW_DIM:(h + 1) * RW_DIM], k.inv_u[:, h, :],
                          R[:, h * RW_DIM:(h + 1) * RW_DIM], start=True, stop=True)
    with nc.Block(no_gpsimd_drain=True) as block:
        @block.scalar
        def _(act):
            act.activation(U, bank(k, 1), ACT.Copy)
    with nc.Block(no_gpsimd_drain=True) as block:
        @block.tensor
        def _(pe):
            for h in range(8):
                ps = bank(k, 2 + 4 * (h % 2))[:, (h // 2) * RW_DIM:(h // 2 + 1) * RW_DIM]
                v = v_tm[:, t, (8 * half + h) * RW_DIM:(8 * half + h + 1) * RW_DIM]
                own = slice(h * RW_DIM, (h + 1) * RW_DIM)
                pe.matmul(ps, X[:, h, 1, :], U[:, own], start=True, stop=False)
                pe.matmul(ps, Y[:, h, 1, :], v, start=False, stop=not t)
                if t:
                    pe.matmul(ps, AR[rows(h), c0 + h // 2, t, 1, :], state[rows(h), c0 + h // 2, :],
                              start=False, stop=True)
            if not t:
                for h in range(8):
                    ps = bank(k, 3 + h % 2)[rows(h), (h // 2) * RW_DIM:(h // 2 + 1) * RW_DIM]
                    v = v_tm[:, t, (8 * half + h) * RW_DIM:(8 * half + h + 1) * RW_DIM]
                    own = slice(h * RW_DIM, (h + 1) * RW_DIM)
                    pe.matmul(ps, b_tm[:, own], U[:, own], start=True, stop=False)
                    pe.matmul(ps, k_tm[:, own], v, start=False, stop=True)
    y3 = y.rearrange("p (h n) -> p h n", n=RW_DIM)
    tmp3 = tmp.rearrange("p (h n) -> p h n", n=RW_DIM)

    def over(x):
        return x.unsqueeze(2).broadcast_to([P, 8, RW_DIM])
    with nc.Block(no_gpsimd_drain=True) as block:
        @block.vector
        def _(dve):
            s.eng = dve
            for b in range(2):
                s.step(dve.tensor_copy(y.rearrange("p (h b n) -> p h b n", b=2, n=RW_DIM)[:, :, b, :],
                                       bank(k, 2 + 4 * b)[:, 0:4 * RW_DIM].rearrange("p (h n) -> p h n", n=RW_DIM)))
            s.settle()
            s.step(dve.tensor_reduce(k.y_mean[:], y3, AX.X, ALU.add))
            s.settle()
            s.step(dve.tensor_scalar(k.y_mean[:], k.y_mean[:], 1.0 / RW_DIM, None, ALU.mult))
            s.settle()
            s.step(dve.tensor_tensor(y3, y3, over(k.y_mean[:]), ALU.subtract))
            s.settle()
            s.step(dve.tensor_tensor(tmp, y, y, ALU.mult))
            s.settle()
            s.step(dve.tensor_reduce(k.y_ssq[:], tmp3, AX.X, ALU.add))
            if not t:
                for c in range(4):
                    for b in range(2):
                        own = slice(RW_DIM * b, RW_DIM * (b + 1))
                        s.step(dve.tensor_scalar(state[own, c0 + c, :], bank(k, 3 + b)[own, c * RW_DIM:(c + 1) * RW_DIM],
                                                 k.carry[own, c0 + c:c0 + c + 1], None, ALU.mult))
            s.settle()
    with nc.Block(no_gpsimd_drain=True) as block:
        @block.scalar
        def _(act):
            act.activation(k.y_ssq[:], k.y_ssq[:], ACT.Sqrt, bias=k.gn_eps[:, 0:1], scale=1.0 / RW_DIM)
    with nc.Block(no_gpsimd_drain=True) as block:
        @block.vector
        def _(dve):
            s.eng = dve
            s.step(dve.reciprocal(k.y_ssq[:], k.y_ssq[:]))
            s.settle()
            s.step(dve.tensor_tensor(y3, y3, over(k.y_ssq[:]), ALU.mult))
            s.settle()
    with nc.Block(no_gpsimd_drain=True) as block:
        @block.tensor
        def _(pe):
            for c in range(4):
                pe.transpose(bank(k, 0)[:, c * P:(c + 1) * P], y[:, c * P:(c + 1) * P], const(k, "ident"))
    with nc.Block(no_gpsimd_drain=True) as block:
        @block.vector
        def _(dve):
            s.eng = dve
            at = out[:, c0:c0 + 4, ts]
            turned = tmp.rearrange("p (c n) -> p c n", n=P)
            s.step(dve.tensor_tensor(turned, bank(k, 0).rearrange("p (c n) -> p c n", n=P), gate[:, c0:c0 + 4, ts],
                                     ALU.mult))
            s.settle()
            s.step(dve.tensor_tensor(at, at, turned, ALU.add))
            s.settle()


def unit_rows(first, chunks, per_unit=UNIT_KC, rows_per_chunk=1, at_col=0):
    return [(first + c // per_unit, (c % per_unit) * rows_per_chunk, at_col) for c in range(chunks)]


def mixer_out(nc, k, mixed, x):
    first, _ = STREAM["w_out"]
    t0 = k.tt
    with nc.Block(no_gpsimd_drain=True) as block:
        @block.sync
        def _(sp):
            with sp.Fori(0, 2) as i:
                for j in range(4):
                    sp.wait_ge(k.tt_done, i * 4 + t0 + 2 * (j // 2 + 1))
                    load_unit(k, sp, i * 4 + first + SLOTS + j, (first + j) % SLOTS)

        @block.tensor
        def _(pe):
            with pe.Fori(0, 2) as i:
                for g in range(2):
                    token_group(k, pe, unit_rows(first + 2 * g, KC), mixed, range(KC), t0 + 2 * g,
                                turn=i, rounds=1, per_turn=4)

        @block.vector
        def _(dve):
            with dve.Fori(0, 2) as i:
                for n in range(4):
                    dve.wait_ge(k.tt_done, i * 4 + t0 + n + 1)
                    at = x[:, n % 2, bass.ds(i * 1024 + (n // 2) * COLS, COLS)]
                    dve.tensor_tensor(at, at, bank(k, 4 + (t0 + n) % 4), ALU.add).then_inc(k.tt_free, 1)
    k.tt += 8


def cross_attention(nc, k, x, scope_sb, mem, h_t, mem_t, mem_in):
    s = k.dve_steps
    k_t, q_t, v_m = scope_sb("xa_k", [P, 4, T]), scope_sb("xa_q", [P, 4, T]), scope_sb("xa_v", [P, TT, 512])
    probs, probs_t, o_t = (scope_sb("xa_probs", [P, XA_HEADS, TT, T]), scope_sb("xa_probs_t", [P, XA_HEADS, TT, T]),
                           scope_sb("xa_o", [P, XA_HEADS, T]))
    top, total = scope_sb("xa_top", [P, XA_HEADS, TT]), scope_sb("xa_total", [P, XA_HEADS, TT])
    norm_turn(nc, k, x, h_t, lambda c: col(k, "xa_norm", c))
    norm_turn(nc, k, mem, mem_t, lambda c: col(k, "mem_norm", c), await_src=mem_in)
    f0, t0 = k.ft, k.tt
    with nc.Block(no_gpsimd_drain=True) as block:
        @block.sync
        def _(sp):
            for part, sem, value in (("xk", k.ft_done, f0 + 4), ("xv", k.tt_done, t0 + 2), ("xq", k.ft_done, f0 + 8)):
                for j in range(2):
                    load_next(k, sp, STREAM[part][0] + j, sem, value)

        @block.tensor
        def _(pe):
            feature_group(k, pe, STREAM["xk"][0], mem_t, f0)
            token_group(k, pe, unit_rows(STREAM["xv"][0], KC), mem_t, range(KC), t0)
            feature_group(k, pe, STREAM["xq"][0], h_t, f0 + 4)

        @block.scalar
        def _(act):
            for n in range(8):
                act.wait_ge(k.ft_done, f0 + n + 1)
                act.activation((k_t, q_t)[n // 4][:, n % 4, :], bank(k, n % 4)[:, 0:T], ACT.Copy).then_inc(k.ft_free, 1)

        @block.vector
        def _(dve):
            for n in range(2):
                dve.wait_ge(k.tt_done, t0 + n + 1)
                dve.tensor_copy(v_m[:, n, :], bank(k, 4 + (t0 + n) % 4)).then_inc(k.tt_free, 1)
    k.ft += 8
    k.tt += 2
    scores = k.psum[:, 0:4, :].rearrange("p h (t m) -> p h t m", t=TT)
    with nc.Block(no_gpsimd_drain=True) as block:
        @block.tensor
        def _(pe):
            for h in range(XA_HEADS):
                for t in range(TT):
                    mm = pe.matmul(scores[:, h, t, :], q_t[:, h, t * P:(t + 1) * P], k_t[:, h, :], start=True, stop=True)
            mm.then_inc(k.pe_sem, 1)

        @block.vector
        def _(dve):
            s.eng = dve
            dve.wait_ge(k.pe_sem, k.pe_n + 1)
            s.step(dve.tensor_reduce(top[:], scores, AX.X, ALU.max))
            s.settle()
            s.step(dve.tensor_scalar(top[:], top[:], -P ** -0.5, None, ALU.mult))

        @block.scalar
        def _(act):
            act.wait_ge(k.dve_sem, k.dve_steps_before + 2)
            for h in range(XA_HEADS):
                for t in range(TT):
                    act.activation(probs[:, h, t, :], scores[:, h, t, :], ACT.Exp, scale=P ** -0.5,
                                   bias=top[:, h, t:t + 1], accum_out=total[:, h, t:t + 1])
    k.pe_n += 1
    with nc.Block(no_gpsimd_drain=True) as block:
        @block.vector
        def _(dve):
            s.eng = dve
            s.step(dve.reciprocal(total[:], total[:]))
            s.settle()
            s.step(dve.tensor_tensor(probs[:], probs[:], total[:].unsqueeze(3).broadcast_to([P, XA_HEADS, TT, T]),
                                     ALU.mult))
            s.settle()
    turn_blocks(nc, k, [([probs[:, h, t, m * P:(m + 1) * P] for m in range(2) for t in range(TT)],
                         probs_t[:, h].rearrange("p m (t n) -> p (m t) n", n=P)) for h in range(XA_HEADS)])
    with nc.Block(no_gpsimd_drain=True) as block:
        @block.tensor
        def _(pe):
            for h in range(XA_HEADS):
                for m in range(2):
                    pe.matmul(bank(k, h)[:, 0:T], v_m[:, m, h * P:(h + 1) * P], probs_t[:, h, m, :],
                              start=(m == 0), stop=(m == 1))
    with nc.Block(no_gpsimd_drain=True) as block:
        @block.scalar
        def _(act):
            act.activation(o_t[:], k.psum[:, 0:4, 0:T], ACT.Copy)
    first, t0 = STREAM["xo"][0], k.tt
    with nc.Block(no_gpsimd_drain=True) as block:
        @block.sync
        def _(sp):
            for j in range(2):
                load_next(k, sp, first + j, k.tt_done, t0 + 8)

        @block.tensor
        def _(pe):
            for n in range(4):
                token_group(k, pe, unit_rows(first, 4, per_unit=2, rows_per_chunk=4, at_col=n * COLS), o_t, range(4),
                            t0 + 2 * n)

        @block.vector
        def _(dve):
            for n in range(8):
                dve.wait_ge(k.tt_done, t0 + n + 1)
                at = x[:, n % 2, (n // 2) * COLS:(n // 2 + 1) * COLS]
                dve.tensor_tensor(at, at, bank(k, 4 + (t0 + n) % 4), ALU.add).then_inc(k.tt_free, 1)
    k.tt += 8


def mlp_and_modulation(nc, k, io, x, u, hid, relu, acc, w_mod, prod, c_silu):
    first, _ = STREAM["ffn"]
    f0, t0 = k.ft, k.tt
    MOD_GROUPS = MOD_COLS // COLS
    with nc.Block(no_gpsimd_drain=True) as block:
        @block.sync
        def _(sp):
            sp.wait_ge(k.pool_sem, 1)
            sp.dma_start(acc[0:2].rearrange("p g n -> p (g n)"), io["b_mod"]).then_inc(k.small_in, 16)
            sp.wait_ge(k.small_in, 48)

        @block.gpsimd
        def _(pool):
            pool.memset(acc[:], 0.0).then_inc(k.pool_sem, 1)

        @block.scalar
        def _(act):
            act.activation(c_silu[:], cols_of(k, "c"), ACT.Silu)
    with nc.Block() as block:
        @block.sync
        def _(sp):
            with sp.Fori(0, FFN_QUARTERS) as i:
                for j in range(16):
                    if j < 8:
                        sp.wait_ge(k.ft_done, i * 16 + f0 + 4 * (j // 2 + 1))
                    else:
                        sp.wait_ge(k.tt_done, i * 8 + t0 + 2 * ((j - 8) // 2 + 1))
                    load_unit(k, sp, i * 16 + first + SLOTS + j, (first + j) % SLOTS)

        @block.tensor
        def _(pe):
            with pe.Fori(0, FFN_QUARTERS) as i:
                for g in range(4):
                    feature_group(k, pe, first + 2 * g, u, f0 + 4 * g, turn=i, rounds=4, per_turn=16)
                for g in range(4):
                    if g == 0:
                        pe.wait_ge(k.ft_free, i * 16 + f0 + 4 + 16)
                    token_group(k, pe, unit_rows(first + 8 + 2 * g, KC), hid, range(KC), t0 + 2 * g,
                                turn=i, rounds=4, per_turn=8)

        @block.scalar
        def _(act):
            with act.Fori(0, FFN_QUARTERS) as i:
                for m in range(16):
                    act.wait_ge(k.ft_done, i * 16 + f0 + m + 1)
                    act.activation(relu[:, m % 2, :], bank(k, m % 4)[:, 0:T], ACT.Relu).then_inc(k.act_sem, 1)
                    act.wait_ge(k.act_sem, i * 16 + k.act_n + m + 1)
                    act.activation(hid[:, m, :], relu[:, m % 2, :], ACT.Square).then_inc(k.ft_free, 1)

        @block.vector
        def _(dve):
            with dve.Fori(0, FFN_QUARTERS) as i:
                for n in range(8):
                    dve.wait_ge(k.tt_done, i * 8 + t0 + n + 1)
                    at = x[:, n % 2, (n // 2) * COLS:(n // 2 + 1) * COLS]
                    dve.tensor_tensor(at, at, bank(k, 4 + (t0 + n) % 4), ALU.add).then_inc(k.tt_free, 1)

        @block.gpsimd
        def _(pool):
            steps = Steps(pool, k.pool_sem)
            steps.n = 1
            sums = acc[:].rearrange("p g n -> p (g n)")

            def load(unit, slot):
                src = io["w_mod"][unit] if isinstance(unit, int) else \
                    io["w_mod"][bass.ds(unit, 1)].rearrange("a p n -> (a p) n")
                pool.dma_start(w_mod[:, slot].rearrange("p k n -> p (k n)"), src).then_inc(k.mod_in[slot], 16)

            def group(g, last):
                for j in range(4):
                    slot = j % 2
                    pool.wait_ge(k.mod_in[slot], g * 32 + 16 * (j // 2 + 1))
                    steps.step(pool.tensor_tensor(prod[:], w_mod[:, slot],
                                                  c_silu[:, 4 * j:4 * j + 4].unsqueeze(2).broadcast_to([P, 4, COLS]),
                                                  ALU.mult))
                    steps.settle()
                    if not last or j < 2:
                        load(g * 4 + (j + 2), slot)
                    steps.step(pool.tensor_tensor(prod[:, 0:2], prod[:, 0:2], prod[:, 2:4], ALU.add))
                    steps.settle()
                    steps.step(pool.tensor_tensor(prod[:, 0], prod[:, 0], prod[:, 1], ALU.add))
                    steps.settle()
                    pool.tensor_tensor(prod[:, 3, 0:1], prod[:, 3, 0:1], prod[:, 3, 1:2], ALU.add)
                    at = sums[:, g * COLS:(g + 1) * COLS] if isinstance(g, int) else sums[:, bass.ds(g * COLS, COLS)]
                    steps.step(pool.tensor_tensor(at, at, prod[:, 0], ALU.add))
                    steps.settle()
            load(0, 0)
            load(1, 1)
            with pool.Fori(0, MOD_GROUPS - 1) as g:
                steps.loop(g, 16)
                group(g, False)
            steps.end(MOD_GROUPS - 1)
            group(MOD_GROUPS - 1, True)
    k.ft += 16 * FFN_QUARTERS
    k.tt += 8 * FFN_QUARTERS
    k.act_n += 16 * FFN_QUARTERS


def modulation(nc, k, acc, gates, mod_cols, scale1, scale2):
    ones = const(k, "ones")
    s = k.dve_steps
    with nc.Block(no_gpsimd_drain=True) as block:
        @block.tensor
        def _(pe):
            for n, section in enumerate((0, 1, 3, 4)):
                for c in range(KC):
                    pe.matmul(bank(k, 0)[:, n * KC + c:n * KC + c + 1],
                              acc[:, section * 4 + c // 4, (c % 4) * P:(c % 4 + 1) * P], ones[:, 0:1],
                              start=True, stop=True)
            for n in range(4):
                pe.matmul(bank(k, 4 + n), ones, acc[:, 8 + n, :], start=True, stop=True)
    for gate in range(2):
        with nc.Block(no_gpsimd_drain=True) as block:
            @block.scalar
            def _(act):
                act.activation(gates[:, gate, :], k.psum[:, 4:8, :].rearrange("p b n -> p (b n)"), ACT.Copy)

            @block.vector
            def _(dve):
                s.eng = dve
                if not gate:
                    s.step(dve.tensor_copy(mod_cols[:], bank(k, 0)[:, 0:64]))
                    s.settle()
                    for dst, at, norm in ((scale1, 16, "norm1"), (scale2, 48, "norm2")):
                        s.step(dve.scalar_tensor_tensor(dst[:], mod_cols[:, at:at + 16], 1.0, cols_of(k, norm),
                                                        ALU.add, ALU.mult))
                    s.settle()
        if not gate:
            with nc.Block(no_gpsimd_drain=True) as block:
                @block.tensor
                def _(pe):
                    for n in range(4):
                        pe.matmul(bank(k, 4 + n), ones, acc[:, 20 + n, :], start=True, stop=True)


def final_norm(nc, k, io, x, weight, squares):
    s = k.dve_steps
    with nc.Block(no_gpsimd_drain=True) as block:
        @block.sync
        def _(sp):
            sp.dma_start(weight[:], io["final_norm"]).then_inc(k.small_in, 16)

        @block.scalar
        def _(act):
            for t in range(TT):
                act.activation(squares, x[:, t, :], ACT.Square, accum_out=k.ssq[:, t:t + 1]).then_inc(k.act_sem, 1)
                act.wait_ge(k.act_sem, k.act_n + t + 1)
            act.activation(k.rms[:], k.ssq[:], ACT.Sqrt, bias=k.eps[:, 0:1], scale=1.0 / D).then_inc(k.act_sem, 1)

        @block.vector
        def _(dve):
            s.eng = dve
            dve.wait_ge(k.act_sem, k.act_n + 3)
            dve.wait_ge(k.small_in, 64)
            s.step(dve.reciprocal(k.rstd[:], k.rms[:]))
            s.settle()
            for t in range(TT):
                s.step(dve.scalar_tensor_tensor(x[:, t, :], x[:, t, :], k.rstd[:, t:t + 1], weight[:],
                                                ALU.mult, ALU.mult))
            s.settle()
    k.act_n += 3


def second_mixer(nc, k, io, x, h_t, gate, scope_sb):
    s = k.dve_steps
    first, _ = STREAM["w_in_2"]
    proj = scope_sb("proj", [P, TT, 5 * COLS])
    ws, gm_norm = scope_sb("gm_ws", [P, GMLP_GROUPS, P]), scope_sb("gm_norm", [P, COLS])
    ssq = scope_sb("proj_ssq", [P, TT, 12])
    squares = scope_sb("squares", [P, TT, 3 * COLS])
    t0 = k.tt
    with nc.Block(no_gpsimd_drain=True) as block:
        @block.sync
        def _(sp):
            sp.dma_start(ws[:], io["gm_ws"]).then_inc(k.small_in, 16)
            sp.dma_start(gm_norm[:], io["gm_norm"]).then_inc(k.small_in, 16)
            for j in range(10):
                load_next(k, sp, first + j, k.tt_done, t0 + 2 * (j // 2 + 1))
            sp.wait_ge(k.small_in, 96)

        @block.tensor
        def _(pe):
            for g in range(5):
                token_group(k, pe, unit_rows(first + 2 * g, KC), h_t, range(KC), t0 + 2 * g)

        @block.scalar
        def _(act):
            for n in range(10):
                act.wait_ge(k.tt_done, t0 + n + 1)
                act.activation(proj[:, n % 2, (n // 2) * COLS:(n // 2 + 1) * COLS], bank(k, 4 + (t0 + n) % 4),
                               ACT.Gelu if n < 4 else ACT.Copy).then_inc(k.tt_free, 1)
    k.tt += 10
    with nc.Block(no_gpsimd_drain=True) as block:
        @block.vector
        def _(dve):
            s.eng = dve
            s.step(dve.tensor_tensor(squares[:], proj[:, :, COLS:4 * COLS], proj[:, :, COLS:4 * COLS], ALU.mult))
            s.step(dve.tensor_tensor(ws[:], ws[:], const(k, "tri_le").unsqueeze(1).broadcast_to([P, GMLP_GROUPS, P]),
                                     ALU.mult))
            s.settle()
            s.step(dve.tensor_reduce(ssq[:], squares[:].rearrange("p t (g n) -> p t g n", n=P), AX.X, ALU.add))
            s.settle()
    with nc.Block(no_gpsimd_drain=True) as block:
        @block.scalar
        def _(act):
            act.activation(ssq[:], ssq[:], ACT.Sqrt, bias=k.eps[:, 0:1], scale=1.0 / P)
    with nc.Block(no_gpsimd_drain=True) as block:
        @block.vector
        def _(dve):
            s.eng = dve
            s.step(dve.reciprocal(ssq[:], ssq[:]))
            s.settle()
            for t in range(TT):
                at = proj[:, t, COLS:4 * COLS].rearrange("p (g n) -> p g n", n=P)
                s.step(dve.tensor_tensor(at, at, ssq[:, t, :].unsqueeze(2).broadcast_to([P, 12, P]), ALU.mult))
            s.settle()
    qk_t = squares[:].rearrange("p t n -> p (t n)")[:, 0:2048].rearrange("p (a h n) -> p a h n", a=2, h=SB_HEADS)
    turn_blocks(nc, k, [([proj[:, t, (2 + a) * COLS + h * P:(2 + a) * COLS + (h + 1) * P] for h in range(SB_HEADS)],
                         qk_t[:, a, :, t * P:(t + 1) * P]) for a in range(2) for t in range(TT)])
    y = scope_sb("y", [P, TT, MIX_GROUPS, P])
    z, sp_, e = (scope_sb(n, [P, SB_HEADS, TT, T]) for n in ("sb_z", "sb_softplus", "sb_exp"))
    with nc.Block(no_gpsimd_drain=True) as block:
        @block.vector
        def _(dve):
            s.eng = dve
            s.step(dve.tensor_scalar(qk_t[:, 0], qk_t[:, 0], col(k, "q_norm"), P ** -0.5, ALU.mult, ALU.mult))
            s.step(dve.tensor_scalar(qk_t[:, 1], qk_t[:, 1], col(k, "k_norm"), None, ALU.mult))
            s.settle()

        @block.tensor
        def _(pe):
            for t in range(TT):
                for g in range(GMLP_GROUPS):
                    pe.matmul(bank(k, 4 + t)[:, g * P:(g + 1) * P], ws[:, g, :],
                              proj[:, t, COLS + g * P:COLS + (g + 1) * P], start=True, stop=True)
    with nc.Block(no_gpsimd_drain=True) as block:
        @block.tensor
        def _(pe):
            for h in range(SB_HEADS):
                for b in range(TT):
                    pe.matmul(bank(k, h)[:, b * T:(b + 1) * T], qk_t[:, 1, h, b * P:(b + 1) * P], qk_t[:, 0, h, :],
                              start=True, stop=True)

        @block.vector
        def _(dve):
            s.eng = dve
            for t in range(TT):
                s.step(dve.tensor_tensor(y[:, t, 0:4, :].rearrange("p g n -> p (g n)"), bank(k, 4 + t), gm_norm[:],
                                         ALU.mult))
            s.settle()
            for g in range(GMLP_GROUPS):
                s.step(dve.scalar_tensor_tensor(y[:, :, g, :], y[:, :, g, :], col(k, "gm_bs", g),
                                                proj[:, :, g * P:(g + 1) * P], ALU.add, ALU.mult))
            s.settle()
    zf, sf, ef = (a[:].rearrange("p h b q -> p (h b q)") for a in (z, sp_, e))
    before = const(k, "before").unsqueeze(1).broadcast_to([P, SB_HEADS, TT * T])

    def heads(a):
        return a[:].rearrange("p h b q -> p h (b q)")
    with nc.Block(no_gpsimd_drain=True) as block:
        @block.vector
        def _(dve):
            s.eng = dve
            ps = k.psum[:, 0:4, :].rearrange("p b n -> p (b n)")
            s.step(dve.tensor_copy(zf, ps))
            s.settle()
            s.step(dve.tensor_scalar(sf, zf, 0.0, None, ALU.max))
            s.settle()
            s.step(dve.scalar_tensor_tensor(ef, sf, -2.0, zf, ALU.mult, ALU.add))
            s.settle()
    with nc.Block(no_gpsimd_drain=True) as block:
        @block.scalar
        def _(act):
            act.activation(ef, ef, ACT.Exp).then_inc(k.act_sem, 1)
            act.wait_ge(k.act_sem, k.act_n + 1)
            act.activation(ef, ef, ACT.Ln, bias=k.one[:, 0:1])
    k.act_n += 1
    with nc.Block(no_gpsimd_drain=True) as block:
        @block.vector
        def _(dve):
            s.eng = dve
            s.step(dve.tensor_tensor(sf, sf, ef, ALU.add))
            s.settle()
            s.step(dve.tensor_tensor(zf, zf, sf, ALU.subtract))
            s.step(dve.tensor_tensor(heads(e), heads(sp_), before, ALU.mult))
            s.settle()
    with nc.Block(no_gpsimd_drain=True) as block:
        @block.tensor
        def _(pe):
            for h in range(SB_HEADS):
                pe.matmul(bank(k, h)[:, 0:T], const(k, "tri_gt"), e[:, h, 0, :], start=True, stop=False)
                pe.matmul(bank(k, h)[:, 0:T], const(k, "ones"), e[:, h, 1, :], start=False, stop=True)
                pe.matmul(bank(k, h)[:, T:2 * T], const(k, "tri_gt"), e[:, h, 1, :], start=True, stop=True)
    with nc.Block(no_gpsimd_drain=True) as block:
        @block.vector
        def _(dve):
            s.eng = dve
            s.step(dve.tensor_tensor(zf, zf, k.psum[:, 0:4, :].rearrange("p b n -> p (b n)"), ALU.subtract))
            s.settle()
    with nc.Block(no_gpsimd_drain=True) as block:
        @block.scalar
        def _(act):
            act.activation(zf, zf, ACT.Exp)
    with nc.Block(no_gpsimd_drain=True) as block:
        @block.vector
        def _(dve):
            s.eng = dve
            s.step(dve.tensor_tensor(heads(z), heads(z), before, ALU.mult))
            s.settle()
    with nc.Block(no_gpsimd_drain=True) as block:
        @block.tensor
        def _(pe):
            for t in range(TT):
                for h in range(SB_HEADS):
                    for b in range(t + 1):
                        pe.matmul(bank(k, t)[:, h * P:(h + 1) * P], z[:, h, b, t * P:(t + 1) * P],
                                  proj[:, b, 4 * COLS + h * P:4 * COLS + (h + 1) * P], start=(b == 0), stop=(b == t))
    y_ssq = scope_sb("y_ssq", [P, TT, MIX_GROUPS])
    y_sq = squares[:].rearrange("p t n -> p (t n)")[:, 0:2048].rearrange("p (t g n) -> p t g n", t=TT, n=P)
    with nc.Block(no_gpsimd_drain=True) as block:
        @block.vector
        def _(dve):
            s.eng = dve
            for t in range(TT):
                s.step(dve.tensor_copy(y[:, t, 4:8, :].rearrange("p g n -> p (g n)"), bank(k, t)))
            s.settle()
            s.step(dve.tensor_tensor(y_sq, y[:], y[:], ALU.mult))
            s.settle()
            s.step(dve.tensor_reduce(y_ssq[:], y_sq, AX.X, ALU.add))
            s.settle()
    with nc.Block(no_gpsimd_drain=True) as block:
        @block.scalar
        def _(act):
            act.activation(y_ssq[:], y_ssq[:], ACT.Sqrt, bias=k.eps[:, 0:1], scale=1.0 / P)
    with nc.Block(no_gpsimd_drain=True) as block:
        @block.vector
        def _(dve):
            s.eng = dve
            s.step(dve.reciprocal(y_ssq[:], y_ssq[:]))
            s.settle()
            s.step(dve.tensor_tensor(y[:], y[:], y_ssq[:].unsqueeze(3).broadcast_to([P, TT, MIX_GROUPS, P]), ALU.mult))
            s.settle()
    y_t = sf.rearrange("p (g t) -> p g t", t=T)
    turn_blocks(nc, k, [([y[:, t, 4 * g + c, :] for c in range(4)], y_t[:, 4 * g:4 * g + 4, t * P:(t + 1) * P])
                        for t in range(TT) for g in range(2)])
    with nc.Block(no_gpsimd_drain=True) as block:
        @block.vector
        def _(dve):
            s.eng = dve
            for g in range(MIX_GROUPS):
                s.step(dve.tensor_scalar(y_t[:, g, :], y_t[:, g, :], col(k, "out_norm", g), None, ALU.mult))
            s.settle()
    first, t0 = STREAM["w_out_2"][0], k.tt
    gated = ef.rearrange("p (n c) -> p n c", c=COLS)
    with nc.Block(no_gpsimd_drain=True) as block:
        @block.sync
        def _(sp):
            for j in range(4):
                load_next(k, sp, first + j, k.tt_done, t0 + 2 * (j + 1))

        @block.tensor
        def _(pe):
            for n in range(4):
                token_group(k, pe, unit_rows(first + n, MIX_GROUPS), y_t, range(MIX_GROUPS), t0 + 2 * n)

        @block.vector
        def _(dve):
            s.eng = dve
            for n in range(8):
                dve.wait_ge(k.tt_done, t0 + n + 1)
                own = slice((n // 2) * COLS, (n // 2 + 1) * COLS)
                dve.tensor_tensor(gated[:, n % 4, :], bank(k, 4 + (t0 + n) % 4), gate[:, own], ALU.mult)\
                   .then_inc(k.tt_free, 1)
                dve.wait_ge(k.tt_free, 4 + t0 + n + 1)
                s.step(dve.tensor_tensor(x[:, n % 2, own], x[:, n % 2, own], gated[:, n % 4, :], ALU.add))
            s.settle()
    k.tt += 8


def route(nc, k, io, h_t, comb, scope_sb):
    s = k.dve_steps
    w, b = scope_sb("w_route", [P, KC, 36]), scope_sb("b_route", [1, 36])
    logits = scope_sb("logits", [P, TT, 36])
    e4, m4 = scope_sb("group_exp", [P, TT, GROUPS]), scope_sb("group_mask", [P, TT, GROUPS])
    one, p_group = scope_sb("route_one", [P, TT, 1]), scope_sb("p_group", [P, TT])
    total = scope_sb("group_total", [P, TT])
    pick = scope_sb("pick", [P, TT, GROUPS, PER_GROUP])
    chosen, rest = scope_sb("chosen", [P, TT, PER_GROUP]), scope_sb("rest", [P, TT, PER_GROUP])
    tmp = scope_sb("route_tmp", [P, TT, PER_GROUP])
    hot = [scope_sb(f"hot{n}", [P, TT, PER_GROUP]) for n in range(2)]
    v = [scope_sb(f"top{n}", [P, TT, 1]) for n in range(2)]
    w1 = scope_sb("weight1", [P, TT, 1])
    with nc.Block(no_gpsimd_drain=True) as block:
        @block.sync
        def _(sp):
            sp.dma_start(w[:], io["w_route"]).then_inc(k.small_in, 16)
            sp.dma_start(b[:], io["b_route"]).then_inc(k.small_in, 16)

        @block.tensor
        def _(pe):
            pe.wait_ge(k.small_in, 128)
            for t in range(TT):
                ps = bank(k, t)[:, 0:36]
                for c in range(KC):
                    pe.matmul(ps, h_t[:, c, t * P:(t + 1) * P], w[:, c, :], start=(c == 0), stop=False)
                pe.matmul(ps, const(k, "ones")[0:1, :], b[:], start=False, stop=True)

    def first_hot(dve, dst, src, top, n, work):
        index = const(k, "index")[:, 0:n].unsqueeze(1).broadcast_to([P, TT, n])
        s.step(dve.tensor_tensor(dst, src, top.broadcast_to([P, TT, n]), ALU.is_ge))
        s.settle()
        s.step(dve.tensor_tensor(work, dst, index, ALU.mult))
        s.settle()
        s.step(dve.tensor_reduce(one[:], work, AX.X, ALU.min))
        s.settle()
        s.step(dve.tensor_tensor(dst, index, one[:].broadcast_to([P, TT, n]), ALU.is_equal))
        s.settle()
    with nc.Block(no_gpsimd_drain=True) as block:
        @block.vector
        def _(dve):
            s.eng = dve
            for t in range(TT):
                s.step(dve.tensor_copy(logits[:, t, :], bank(k, t)[:, 0:36]))
            s.settle()
            g = logits[:, :, 0:GROUPS]
            s.step(dve.tensor_reduce(v[0][:], g, AX.X, ALU.max))
            s.settle()
            s.step(dve.tensor_tensor(e4[:], g, v[0][:].broadcast_to([P, TT, GROUPS]), ALU.subtract))
            first_hot(dve, m4[:], g, v[0][:], GROUPS, tmp[:, :, 0:GROUPS])
            for t in range(TT):
                s.step(dve.tensor_tensor(pick[:, t], logits[:, t, GROUPS:].rearrange("p (g j) -> p g j", g=GROUPS),
                                         m4[:, t, :].unsqueeze(2).broadcast_to([P, GROUPS, PER_GROUP]), ALU.mult))
            s.settle()
            s.step(dve.tensor_reduce(chosen[:], pick[:].rearrange("p t g j -> p t j g"), AX.X, ALU.add))
            s.settle()
            s.step(dve.tensor_reduce(v[0][:], chosen[:], AX.X, ALU.max))
            s.settle()
            first_hot(dve, hot[0][:], chosen[:], v[0][:], PER_GROUP, tmp[:])
            s.step(dve.scalar_tensor_tensor(rest[:], hot[0][:], -3.0e38, chosen[:], ALU.mult, ALU.add))
            s.settle()
            s.step(dve.tensor_reduce(v[1][:], rest[:], AX.X, ALU.max))
            s.settle()
            first_hot(dve, hot[1][:], rest[:], v[1][:], PER_GROUP, tmp[:])
            s.step(dve.tensor_tensor(w1[:], v[1][:], v[0][:], ALU.subtract))
            s.settle()
    with nc.Block(no_gpsimd_drain=True) as block:
        @block.scalar
        def _(act):
            act.activation(w1[:], w1[:], ACT.Exp)
            for t in range(TT):
                act.activation(e4[:, t, :], e4[:, t, :], ACT.Exp, accum_out=total[:, t:t + 1])
    with nc.Block(no_gpsimd_drain=True) as block:
        @block.vector
        def _(dve):
            s.eng = dve
            s.step(dve.scalar_tensor_tensor(p_group[:], w1[:].rearrange("p t a -> p (t a)"), 1.0, total[:],
                                            ALU.add, ALU.mult))
            s.settle()
            s.step(dve.reciprocal(p_group[:], p_group[:]))
            for n in range(2):
                if n:
                    s.step(dve.tensor_tensor(hot[1][:], hot[1][:], w1[:].broadcast_to([P, TT, PER_GROUP]), ALU.mult))
            s.settle()
            s.step(dve.tensor_tensor(hot[0][:], hot[0][:], hot[1][:], ALU.add))
            s.settle()
            s.step(dve.tensor_tensor(hot[0][:], hot[0][:],
                                     p_group[:].unsqueeze(2).broadcast_to([P, TT, PER_GROUP]), ALU.mult))
            s.settle()
            for t in range(TT):
                s.step(dve.tensor_tensor(comb[:, t, :].rearrange("p (g j) -> p g j", g=GROUPS),
                                         hot[0][:, t, :].unsqueeze(1).broadcast_to([P, GROUPS, PER_GROUP]),
                                         m4[:, t, :].unsqueeze(2).broadcast_to([P, GROUPS, PER_GROUP]), ALU.mult))
            s.settle()


MOE_HALVES = 6
RAW_SLOTS, SPLIT_SLOTS = 6, 3
HALF = UNIT // 2


def load_half(k, sp, unit, half, down, slot):
    src = k.stream[unit] if isinstance(unit, int) else k.stream[bass.ds(unit, 1)].rearrange("a p n -> (a p) n")
    if down:
        src = src.rearrange("p (c n) -> p c n", c=2)[:, :, half * (D // 2):(half + 1) * (D // 2)]
        dst = k.raw[:, slot].rearrange("p (c n) -> p c n", c=2)
    else:
        src, dst = src[:, half * HALF:(half + 1) * HALF], k.raw[:, slot]
    sp.dma_start(dst, src).then_inc(k.raw_in[slot], 16)


def first_halves(k, sp):
    first, _ = STREAM["moe"]
    for s in range(RAW_SLOTS):
        load_half(k, sp, first + 3 * (s // 4) + s % 4 // 2, s % 2, False, s)


def experts(nc, k, h_hi, h_lo, comb, acc, silu, hid, hid_hi, hid_lo):
    first, _ = STREAM["moe"]
    f0, t0 = k.ft, k.tt
    U = 2
    trips = (EXPERTS - 2) // U

    def at(e, per, c=0):
        i, n = e
        return n * per + c if i is None else i * (U * per) + (n * per + c)

    def is_step(e, n):
        return e[0] is None and e[1] == n

    def slots(j):
        return (j - 2) % RAW_SLOTS, (j - 2) % SPLIT_SLOTS

    def split(e, j):
        raw, part = slots(j)
        return k.raw[:, raw], k.w_hi[:, part], k.w_lo[:, part]

    with nc.Block(no_gpsimd_drain=True) as block:
        @block.sync
        def _(sp):
            def load(e, j, unit, half, down):
                sp.wait_ge(k.lo_done, at(e, 6, j - 2 - RAW_SLOTS + 1))
                load_half(k, sp, unit, half, down, slots(j)[0])

            def step(e, last=False):
                for j in (2, 3):
                    load(e, j, at(e, 3, first + 1), j % 2, False)
                for j in (4, 5):
                    load(e, j, at(e, 3, first - 1), j % 2, True)
                for j in (6, 7):
                    load(e, j, at(e, 3, first + (2 if last else 3)), j % 2, last)
            with sp.Fori(0, trips) as i:
                for r in range(U):
                    step((i, 1 + r))
            step((None, EXPERTS - 1), last=True)

        @block.scalar
        def _(act):
            def high(e, j):
                raw, part = slots(j)
                act.wait_ge(k.raw_in[raw], at(e, 16, 16 * ((j - 2) // RAW_SLOTS + 1)))
                if is_step(e, 0):
                    if j > 4:
                        act.wait_ge(k.gate_up_used, j - 4)
                elif j == 2:
                    act.wait_ge(k.gate_up_used, at(e, 4))
                    act.wait_ge(k.tt_done, at(e, 8, t0 - 8))
                elif j == 7:
                    act.wait_ge(k.tt_done, at(e, 8, t0 - 4))
                else:
                    act.wait_ge(k.gate_up_used, at(e, 4, j - 2))
                act.activation(k.w_hi[:, part], k.raw[:, raw], ACT.Copy).then_inc(k.hi_done, 1)

            def gate(e):
                act.wait_ge(k.gate_up_used, at(e, 4, 4))
                if not is_step(e, 0):
                    act.wait_ge(k.hid_ready, at(e, 1))
                act.activation(silu[:], k.psum[:, 0:4:2, 0:T], ACT.Silu).then_inc(k.silu_done, 1)

            def step(e):
                for j in (2, 3, 4, 5):
                    high(e, j)
                gate(e)
                for j in (6, 7):
                    high(e, j)
            for j in (2, 3, 4, 5, 6, 7):
                high((None, 0), j)
            gate((None, 0))
            with act.Fori(0, trips) as i:
                for r in range(U):
                    step((i, 1 + r))
            step((None, EXPERTS - 1))

        @block.vector
        def _(dve):
            s = Steps(dve, k.dve_sem)
            s.n = k.dve_steps.n

            def low(e, j):
                raw, part = slots(j)
                dve.wait_ge(k.hi_done, at(e, 6, j - 2 + 1))
                dve.tensor_tensor(k.w_lo[:, part], k.raw[:, raw], k.w_hi[:, part].bitcast(F32), ALU.subtract)\
                   .then_inc(k.lo_done, 1)

            def hidden(e):
                b = e[1] % 2
                dve.wait_ge(k.silu_done, at(e, 1, 1))
                if not is_step(e, 0):
                    dve.wait_ge(k.hid_ready, at(e, 1))
                dve.tensor_tensor(hid[:], silu[:], k.psum[:, 1:4:2, 0:T], ALU.mult).then_inc(k.ft_free, 4)
                dve.wait_ge(k.ft_free, at(e, 4, f0 + 8))
                dve.tensor_copy(hid_hi[:, b], hid[:]).then_inc(k.hid_high, 1)
                dve.wait_ge(k.hid_high, at(e, 1, 1))
                dve.tensor_tensor(hid_lo[:, b], hid[:], hid_hi[:, b].bitcast(F32), ALU.subtract)\
                   .then_inc(k.hid_ready, 1)

            def gather(e, ns):
                for n in ns:
                    dve.wait_ge(k.tt_done, at(e, 8, t0 - 8 + n + 1))
                    out = acc[:, n % 2, (n // 2) * COLS:(n // 2 + 1) * COLS]
                    i, c = e
                    expert = slice(c - 1, c) if i is None else bass.ds(i * U + (c - 1), 1)
                    dve.scalar_tensor_tensor(out, bank(k, 4 + (t0 + n) % 4), comb[:, n % 2, expert],
                                             out, ALU.mult, ALU.add).then_inc(k.tt_free, 1)

            def step(e):
                for j in (2, 3, 4, 5):
                    low(e, j)
                hidden(e)
                low(e, 6)
                gather(e, range(4))
                low(e, 7)
                gather(e, range(4, 8))
            for j in (2, 3, 4, 5, 6, 7):
                low((None, 0), j)
            hidden((None, 0))
            with dve.Fori(0, trips) as i:
                for r in range(U):
                    step((i, 1 + r))
            step((None, EXPERTS - 1))
            gather((None, EXPERTS), range(8))

        @block.tensor
        def _(pe):
            def product(out, lhs, rhs, first_of, last_of):
                pe.matmul(out, lhs[0], rhs[0], start=first_of, stop=False)
                pe.matmul(out, lhs[0], rhs[1], start=False, stop=False)
                return pe.matmul(out, lhs[1], rhs[0], start=False, stop=last_of)

            def gate_up(e):
                pe.wait_ge(k.ft_free, at(e, 4, f0 + 4))
                for half in range(4):
                    j = half + 2 if is_step(e, 0) else half
                    part = slots(j)[1]
                    hi, lo = (w[:, part].rearrange("p (c n) -> p c n", c=4) for w in (k.w_hi, k.w_lo))
                    pe.wait_ge(k.lo_done, at(e, 6, j - 2 + 1))
                    for m in range(4):
                        for c in range(4):
                            cols, chunk = slice(m * P, (m + 1) * P), 4 * half + c
                            mm = product(bank(k, m)[:, 0:T], (hi[:, c, cols], lo[:, c, cols]),
                                         (h_hi[:, chunk, :], h_lo[:, chunk, :]), chunk == 0, chunk == KC - 1)
                    mm.then_inc(k.gate_up_used, 1)

            def down(e):
                b = (e[1] - 1) % 2
                pe.wait_ge(k.hid_ready, at(e, 1))
                for half in range(2):
                    j = half if is_step(e, EXPERTS) else 4 + half
                    part = slots(j)[1]
                    pe.wait_ge(k.lo_done, at(e, 6, j - 2 + 1))
                    hi, lo = (w[:, part].rearrange("p (c n) -> p c n", c=2) for w in (k.w_hi, k.w_lo))
                    for n in range(2):
                        for t in range(TT):
                            tile = 4 * half + 2 * n + t
                            pe.wait_ge(k.tt_free, at(e, 8, t0 - 8 + tile + 1))
                            for c in range(2):
                                rows, cols = slice(t * P, (t + 1) * P), slice(n * COLS, (n + 1) * COLS)
                                mm = product(bank(k, 4 + (t0 + tile) % 4),
                                             (hid_hi[:, b, c, rows], hid_lo[:, b, c, rows]),
                                             (hi[:, c, cols], lo[:, c, cols]), c == 0, c == 1)
                            mm.then_inc(k.tt_done, 1)
            gate_up((None, 0))
            with pe.Fori(0, trips) as i:
                for r in range(U):
                    gate_up((i, 1 + r))
                    down((i, 1 + r))
            gate_up((None, EXPERTS - 1))
            down((None, EXPERTS - 1))
            down((None, EXPERTS))
    k.ft += 4 * EXPERTS
    k.tt += 8 * EXPERTS


def finish(nc, k, io, x, acc, gate):
    s = k.dve_steps
    with nc.Block(no_gpsimd_drain=True) as block:
        @block.vector
        def _(dve):
            s.eng = dve
            for t in range(TT):
                s.step(dve.tensor_tensor(acc[:, t, :], acc[:, t, :], gate, ALU.mult))
                s.settle()
                dve.tensor_tensor(x[:, t, :], x[:, t, :], acc[:, t, :], ALU.add).then_inc(k.out_ready, 1)

        @block.sync
        def _(sp):
            for t in range(TT):
                sp.wait_ge(k.out_ready, t + 1)
                sp.dma_start(io["out"][t * P:(t + 1) * P, :], x[:, t, :]).then_inc(k.out_written, 16)
            sp.wait_ge(k.out_written, 16 * TT)


def program(nc, io):
    k = Kit(io["stream"])
    with ExitStack() as ctx:
        def sb(name, shape, scope=ctx, dtype=F32, side=None):
            return scope.enter_context(nc.sbuf_tensor(name, shape, dtype, side=side))

        def kept(name, shape, dtype=F32):
            return sb(name, shape, dtype=dtype, side="right")

        def sem(name):
            return ctx.enter_context(nc.semaphore(name))
        k.norm_ssq, k.norm_rms, k.norm_diag, k.norm_mm = \
            sem("norm_ssq"), sem("norm_rms"), sem("norm_diag"), sem("norm_mm")
        k.ft_done, k.ft_free, k.tt_done, k.tt_free = \
            sem("ft_done"), sem("ft_free"), sem("tt_done"), sem("tt_free")
        k.turned, k.turn_taken, k.gates_ready, k.inv_masked = \
            sem("turned"), sem("turn_taken"), sem("gates_ready"), sem("inv_masked")
        k.inv_first, k.inv_second, k.inv_taken, k.hi_done = \
            sem("inv_first"), sem("inv_second"), sem("inv_taken"), sem("hi_done")
        k.lo_done, k.gate_up_used, k.silu_done, k.hid_high = \
            sem("lo_done"), sem("gate_up_used"), sem("silu_done"), sem("hid_high")
        k.hid_ready, k.dve_sem, k.act_sem, k.pe_sem = \
            sem("hid_ready"), sem("dve_sem"), sem("act_sem"), sem("pe_sem")
        k.pool_sem, k.consts_in, k.out_ready, k.out_written = \
            sem("pool_sem"), sem("consts_in"), sem("out_ready"), sem("out_written")
        k.small_in = \
            sem("small_in")
        k.loaded = [sem(f"loaded{n}") for n in range(SLOTS)]
        k.raw_in = [sem(f"raw_in{n}") for n in range(RAW_SLOTS)]
        k.x_in, k.mem_in, k.mod_in = ([sem(f"{what}{n}") for n in range(2)] for what in ("x_in", "mem_in", "mod_in"))
        k.dve_steps = Steps(None, k.dve_sem)
        k.psum = ctx.enter_context(nc.psum_tensor("psum", [P, 8, 512], F32))
        k.consts = kept("consts", [P, N_CONST])
        k.cols = kept("cols", [P, N_COLS])
        x = kept("x", [P, TT, D])
        k.diag = kept("diag", [P, TT, P])
        k.ssq, k.rms, k.rstd = kept("ssq", [P, TT]), kept("rms", [P, TT]), kept("rstd", [P, TT])
        k.eps, k.one = kept("eps", [P, 1]), kept("one", [P, 1])
        ring = ctx.enter_context(ExitStack())
        k.ring = sb("ring", [P, SLOTS, UNIT_KC, COLS], ring)

        def begin(sp):
            sp.dma_start(k.consts[:], io["consts"]).then_inc(k.consts_in, 16)
            sp.dma_start(k.cols[:], io["cols"]).then_inc(k.consts_in, 16)
            for t in range(TT):
                sp.dma_start(x[:, t, :], io["x"][t * P:(t + 1) * P, :]).then_inc(k.x_in[t], 16)
            for u in range(SLOTS):
                load_unit(k, sp, u, u)
            sp.wait_ge(k.consts_in, 32)
        with nc.Block(no_gpsimd_drain=True) as block:
            @block.vector
            def _(dve):
                dve.memset(k.eps[:], EPS)
                dve.memset(k.one[:], 1.0)

            @block.tensor
            def _(pe):
                pe.sem_inc(k.ft_free, 4)
                pe.sem_inc(k.tt_free, 4)
        with ExitStack() as mixer:
            mixed = sb("mixed", [P, 16, T], mixer)
            u = sb("u", [P, KC, T], mixer)
            norm_turn(nc, k, x, u, lambda c: col(k, "mix_norm", c), sync=begin, await_src=k.x_in)
            with ExitStack() as dn:
                qkvz = sb("qkvz", [P, 32, T], dn)
                w_gate = sb("w_gate", [P, KC, 16], dn)
                bufs = [sb(f"dn{n}", [P, TT, 8, P], dn) for n in range(4)]
                q_tm, k_tm, v_tm, kb_tm = bufs
                X = sb("dn_x", [P, 8, 2, P], dn)
                state = sb("dn_state", [P, 8, P], dn)
                k.beta, k.g, k.sp_pos = (sb(n, [P, TT, 8], dn) for n in ("beta", "g", "sp_pos"))
                k.a_exp, k.egc, k.o_ssq = sb("a_exp", [P, 8], dn), sb("egc", [P, 16], dn), sb("o_ssq", [P, 8], dn)
                k.qk_ssq = sb("qk_ssq", [P, 2, TT, 8], dn)
                k.scratch8 = X[:].rearrange("p h a n -> p (h a n)")
                k.inv_u, k.inv_w = q_tm[:, 0], q_tm[:, 1]
                k.inv_m, k.inv_p = kb_tm[:, 0], kb_tm[:, 1]
                KQ = qkvz[:, 0:16, :].rearrange("p (h t) (a n) -> p h t a n", t=TT, n=P)
                kT = qkvz[:, 16:24, :].rearrange("p h (t n) -> p h t n", n=P)
                with nc.Block(no_gpsimd_drain=True) as block:
                    @block.sync
                    def _(sp):
                        sp.dma_start(w_gate[:], io["w_gate"]).then_inc(k.small_in, 16)
                        sp.wait_ge(k.small_in, 16)
                deltanet_project(nc, k, u, qkvz)
                deltanet_prepare(nc, k, u, qkvz, w_gate, q_tm, k_tm, v_tm, kb_tm, KQ, kT)
                for t in range(TT):
                    deltanet_tile(nc, k, t, v_tm, k_tm, KQ, kT, X, k.inv_m, k.inv_p, state, qkvz[:, 24:32, :], mixed)
            with ExitStack() as rw:
                mix = sb("rw_mix", [P, 26, T], rw)
                k.one_less_mu, k.one_less_ka = sb("one_less_mu", [P, 26], rw), sb("one_less_ka", [P, 8], rw)
                AR = sb("rw_ar", [P, RW_TILES, TT, 2, P], rw)
                sig = sb("rw_sig", [P, TT, 1024], rw)
                neg, a_b, gate = (sb(n, [P, RW_TILES, T], rw) for n in ("rw_neg", "rw_ab", "rw_gate"))
                k.tanh = sb("rw_tanh", [P, T], rw)
                k.carry, k.y_mean, k.y_ssq = (sb(n, [P, 8], rw) for n in ("rw_carry", "rw_mean", "rw_ssq"))
                k.gn_eps = sb("gn_eps", [P, 1], rw)
                state = sb("rw_state", [P, RW_TILES, RW_DIM], rw)
                lora = AR[:].rearrange("p c t a n -> p (c t a n)")[:, 0:3072].rearrange("p (a n) -> p a n", a=3)
                with nc.Block(no_gpsimd_drain=True) as block:
                    @block.sync
                    def _(sp):
                        sp.dma_start(lora, io["lora"]).then_inc(k.small_in, 16)

                    @block.vector
                    def _(dve):
                        dve.memset(k.gn_eps[:], RW_GN_EPS)
                rwkv_project(nc, k, u, mix)
                kk, scratch = u[:, 0:8, :], u[:, 8:16, :]
                rwkv_prepare(nc, k, mix, lora, AR, sig, neg, a_b, gate, kk, scratch, mixed[:, 8:16, :])
                X = mix[:, 0:8, :].rearrange("p h (a n) -> p h a n", a=2)
                v_tm = sig
                turn_blocks(nc, k, [([mix[:, 16 + 4 * g + c, t * P:(t + 1) * P] for c in range(4)],
                                     v_tm[:, t, 512 * g:512 * g + 512].rearrange("p (c n) -> p c n", n=P))
                                    for t in range(TT) for g in range(2)])
                Y = mix[:, 16:24, :].rearrange("p h (a n) -> p h a n", a=2)
                k.inv_u, k.inv_w, k.inv_m, k.inv_p = (u[:, 4 * n:4 * n + 4, :].rearrange("p a (b n) -> p (a b) n", n=P)
                                                      for n in range(4))
                flat = neg[:].rearrange("p c t -> p (c t)")
                b_tm, k_tm, R, U = (flat[:, 512 * n:512 * n + 512] for n in range(4))
                y, tmp = mix[:, 24:26, :].rearrange("p c t -> p (c t)"), sb("rw_tmp", [P, 512], rw)[:]
                for t in range(TT):
                    for half in range(2):
                        rwkv_batch(nc, k, t, half, X, Y, AR, a_b, mix[:, 8:16, :], v_tm, b_tm, k_tm, R, U, y, tmp,
                                   state, gate, mixed[:, 8:16, :])
            mixer_out(nc, k, mixed, x)
        with ExitStack() as xa:
            mem, h_t, mem_t = (sb(n, [P, TT, D], xa) for n in ("mem", "xa_h", "mem_t"))
            with nc.Block(no_gpsimd_drain=True) as block:
                @block.sync
                def _(sp):
                    for t in range(TT):
                        sp.dma_start(mem[:, t, :], io["mem"][t * P:(t + 1) * P, :]).then_inc(k.mem_in[t], 16)
            k.dve_steps_before = k.dve_steps.n
            cross_attention(nc, k, x, lambda n, shape: sb(n, shape, xa), mem, features(h_t), features(mem_t), k.mem_in)
        shared = kept("shared", [P, TT, D])
        mod_cols, scale1, scale2 = kept("mod_cols", [P, 64]), kept("scale1", [P, 16]), kept("scale2", [P, 16])
        norm_turn(nc, k, x, features(shared), lambda c: col(k, "ffn_norm", c))
        with ExitStack() as ffn:
            hid, relu = sb("ffn_hid", [P, KC, T], ffn), sb("ffn_relu", [P, 2, T], ffn)
            acc = sb("mod_acc", [P, MOD_COLS // COLS, COLS], ffn)
            w_mod, prod = sb("w_mod", [P, 2, 4, COLS], ffn), sb("mod_prod", [P, 4, COLS], ffn)
            c_silu = sb("c_silu", [P, KC], ffn)
            mlp_and_modulation(nc, k, io, x, features(shared), hid, relu, acc, w_mod, prod, c_silu)
            modulation(nc, k, acc, shared, mod_cols, scale1, scale2)
            weight = w_mod[:].rearrange("p a k n -> p (a k n)")[:, 0:D]
            final_norm(nc, k, io, x, weight, hid[:, 0:8, :].rearrange("p a t -> p (a t)"))
        with ExitStack() as second:
            h_t = sb("h_t", [P, KC, T], second)
            norm_turn(nc, k, x, h_t, lambda c: scale1[:, c:c + 1], lambda c: mod_cols[:, c:c + 1])
            with ExitStack() as mixer:
                second_mixer(nc, k, io, x, h_t, shared[:, 0, :], lambda n, shape: sb(n, shape, mixer))
        ring.close()
        h_hi, h_lo = (kept(n, [P, KC, T], F32R) for n in ("h_hi", "h_lo"))
        comb, acc = kept("comb", [P, TT, EXPERTS]), kept("moe_acc", [P, TT, D])
        k.raw = sb("raw", [P, RAW_SLOTS, HALF])
        with ExitStack() as routing:
            h_t = sb("h2_t", [P, KC, T], routing)
            norm_turn(nc, k, x, h_t, lambda c: scale2[:, c:c + 1], lambda c: mod_cols[:, 32 + c:33 + c],
                      sync=lambda sp: first_halves(k, sp))
            with nc.Block(no_gpsimd_drain=True) as block:
                @block.scalar
                def _(act):
                    act.activation(h_hi[:], h_t[:], ACT.Copy)

                @block.vector
                def _(dve):
                    dve.memset(acc[:], 0.0)
            with nc.Block(no_gpsimd_drain=True) as block:
                @block.vector
                def _(dve):
                    dve.tensor_tensor(h_lo[:], h_t[:], h_hi[:].bitcast(F32), ALU.subtract)
            route(nc, k, io, h_t, comb, lambda n, shape: sb(n, shape, routing))
        k.w_hi, k.w_lo = (sb(n, [P, SPLIT_SLOTS, HALF], dtype=F32R) for n in ("w_hi", "w_lo"))
        silu, hid = sb("moe_silu", [P, 2, T]), sb("moe_hid", [P, 2, T])
        hid_hi, hid_lo = (sb(n, [P, 2, 2, T], dtype=F32R) for n in ("hid_hi", "hid_lo"))
        experts(nc, k, h_hi, h_lo, comb, acc, silu, hid, hid_hi, hid_lo)
        finish(nc, k, io, x, acc, shared[:, 1, :])




def lay_out(a):
    def units(w, order):
        w = w.reshape(-1, UNIT_KC, P, w.shape[1] // COLS, COLS)
        w = w.transpose(3, 0, 2, 1, 4) if order == "columns" else w.transpose(0, 3, 2, 1, 4)
        return w.reshape(-1, P, UNIT)

    w_in = a["w_in"][0]
    dn_cols = 4 * 1024
    rw = w_in[:, dn_cols + 16:]
    parts = [units(w_in[:, :dn_cols], "columns"), units(rw[:, :3072], "columns"),
             rw[:, 3072:].reshape(KC, P, 256).transpose(1, 0, 2).reshape(1, P, UNIT),
             units(a["w_out"][0], "columns"), units(a["xa_wk"][0], "columns"), units(a["xa_wv"][0], "columns"),
             units(a["xa_wq"][0], "columns"),
             a["xa_wo"][0].reshape(2, 2, P, D).transpose(0, 2, 1, 3).reshape(2, P, UNIT)]
    for q in range(FFN_QUARTERS):
        parts += [units(a["ffn_w1"][0][:, q * D:(q + 1) * D], "columns"),
                  units(a["ffn_w2"][0][q * D:(q + 1) * D], "columns")]
    parts += [units(a["w_in_2"][0], "columns"), units(a["w_out_2"][0], "columns")]
    for e in range(EXPERTS):
        gate_up = np.stack([a["w_gate_2"][0, e].reshape(D, 2, P), a["w_up_2"][0, e].reshape(D, 2, P)], 2)
        gate_up = gate_up.reshape(D, COLS)
        parts += [units(gate_up, "columns"),
                  a["w_down_2"][0, e].reshape(2, P, D).transpose(1, 0, 2).reshape(1, P, UNIT)]
    stream = np.concatenate(parts)
    assert stream.shape == (UNITS, P, UNIT), stream.shape

    def tiles(v):
        return np.ascontiguousarray(v).reshape(-1, P).T
    cols = {
        "mix_norm": tiles(a["mix_norm_w"][0]),
        "conv": a["dn_conv_w"][0].reshape(4, DN_TILES, P).transpose(2, 1, 0).reshape(P, -1),
        "dn_norm": tiles(a["dn_norm_w"][0]), "mu": tiles(a["rw_mu"][0]), "a0": tiles(a["rw_a0"][0]),
        "k_k": tiles(a["rw_k_k"][0]), "k_a": tiles(a["rw_k_a"][0]), "r_k": tiles(a["rw_r_k"][0]),
        "ln_w": tiles(a["rw_ln_w"][0]), "ln_b": tiles(a["rw_ln_b"][0]), "xa_norm": tiles(a["xa_norm_w"][0]),
        "mem_norm": tiles(a["mem_norm_w"][0]), "ffn_norm": tiles(a["ffn_norm_w"][0]),
        "norm1": tiles(a["norm1_g_2"][0]), "norm2": tiles(a["norm2_g_2"][0]), "out_norm": tiles(a["out_norm_g_2"][0]),
        "q_norm": tiles(a["q_norm_g_2"][0]), "k_norm": tiles(a["k_norm_g_2"][0]), "gm_bs": a["gm_bs_2"][0].T,
        "c": tiles(a["c_2"][0]),
        "dn_gate": np.concatenate([np.broadcast_to(a["dn_a_log"][0], (P, 8)),
                                   np.broadcast_to(a["dn_dt_bias"][0], (P, 8))], 1),
    }
    cols = np.concatenate([cols[n] for n in COL], 1)
    m, j = np.arange(P)[:, None], np.arange(P)[None, :]
    levels = []
    for level in range(7):
        s = 1 << level
        levels.append((j // s % 2 == 1) & (m // s % 2 == 0) & (m // (2 * s) == j // (2 * s)))
    mid = m < P // 2
    consts = {
        "ident": m == j, "ones": m >= 0 * j, "tri_le": m <= j, "tri_gt": m > j, "levels": np.concatenate(levels, 1),
        "strict_incl": np.concatenate([m < j, m <= j], 1), "head_ones": m // RW_DIM == j // RW_DIM,
        "g_incl": (m <= j) * 1.0 - mid, "g_excl": (m < j) * 1.0 - mid, "g_pre": mid, "g_post": ~mid,
        "before": np.concatenate([m + P * b < np.arange(T)[None, :] for b in range(TT)], 1),
        "index": np.broadcast_to(np.arange(PER_GROUP) - 99.0, (P, PER_GROUP)),
    }
    consts = np.concatenate([np.asarray(consts[n], np.float32) for n in CONST], 1)
    lora = np.zeros((P, 3, 1024), np.float32)
    lora[0:64, 0], lora[64, 0] = a["rw_w2"][0], a["rw_w0"][0]
    lora[64:128, 1], lora[:, 2] = a["rw_a2"][0], a["rw_g2"][0]
    w_route = np.concatenate([a["w_group_2"][0], a["w_route_2"][0]], 1)
    return {
        "stream": stream, "cols": cols, "consts": consts, "x": a["x"][0], "mem": a["mem"][0],
        "w_gate": w_in[:, dn_cols:dn_cols + 16].reshape(KC, P, 16).transpose(1, 0, 2),
        "lora": lora,
        "w_mod": a["w_mod_2"].reshape(KC // 4, 4, P, MOD_COLS // COLS, COLS).transpose(3, 0, 2, 1, 4)
                              .reshape(-1, P, 4 * COLS),
        "b_mod": np.stack([a["b_mod_2"], a["mod_layer_2"][0]]),
        "final_norm": np.broadcast_to(a["final_norm_w"], (P, D)),
        "gm_norm": np.broadcast_to(a["gm_norm_g_2"][0], (P, 512)),
        "gm_ws": a["gm_ws_2"][0].transpose(2, 0, 1),
        "w_route": w_route.reshape(KC, P, 36).transpose(1, 0, 2),
        "b_route": np.concatenate([a["b_group_2"][0], a["b_route_2"][0]])[None],
    }


def kernel(**inputs):
    import concourse.bacc as bacc
    from concourse.bass_utils import run_bass_kernel_spmd

    nc = bacc.Bacc("TRN2", target_bir_lowering=False, num_devices=1)
    arrays = lay_out({n: np.asarray(v) for n, v in inputs.items()})
    arrays = {n: np.ascontiguousarray(v) for n, v in arrays.items()}
    io = {n: nc.dram_tensor("in_" + n, v.shape, mybir.dt.from_np(v.dtype), kind="ExternalInput").ap()
                            for n, v in arrays.items()}
    io["out"] = nc.dram_tensor("out", (T, D), F32, kind="ExternalOutput").ap()
    program(nc, io)
    got = run_bass_kernel_spmd(nc, [{"in_" + n: v for n, v in arrays.items()}], core_ids=[0])
    return got.results[0]["out"].reshape(1, T, D)
```

```python
from contextlib import ExitStack

import numpy as np

import concourse.bass as bass
from concourse import mybir

F32 = mybir.dt.float32
F32R = mybir.dt.float32r
ALU = mybir.AluOpType
ACT = mybir.ActivationFunctionType
AX = mybir.AxisListType

P = 128
D = 2048
T = 256
TT = T // P
KC = D // P
UNIT_KC = 8
COLS = 512
UNIT = UNIT_KC * COLS
HALF = UNIT // 2
SLOTS = 4
EPS = 1e-6
HALF_E = float(np.exp(-0.5))

DN_HEADS, DN_DIM = 8, 128
DN_TILES = 24
RW_HEADS, RW_DIM = 16, 64
RW_TILES = 8
RW_GN_EPS = 64e-5
XA_HEADS = 4
FFN_BLOCKS = 16
SB_HEADS = 4
GMLP_GROUPS = 4
MIX_GROUPS = 8
GROUPS, PER_GROUP = 4, 8
EXPERTS = GROUPS * PER_GROUP
D_EXPERT = 256
MOD_COLS = 6 * D
MOD_SLOTS = 4

STREAM, _at = {}, 0
for _name, _units in (("dn", 16), ("rw", 12), ("lora", 1), ("w_out", 8), ("xk", 2), ("xv", 2), ("xq", 2),
                      ("xo", 2), ("w_in_2", 10), ("w_out_2", 4)):
    STREAM[_name] = (_at, _units)
    _at += _units
UNITS = _at

COL, _at = {}, 0
for _name, _n in (("mix_norm", 16), ("conv", 4 * DN_TILES), ("dn_norm", 1), ("mu", 26), ("a0", 8), ("k_k", 8),
                  ("k_a", 8), ("r_k", 8), ("ln_w", 8), ("ln_b", 8), ("xa_norm", 16), ("mem_norm", 16), ("ffn_norm", 16),
                  ("norm1", 16), ("norm2", 16), ("out_norm", 8), ("q_norm", 1), ("k_norm", 1), ("gm_bs", 4), ("c", 16),
                  ("dn_gate", 2 * DN_HEADS)):
    COL[_name] = (_at, _n)
    _at += _n
N_COLS = _at

CONST, _at = {}, 0
for _name, _n in (("ident", P), ("ones", P), ("tri_le", P), ("tri_gt", P), ("before", TT * T), ("index", PER_GROUP),
                  ("levels", 7 * P), ("strict_incl", 2 * P), ("head_ones", P), ("g_incl", P), ("g_excl", P),
                  ("g_pre", 1), ("g_post", 1)):
    CONST[_name] = (_at, _n)
    _at += _n
N_CONST = _at
N_KEPT = CONST["levels"][0]


class Kit:

    def __init__(self, stream):
        self.stream = stream
        self.norm_uses = self.inv_uses = self.turns = self.dve_at = 0
        self.tt = self.act_n = self.pe_n = self.pieces = 0
        self.ft = 4


class Steps:

    def __init__(self, eng, sem):
        self.eng, self.sem, self.n, self.turn, self.per = eng, sem, 0, None, 0

    def step(self, ins):
        ins.then_inc(self.sem, 1)
        self.n += 1

    def value(self):
        return self.n if self.turn is None else self.turn * self.per + self.n

    def settle(self):
        self.eng.wait_ge(self.sem, self.value())

    def loop(self, turn, per):
        self.turn, self.per, self.start = turn, per, self.n

    def end(self, trips):
        assert self.n - self.start == self.per
        self.n, self.turn = self.start + trips * self.per, None


def load_unit(k, sp, unit, slot):
    src = k.stream[unit] if isinstance(unit, int) else k.stream[bass.ds(unit, 1)].rearrange("a p n -> (a p) n")
    sp.dma_start(k.ring[:, slot].rearrange("p k n -> p (k n)"), src).then_inc(k.loaded[slot], 16)


def col(k, name, n=0):
    at, count = COL[name]
    assert n < count
    return k.cols[:, at + n:at + n + 1]


def cols_of(k, name):
    at, count = COL[name]
    return k.cols[:, at:at + count]


def const(k, name):
    at, n = CONST[name]
    return k.consts[:, at:at + n] if at < N_KEPT else k.mixer_consts[:, at - N_KEPT:at - N_KEPT + n]


def bank(k, b):
    return k.psum[:, b, :]


def features(a):
    return a[:].rearrange("p t n -> p (t n)").rearrange("p (c t) -> p c t", t=T)


def norm_turn(nc, k, src, dst, scale, bias=None, sync=None, await_src=None):
    u = k.norm_uses
    k.norm_uses += 1
    with nc.Block(no_gpsimd_drain=True) as block:
        if sync is not None:
            @block.sync
            def _(sp):
                sync(sp)

        @block.scalar
        def _(act):
            for t in range(TT):
                if await_src is not None:
                    act.wait_ge(await_src[t], 16)
                act.activation(dst[:, 8 * t:8 * t + 8, :].rearrange("p a b -> p (a b)"), src[:, t, :], ACT.Square,
                               accum_out=k.ssq[:, t:t + 1]).then_inc(k.norm_ssq, 1)
            act.wait_ge(k.norm_ssq, 2 * u + 2)
            if await_src is not None:
                act.wait_ge(k.consts_in, 48)
            act.activation(k.rms[:, 0:TT], k.ssq[:, 0:TT], ACT.Sqrt, bias=k.eps[:, 0:1], scale=1.0 / D)\
               .then_inc(k.norm_rms, 1)
            for b in range(0, 8, 2):
                act.wait_ge(k.norm_mm, 8 * u + b + 1)
                for c in (2 * b, 2 * b + 1):
                    act.activation(dst[:, c, :], bank(k, b)[:, (c % 2) * T:(c % 2) * T + T], ACT.Identity,
                                   scale=scale(c), bias=0.0 if bias is None else bias(c))

        @block.vector
        def _(dve):
            dve.wait_ge(k.norm_rms, u + 1)
            dve.reciprocal(k.rstd[:, 0:TT], k.rms[:, 0:TT]).then_inc(k.norm_diag, 1)
            dve.wait_ge(k.norm_diag, 3 * u + 1)
            for t in range(TT):
                dve.tensor_scalar(k.diag[:, t, :], const(k, "ident"), k.rstd[:, t:t + 1], None, ALU.mult)\
                   .then_inc(k.norm_diag, 1)
            for b in range(1, 8, 2):
                dve.wait_ge(k.norm_mm, 8 * u + b + 1)
                for c in (2 * b, 2 * b + 1):
                    ps = bank(k, b)[:, (c % 2) * T:(c % 2) * T + T]
                    if bias is None:
                        dve.tensor_scalar(dst[:, c, :], ps, scale(c), None, ALU.mult)
                    else:
                        dve.tensor_scalar(dst[:, c, :], ps, scale(c), bias(c), ALU.mult, ALU.add)

        @block.tensor
        def _(pe):
            pe.wait_ge(k.norm_diag, 3 * u + 3)
            for c in range(KC):
                for t in range(TT):
                    mm = pe.matmul(bank(k, c // 2)[:, (c % 2) * T + t * P:(c % 2) * T + (t + 1) * P],
                                   src[:, t, c * P:(c + 1) * P], k.diag[:, t, :], start=True, stop=True)
                if c % 2:
                    mm.then_inc(k.norm_mm, 1)


def feature_group(k, pe, unit, rhs, tile, tiles=4, width=COLS, turn=None, rounds=0, per_turn=0):
    def at(value):
        return value if turn is None else turn * per_turn + value
    for half in range(2):
        pe.wait_ge(k.loaded[(unit + half) % SLOTS], (16 * ((unit + half) // SLOTS + 1)) if turn is None
                   else turn * (16 * rounds) + 16 * ((unit + half) // SLOTS + 1))
    for m in range(tiles):
        pe.wait_ge(k.ft_free, at(tile + m + 1))
        for c in range(KC):
            w = k.ring[:, (unit + c // UNIT_KC) % SLOTS, c % UNIT_KC, m * P:(m + 1) * P]
            mm = pe.matmul(bank(k, m)[:, 0:T], w, rhs[:, c, :], start=(c == 0), stop=(c == KC - 1))
        mm.then_inc(k.ft_done, 1)


class SplitTiles:

    def __init__(self, k, first, sb, name):
        self.k, self.first, self.f0, self.p0 = k, first, k.ft, k.pieces
        self.u_hi, self.u_lo = (sb(f"{name}_u_{n}", [P, KC, T], dtype=F32R) for n in ("hi", "lo"))
        self.w_hi, self.w_lo = (sb(f"{name}_w_{n}", [P, 2, UNIT_KC, P], dtype=F32R) for n in ("hi", "lo"))

    @staticmethod
    def at(turn, per, value):
        return value if turn is None else turn * per + value

    def weights(self, x, half):
        unit = self.first + 2 * (x // 4) + half
        return self.k.ring[:, unit % SLOTS, :, x % 4 * P:(x % 4 + 1) * P]

    def split_input(self, nc, u):
        k = self.k
        with nc.Block(no_gpsimd_drain=True) as block:
            @block.scalar
            def _(act):
                for n in range(2):
                    act.activation(self.u_hi[:, 8 * n:8 * n + 8], u[:, 8 * n:8 * n + 8, :], ACT.Copy)\
                       .then_inc(k.act_sem, 1)

            @block.vector
            def _(dve):
                for n in range(2):
                    dve.wait_ge(k.act_sem, k.act_n + n + 1)
                    dve.tensor_tensor(self.u_lo[:, 8 * n:8 * n + 8], u[:, 8 * n:8 * n + 8, :],
                                      self.u_hi[:, 8 * n:8 * n + 8].bitcast(F32), ALU.subtract)
        k.act_n += 2

    def high(self, act, x, halves, turn=None):
        k, at = self.k, self.at
        for half in halves:
            unit = self.first + 2 * (x // 4) + half
            act.wait_ge(k.loaded[unit % SLOTS], at(turn, 16, 16 * (unit // SLOTS + 1)))
            if half:
                act.wait_ge(k.ft_done, at(turn, 8, self.f0 + x))
            else:
                act.wait_ge(k.piece_used, at(turn, 8, self.p0 + x + 1))
            act.activation(self.w_hi[:, half], self.weights(x, half), ACT.Copy).then_inc(k.piece_high, 1)

    def low(self, dve, x, halves, turn=None):
        k = self.k
        for half in halves:
            dve.wait_ge(k.piece_high, self.at(turn, 16, 2 * (self.p0 + x) + half + 1))
            dve.tensor_tensor(self.w_lo[:, half], self.weights(x, half), self.w_hi[:, half].bitcast(F32),
                              ALU.subtract).then_inc(k.piece_low, 1)

    def product(self, pe, x, turn=None):
        k, at = self.k, self.at
        pe.wait_ge(k.ft_free, at(turn, 8, self.f0 + x + 1))
        out = bank(k, x % 4)[:, 0:T]
        for half in range(2):
            pe.wait_ge(k.piece_low, at(turn, 16, 2 * (self.p0 + x) + half + 1))
            for c in range(UNIT_KC):
                hi, lo, chunk = self.w_hi[:, half, c, :], self.w_lo[:, half, c, :], UNIT_KC * half + c
                pe.matmul(out, hi, self.u_hi[:, chunk, :], start=chunk == 0, stop=False)
                pe.matmul(out, hi, self.u_lo[:, chunk, :], start=False, stop=False)
                mm = pe.matmul(out, lo, self.u_hi[:, chunk, :], start=False, stop=chunk == KC - 1)
            mm.then_inc(k.ft_done if half else k.piece_used, 1)


def token_group(k, pe, units, lhs, chunks, tile, where=0, turn=None, rounds=0, per_turn=0, wait=True):
    def at(value):
        return value if turn is None else turn * per_turn + value
    if wait:
        for u in sorted({u for u, _, _ in units}):
            pe.wait_ge(k.loaded[u % SLOTS], (16 * (u // SLOTS + 1)) if turn is None
                       else turn * (16 * rounds) + 16 * (u // SLOTS + 1))
    for t in range(TT):
        pe.wait_ge(k.tt_free, at(tile + t + 1))
    for n, (u, row, at_col) in enumerate(units):
        flat = k.ring[:, u % SLOTS].rearrange("p k n -> p (k n)")
        w = flat[:, row * COLS + at_col:row * COLS + at_col + COLS]
        for t in range(TT):
            mm = pe.matmul(bank(k, 4 + (tile + t) % 4), lhs[:, chunks[n], t * P:(t + 1) * P], w,
                           start=(n == 0), stop=(n == len(units) - 1))
            if n == len(units) - 1:
                mm.then_inc(k.tt_done, 1)


def load_next(k, sp, unit, sem, value):
    if unit + SLOTS < k.stream_end:
        sp.wait_ge(sem, value)
        load_unit(k, sp, unit + SLOTS, unit % SLOTS)


def invert(nc, k, X):
    u = k.inv_uses
    k.inv_uses += 1
    LEVELS = 7
    per = 2 * (LEVELS - 1)
    levels = const(k, "levels").rearrange("p (l n) -> p l n", l=LEVELS)
    ident = const(k, "ident")
    U, W, M, PR = k.inv_u, k.inv_w, k.inv_m, k.inv_p

    def mats(b):
        return bank(k, b).rearrange("p (h n) -> p h n", h=4)

    def four(g):
        return slice(4 * g, 4 * g + 4)

    def rep(a):
        return a.unsqueeze(1).broadcast_to([P, 4, P])

    def columns(a, level, odd):
        dims = "p h (q b s) -> p h q b s" if len(a.shape) == 3 else "p (q b s) -> p q b s"
        a = a.rearrange(dims, b=2, s=1 << level)
        return a[:, :, :, odd, :] if len(a.shape) == 5 else a[:, :, odd, :]

    def packed(a, level):
        return a[:, :, 0:P // 2].rearrange("p h (q s) -> p h q s", s=1 << level)

    with nc.Block(no_gpsimd_drain=True) as block:
        @block.vector
        def _(dve):
            s = k.dve_steps
            s.eng = dve
            for g in range(2):
                s.step(dve.tensor_tensor(W[:, four(g), :], X[:, four(g), 0, :], rep(levels[:, 0, :]), ALU.mult))
                s.settle()
                s.step(dve.tensor_tensor(U[:, four(g), :], rep(ident), W[:, four(g), :], ALU.subtract))
                s.settle()
                dve.tensor_tensor(M[:, four(g), :], X[:, four(g), 0, :], rep(levels[:, 1, :]), ALU.mult)\
                   .then_inc(k.inv_masked, 1)
            for level in range(1, LEVELS):
                for g in range(2):
                    n = 2 * (level - 1) + g
                    dve.wait_ge(k.inv_second, u * per + n + 1)
                    if level < LEVELS - 1:
                        w = columns(W[:, four(g), :], level, 0)
                        s.step(dve.tensor_tensor(w, w, packed(mats(4 + g), level), ALU.subtract))
                        s.step(dve.tensor_tensor(M[:, four(g), :], X[:, four(g), 0, :], rep(levels[:, level + 1, :]),
                                                 ALU.mult))
                    s.settle()
                    w = columns(U[:, four(g), :], level, 1)
                    dve.tensor_tensor(w, w, packed(mats(6 + g), level), ALU.subtract).then_inc(k.inv_masked, 1)
            s.settle()

        @block.tensor
        def _(pe):
            for g in range(2):
                pe.wait_ge(k.inv_masked, u * (per + 2) + g + 1)
                for h in range(4):
                    mm = pe.transpose(mats(g)[:, h, :], U[:, 4 * g + h, :], ident)
                mm.then_inc(k.inv_first, 1)
            for level in range(1, LEVELS):
                for g in range(2):
                    n = 2 * (level - 1) + g
                    pe.wait_ge(k.inv_masked, u * (per + 2) + n + 1)
                    pe.wait_ge(k.inv_taken, u * (per + 2) + n + 1)
                    for h in range(4):
                        mm = pe.matmul(mats(g)[:, h, :], M[:, 4 * g + h, :], W[:, 4 * g + h, :], start=True, stop=True)
                    mm.then_inc(k.inv_first, 1)
                for g in range(2):
                    n = 2 * (level - 1) + g
                    pe.wait_ge(k.inv_taken, u * (per + 2) + n + 3)
                    for h in range(4):
                        if level < LEVELS - 1:
                            pe.matmul(mats(4 + g)[:, h, 0:P // 2], U[:, 4 * g + h, :],
                                      columns(PR[:, 4 * g + h, :], level, 0), start=True, stop=True)
                    for h in range(4):
                        mm = pe.matmul(mats(6 + g)[:, h, 0:P // 2], PR[:, 4 * g + h, :],
                                       columns(U[:, 4 * g + h, :], level, 1), start=True, stop=True)
                    mm.then_inc(k.inv_second, 1)

        @block.scalar
        def _(act):
            for n in range(per + 2):
                g = n % 2
                act.wait_ge(k.inv_first, u * (per + 2) + n + 1)
                act.activation((W if n < 2 else PR)[:, four(g), :], mats(g), ACT.Copy).then_inc(k.inv_taken, 1)


def deltanet_project(nc, k, tiles, qkvz):
    first, _ = STREAM["dn"]
    f0 = k.ft
    with nc.Block(no_gpsimd_drain=True) as block:
        @block.sync
        def _(sp):
            with sp.Fori(0, 3) as i:
                for j in range(4):
                    sp.wait_ge(k.ft_done, i * 8 + f0 + 4 * (j // 2 + 1))
                    load_unit(k, sp, i * 4 + first + SLOTS + j, (first + j) % SLOTS)
            for j in range(12, 16):
                load_next(k, sp, first + j, k.ft_done, f0 + 4 * (j // 2 + 1))

        @block.tensor
        def _(pe):
            with pe.Fori(0, 3) as i:
                for m in range(8):
                    tiles.product(pe, m, turn=i)
            for m in range(24, 32):
                tiles.product(pe, m)

        @block.vector
        def _(dve):
            s = k.dve_steps
            s.eng = dve
            tiles.low(dve, 0, (0, 1))
            with dve.Fori(0, 3) as i:
                s.loop(i, 8 * 4)
                for m in range(8):
                    tiles.low(dve, m + 1, (0,), turn=i)
                    dve.wait_ge(k.ft_done, i * 8 + f0 + m + 1)
                    ps = bank(k, m % 4)
                    at = COL["conv"][0] + 4 * m

                    def tap(n):
                        return k.cols[:, bass.ds(i * 32 + at + n, 1)]

                    def out(lag):
                        return qkvz[:, bass.ds(i * 8 + m, 1), lag:T].rearrange("p a t -> p (a t)")
                    s.step(dve.tensor_scalar(out(0), ps[:, 0:T], tap(3), None, ALU.mult))
                    for lag in (1, 2, 3):
                        if lag == 2:
                            tiles.low(dve, m + 1, (1,), turn=i)
                        s.settle()
                        s.step(dve.scalar_tensor_tensor(out(lag), ps[:, 0:T - lag], tap(3 - lag), out(lag),
                                                        ALU.mult, ALU.add))
            s.end(3)
            for m in range(25, 32):
                tiles.low(dve, m, (0, 1))

        @block.scalar
        def _(act):
            d0 = k.dve_at
            tiles.high(act, 0, (0, 1))
            tiles.high(act, 1, (0,))
            with act.Fori(0, 3) as i:
                for m in range(8):
                    tiles.high(act, m + 1, (1,), turn=i)
                    tiles.high(act, m + 2, (0,), turn=i)
                    act.wait_ge(k.dve_sem, i * 32 + d0 + 4 * (m + 1))
                    y = qkvz[:, bass.ds(i * 8 + m, 1), :].rearrange("p a t -> p (a t)")
                    act.activation(y, y, ACT.Silu).then_inc(k.ft_free, 1)
            for m in range(24, 32):
                if m < 31:
                    tiles.high(act, m + 1, (1,))
                if m < 30:
                    tiles.high(act, m + 2, (0,))
                act.wait_ge(k.ft_done, f0 + m + 1)
                act.activation(qkvz[:, m, :], bank(k, m % 4)[:, 0:T], ACT.Silu).then_inc(k.ft_free, 1)
    k.dve_at = k.dve_steps.n
    k.ft += 32
    k.pieces += 32


def deltanet_prepare(nc, k, u, qkvz, w_gate, q_tm, k_tm, v_tm, kb_tm, KQ, kT):
    s = k.dve_steps
    grids = [(q_tm, 0), (k_tm, 8), (v_tm, 16)]
    with nc.Block(no_gpsimd_drain=True) as block:
        @block.tensor
        def _(pe):
            n = 0
            for t in range(TT):
                for _, at in grids:
                    for g in range(2):
                        if n >= 6:
                            pe.wait_ge(k.turn_taken, k.turns + n - 5)
                        for h in range(4):
                            mm = pe.transpose(bank(k, n % 6)[:, h * P:(h + 1) * P],
                                              qkvz[:, at + 4 * g + h, t * P:(t + 1) * P], const(k, "ident"))
                        mm.then_inc(k.turned, 1)
                        n += 1
            for t in range(TT):
                for c in range(KC):
                    mm = pe.matmul(bank(k, 6 + t)[:, 0:16], u[:, c, t * P:(t + 1) * P], w_gate[:, c, :],
                                   start=(c == 0), stop=(c == KC - 1))
                mm.then_inc(k.gates_ready, 1)

        @block.scalar
        def _(act):
            n = 0
            for t in range(TT):
                for dst, _ in grids:
                    for g in range(2):
                        act.wait_ge(k.turned, k.turns + n + 1)
                        act.activation(dst[:, t, 4 * g:4 * g + 4, :], bank(k, n % 6).rearrange("p (h n) -> p h n", h=4),
                                       ACT.Copy).then_inc(k.turn_taken, 1)
                        n += 1

        @block.vector
        def _(dve):
            s.eng = dve
            dve.wait_ge(k.gates_ready, 2)
            for t in range(TT):
                s.step(dve.tensor_copy(k.beta[:, t, :], bank(k, 6 + t)[:, 8:16]))
                s.step(dve.tensor_tensor(k.g[:, t, :], bank(k, 6 + t)[:, 0:8],
                                         k.cols[:, COL["dn_gate"][0] + 8:COL["dn_gate"][0] + 16], ALU.add))
            s.settle()
            s.step(dve.tensor_scalar(k.sp_pos[:], k.g[:], 0.0, None, ALU.max))
            s.settle()
            s.step(dve.scalar_tensor_tensor(k.g[:], k.sp_pos[:], -2.0, k.g[:], ALU.mult, ALU.add))
            s.settle()
    k.turns += 12
    with nc.Block(no_gpsimd_drain=True) as block:
        @block.scalar
        def _(act):
            act.activation(k.beta[:], k.beta[:], ACT.Sigmoid).then_inc(k.act_sem, 1)
            act.activation(k.g[:], k.g[:], ACT.Exp).then_inc(k.act_sem, 1)
            act.activation(k.a_exp[:], k.cols[:, COL["dn_gate"][0]:COL["dn_gate"][0] + 8], ACT.Exp).then_inc(k.act_sem, 1)
            act.wait_ge(k.act_sem, k.act_n + 3)
            act.activation(k.g[:], k.g[:], ACT.Ln, bias=k.one[:, 0:1])

        @block.vector
        def _(dve):
            s.eng = dve
            for n, src in enumerate((q_tm, k_tm)):
                s.step(dve.tensor_tensor(k.scratch8[:], src[:].rearrange("p t h d -> p (t h d)"),
                                         src[:].rearrange("p t h d -> p (t h d)"), ALU.mult))
                s.settle()
                s.step(dve.tensor_reduce(k.qk_ssq[:, n], k.scratch8[:].rearrange("p (t h d) -> p t h d", t=2, h=8),
                                         AX.X, ALU.add))
                s.settle()
    k.act_n += 3
    with nc.Block(no_gpsimd_drain=True) as block:
        @block.scalar
        def _(act):
            act.activation(k.qk_ssq[:], k.qk_ssq[:], ACT.Sqrt, bias=k.eps[:, 0:1])

        @block.vector
        def _(dve):
            s.eng = dve
            s.step(dve.tensor_tensor(k.g[:], k.g[:], k.sp_pos[:], ALU.add))
            s.settle()
            s.step(dve.scalar_tensor_tensor(k.g[:], k.g[:], -1.0, k.a_exp[:].unsqueeze(1).broadcast_to([P, TT, 8]),
                                            ALU.mult, ALU.mult))
            s.settle()
    with nc.Block(no_gpsimd_drain=True) as block:
        @block.vector
        def _(dve):
            s.eng = dve
            s.step(dve.reciprocal(k.qk_ssq[:], k.qk_ssq[:]))
            s.settle()
            s.step(dve.tensor_scalar(k.qk_ssq[:, 0], k.qk_ssq[:, 0], DN_DIM ** -0.5, None, ALU.mult))
            s.settle()

            def over(a):
                return a.unsqueeze(3).broadcast_to([P, TT, 8, P])
            s.step(dve.tensor_tensor(q_tm[:], q_tm[:], over(k.qk_ssq[:, 0]), ALU.mult))
            s.step(dve.tensor_tensor(k_tm[:], k_tm[:], over(k.qk_ssq[:, 1]), ALU.mult))
            s.settle()
            s.step(dve.tensor_tensor(kb_tm[:], k_tm[:], over(k.beta[:]), ALU.mult))
            s.step(dve.tensor_scalar(qkvz[:, 24:32, :], qkvz[:, 24:32, :], col(k, "dn_norm"), None, ALU.mult))
            s.settle()
    jobs = [(k_tm, t, g, kT[:, 4 * g:4 * g + 4, t, :]) for t in range(TT) for g in range(2)]
    jobs += [(kb_tm, t, g, KQ[:, 4 * g:4 * g + 4, t, 0, :]) for t in range(TT) for g in range(2)]
    jobs += [(q_tm, t, g, KQ[:, 4 * g:4 * g + 4, t, 1, :]) for t in range(TT) for g in range(2)]
    turn_blocks(nc, k, [([src[:, t, 4 * g + h, :] for h in range(4)], dst) for src, t, g, dst in jobs])


def turn_blocks(nc, k, jobs):
    n0 = k.turns
    with nc.Block(no_gpsimd_drain=True) as block:
        @block.tensor
        def _(pe):
            for n, (pieces, _) in enumerate(jobs):
                if n >= 8:
                    pe.wait_ge(k.turn_taken, n0 + n - 7)
                for h, piece in enumerate(pieces):
                    mm = pe.transpose(bank(k, n % 8)[:, h * P:(h + 1) * P], piece, const(k, "ident"))
                mm.then_inc(k.turned, 1)

        @block.scalar
        def _(act):
            for n, (pieces, dst) in enumerate(jobs):
                if n % 2 == 0 or n >= 0:
                    act.wait_ge(k.turned, n0 + n + 1)
                    act.activation(dst, bank(k, n % 8)[:, 0:len(pieces) * P].rearrange("p (h n) -> p h n", n=P),
                                   ACT.Copy).then_inc(k.turn_taken, 1)
    k.turns += len(jobs)


def deltanet_tile(nc, k, t, v_tm, k_tm, KQ, kT, X, dec, dec_rhs, state, zs, out):
    s = k.dve_steps
    le, gt = const(k, "tri_le"), const(k, "tri_gt")
    with nc.Block(no_gpsimd_drain=True) as block:
        @block.vector
        def _(dve):
            s.eng = dve
            s.step(dve.tensor_tensor(dec_rhs[:], le.unsqueeze(1).broadcast_to([P, 8, P]),
                                     k.g[:, t, :].unsqueeze(2).broadcast_to([P, 8, P]), ALU.mult))
            s.settle()

        @block.tensor
        def _(pe):
            pe.matmul(bank(k, 7)[:, 0:8], le, k.g[:, t, :], start=True, stop=True)
            pe.matmul(bank(k, 7)[:, 8:16], gt, k.g[:, t, :], start=True, stop=True)
            for h in range(6):
                pe.matmul(bank(k, h // 2)[:, (h % 2) * T:(h % 2) * T + T], kT[:, h, t, :],
                          KQ[:, h, t].rearrange("p a n -> p (a n)"), start=True, stop=True)
            for h in range(6, 8):
                pe.matmul(bank(k, h // 2)[:, (h % 2) * T:(h % 2) * T + T], kT[:, h, t, :],
                          KQ[:, h, t].rearrange("p a n -> p (a n)"), start=True, stop=True)
    with nc.Block(no_gpsimd_drain=True) as block:
        @block.tensor
        def _(pe):
            for b in range(2):
                pe.matmul(bank(k, 4 + b), gt, dec_rhs[:, 4 * b:4 * b + 4, :].rearrange("p h n -> p (h n)"),
                          start=True, stop=True).then_inc(k.pe_sem, 1)

        @block.scalar
        def _(act):
            act.activation(k.egc[:], bank(k, 7)[:, 0:16], ACT.Exp)
            for b in range(2):
                act.wait_ge(k.pe_sem, k.pe_n + b + 1)
                act.activation(dec[:, 4 * b:4 * b + 4, :].rearrange("p h n -> p (h n)"), bank(k, 4 + b), ACT.Exp)

        @block.vector
        def _(dve):
            s.eng = dve
            mask = const(k, "strict_incl")
            for b in range(4):
                s.step(dve.tensor_tensor(X[:, 2 * b:2 * b + 2].rearrange("p h a n -> p h (a n)"),
                                         bank(k, b).rearrange("p (h n) -> p h n", h=2),
                                         mask.unsqueeze(1).broadcast_to([P, 2, 2 * P]), ALU.mult))
            s.settle()
    k.pe_n += 2
    with nc.Block(no_gpsimd_drain=True) as block:
        @block.vector
        def _(dve):
            s.eng = dve
            for a in range(2):
                s.step(dve.tensor_tensor(X[:, :, a, :], X[:, :, a, :], dec[:], ALU.mult))
            s.settle()
    invert(nc, k, X)
    R, V, O = k.inv_w, k.inv_m, k.inv_p

    def over(a):
        return a.unsqueeze(2).broadcast_to([P, 8, P])

    def product(lhs, rhs, b0):
        def _(pe):
            for h in range(8):
                pe.matmul(bank(k, b0 + h // 4)[:, (h % 4) * P:(h % 4 + 1) * P], lhs(h), rhs[:, h, :],
                          start=True, stop=True)
        return _
    two = [k.psum[:, b:b + 2, :].rearrange("p b (h n) -> p (b h) n", n=P) for b in (0, 2, 4, 6)]
    if t:
        with nc.Block(no_gpsimd_drain=True) as block:
            block.tensor(product(lambda h: kT[:, h, t, :], state, 0))
    with nc.Block(no_gpsimd_drain=True) as block:
        @block.vector
        def _(dve):
            s.eng = dve
            if t:
                s.step(dve.tensor_tensor(R[:], two[0], over(k.egc[:, 0:8]), ALU.mult))
                s.settle()
                s.step(dve.tensor_tensor(R[:], v_tm[:, t], R[:], ALU.subtract))
                s.settle()
            s.step(dve.tensor_tensor(R[:], R[:] if t else v_tm[:, t], over(k.beta[:, t, :]), ALU.mult))
            if not t:
                s.step(dve.tensor_tensor(k_tm[:, 0], k_tm[:, 0], over(k.egc[:, 8:16]), ALU.mult))
            s.settle()
    with nc.Block(no_gpsimd_drain=True) as block:
        block.tensor(product(lambda h: k.inv_u[:, h, :], R, 2))
    with nc.Block(no_gpsimd_drain=True) as block:
        @block.scalar
        def _(act):
            act.activation(V[:], two[1], ACT.Copy)
    with nc.Block(no_gpsimd_drain=True) as block:
        @block.tensor
        def _(pe):
            product(lambda h: X[:, h, 1, :], V, 4)(pe)
            if t:
                product(lambda h: KQ[:, h, t, 1, :], state, 6)(pe)
            else:
                product(lambda h: k_tm[:, 0, h, :], V, 6)(pe)
    with nc.Block(no_gpsimd_drain=True) as block:
        if not t:
            @block.scalar
            def _(act):
                act.activation(state[:], two[3], ACT.Copy)

        @block.vector
        def _(dve):
            s.eng = dve
            if t:
                s.step(dve.tensor_tensor(O[:], two[3], over(k.egc[:, 0:8]), ALU.mult))
                s.settle()
                s.step(dve.tensor_tensor(O[:], O[:], two[2], ALU.add))
            else:
                s.step(dve.tensor_copy(O[:], two[2]))
            s.settle()
            s.step(dve.tensor_tensor(R[:], O[:], O[:], ALU.mult))
            s.settle()
            s.step(dve.tensor_reduce(k.o_ssq[:], R[:], AX.X, ALU.add))
            s.settle()
    with nc.Block(no_gpsimd_drain=True) as block:
        @block.scalar
        def _(act):
            act.activation(k.o_ssq[:], k.o_ssq[:], ACT.Sqrt, bias=k.eps[:, 0:1], scale=1.0 / DN_DIM)
    with nc.Block(no_gpsimd_drain=True) as block:
        @block.vector
        def _(dve):
            s.eng = dve
            s.step(dve.reciprocal(k.o_ssq[:], k.o_ssq[:]))
            s.settle()
            s.step(dve.tensor_tensor(O[:], O[:], over(k.o_ssq[:]), ALU.mult))
            s.settle()
    with nc.Block(no_gpsimd_drain=True) as block:
        @block.tensor
        def _(pe):
            for h in range(8):
                pe.transpose(bank(k, h // 4)[:, (h % 4) * P:(h % 4 + 1) * P], O[:, h, :], const(k, "ident"))
    with nc.Block(no_gpsimd_drain=True) as block:
        @block.vector
        def _(dve):
            s.eng = dve
            s.step(dve.tensor_tensor(out[:, 0:8, t * P:(t + 1) * P], two[0], zs[:, :, t * P:(t + 1) * P], ALU.mult))
            s.settle()


def rwkv_project(nc, k, tiles, u, mix):
    first, _ = STREAM["rw"]
    lora, _ = STREAM["lora"]
    f0 = k.ft
    s = k.dve_steps
    with nc.Block(no_gpsimd_drain=True) as block:
        @block.sync
        def _(sp):
            with sp.Fori(0, 3) as i:
                for j in range(4):
                    sp.wait_ge(k.ft_done, i * 8 + f0 + 4 * (j // 2 + 1))
                    load_unit(k, sp, i * 4 + first + SLOTS + j, (first + j) % SLOTS)
            load_next(k, sp, lora, k.ft_done, f0 + 26)

        @block.tensor
        def _(pe):
            with pe.Fori(0, 3) as i:
                for m in range(8):
                    tiles.product(pe, m, turn=i)
            pe.wait_ge(k.loaded[lora % SLOTS], 16 * (lora // SLOTS + 1))
            w = k.ring[:, lora % SLOTS].rearrange("p k n -> p (k n)").rearrange("p (k n) -> p k n", n=2 * P)
            for m in range(2):
                pe.wait_ge(k.ft_free, f0 + 24 + m + 1)
                for c in range(KC):
                    mm = pe.matmul(bank(k, m)[:, 0:T], w[:, c, m * P:(m + 1) * P], u[:, c, :],
                                   start=(c == 0), stop=(c == KC - 1))
                mm.then_inc(k.ft_done, 1)

        @block.scalar
        def _(act):
            with act.Fori(0, 3) as i:
                for m in range(8):
                    tiles.high(act, m, (0, 1), turn=i)

        @block.vector
        def _(dve):
            s.eng = dve
            s.step(dve.tensor_scalar(k.one_less_mu[:], cols_of(k, "mu"), -1.0, 1.0, ALU.mult, ALU.add))
            s.step(dve.tensor_scalar(k.one_less_ka[:], cols_of(k, "k_a"), -1.0, 1.0, ALU.mult, ALU.add))
            s.settle()

            def shift(ps, less, mu, now, later):
                s.step(dve.tensor_scalar(now, ps[:, 0:T], less, None, ALU.mult))
                s.settle()
                dve.scalar_tensor_tensor(later, ps[:, 0:T - 1], mu, later, ALU.mult, ALU.add).then_inc(k.ft_free, 1)
            tiles.low(dve, 0, (0, 1))
            with dve.Fori(0, 2) as i:
                s.loop(i, 8)
                for m in range(8):
                    tiles.low(dve, m + 1, (0,), turn=i)
                    dve.wait_ge(k.ft_done, i * 8 + f0 + m + 1)
                    shift(bank(k, m % 4), k.one_less_mu[:, bass.ds(i * 8 + m, 1)],
                          k.cols[:, bass.ds(i * 8 + (COL["mu"][0] + m), 1)],
                          mix[:, bass.ds(i * 8 + m, 1), :].rearrange("p a t -> p (a t)"),
                          mix[:, bass.ds(i * 8 + m, 1), 1:T].rearrange("p a t -> p (a t)"))
                    tiles.low(dve, m + 1, (1,), turn=i)
            s.end(2)
            for m in range(16, 24):
                if m < 23:
                    tiles.low(dve, m + 1, (0,))
                dve.wait_ge(k.ft_done, f0 + m + 1)
                shift(bank(k, m % 4), k.one_less_mu[:, m:m + 1], col(k, "mu", m), mix[:, m, :], mix[:, m, 1:T])
                if m < 23:
                    tiles.low(dve, m + 1, (1,))
            for m in range(2):
                dve.wait_ge(k.ft_done, f0 + 24 + m + 1)
                shift(bank(k, m), k.one_less_mu[:, 24 + m:25 + m], col(k, "mu", 24 + m), mix[:, 24 + m, :],
                      mix[:, 24 + m, 1:T])
    k.ft += 26
    k.pieces += 24


def rwkv_prepare(nc, k, mix, lora, AR, sig, neg, a, gate, kk, scratch, out):
    s = k.dve_steps
    r, kv, v = mix[:, 0:8, :], mix[:, 8:16, :], mix[:, 16:24, :]
    th = k.tanh
    with nc.Block(no_gpsimd_drain=True) as block:
        @block.sync
        def _(sp):
            sp.wait_ge(k.small_in, 32)

        @block.scalar
        def _(act):
            act.activation(th[0:64, :], mix[0:64, 24, :], ACT.Tanh)
            act.activation(mix[:, 25, :], mix[:, 25, :], ACT.Sigmoid)

        @block.vector
        def _(dve):
            s.eng = dve
            s.step(dve.memset(th[64:65, :], 1.0))
            for c in range(8):
                s.step(dve.tensor_scalar(kk[:, c, :], kv[:, c, :], col(k, "k_k", c), None, ALU.mult))
            s.settle()
            s.step(dve.tensor_tensor(scratch[:], kk[:], kk[:], ALU.mult))
            s.settle()
    with nc.Block(no_gpsimd_drain=True) as block:
        @block.tensor
        def _(pe):
            for t in range(TT):
                for n in range(2):
                    pe.matmul(bank(k, 2 * t + n), th[0:65, t * P:(t + 1) * P], lora[0:65, 0, n * 512:(n + 1) * 512],
                              start=True, stop=True)
            for c in range(8):
                pe.matmul(bank(k, 4 + c // 2)[:, (c % 2) * T:(c % 2) * T + T], lora[64:128, 1, c * P:(c + 1) * P],
                          mix[64:128, 24, :], start=True, stop=True)
    with nc.Block(no_gpsimd_drain=True) as block:
        @block.scalar
        def _(act):
            act.activation(sig[:].rearrange("p t n -> p (t n)"),
                           k.psum[:, 0:4, :].rearrange("p b n -> p (b n)"), ACT.Sigmoid).then_inc(k.act_sem, 1)
            for c in range(8):
                act.activation(a[:, c, :], bank(k, 4 + c // 2)[:, (c % 2) * T:(c % 2) * T + T], ACT.Sigmoid,
                               bias=col(k, "a0", c))

        @block.tensor
        def _(pe):
            pe.wait_ge(k.act_sem, k.act_n + 1)
            for c in range(8):
                pe.matmul(bank(k, c // 2)[:, (c % 2) * T:(c % 2) * T + T], lora[:, 2, c * P:(c + 1) * P], mix[:, 25, :],
                          start=True, stop=True)
    k.act_n += 1
    with nc.Block(no_gpsimd_drain=True) as block:
        @block.tensor
        def _(pe):
            for b in range(4):
                pe.matmul(bank(k, 4 + b), const(k, "head_ones"),
                          scratch[:, 2 * b:2 * b + 2, :].rearrange("p c t -> p (c t)"), start=True, stop=True)

        @block.vector
        def _(dve):
            s.eng = dve
            s.step(dve.tensor_copy(gate[:].rearrange("p c t -> p (c t)"),
                                   k.psum[:, 0:4, :].rearrange("p b n -> p (b n)")))
            for c in range(8):
                s.step(dve.tensor_scalar(out[:, c, :], a[:, c, :], col(k, "k_a", c), k.one_less_ka[:, c:c + 1],
                                         ALU.mult, ALU.add))
            s.settle()
            s.step(dve.tensor_tensor(kv, kv, out, ALU.mult))
            s.settle()
    with nc.Block(no_gpsimd_drain=True) as block:
        @block.scalar
        def _(act):
            act.activation(scratch[:].rearrange("p c t -> p (c t)"), k.psum[:, 4:8, :].rearrange("p b n -> p (b n)"),
                           ACT.Sqrt)
    with nc.Block(no_gpsimd_drain=True) as block:
        @block.vector
        def _(dve):
            s.eng = dve
            s.step(dve.tensor_scalar(scratch[:], scratch[:], 1e-12, None, ALU.max))
            s.settle()
            s.step(dve.reciprocal(scratch[:], scratch[:]))
            s.settle()
            s.step(dve.tensor_tensor(kk[:], kk[:], scratch[:], ALU.mult))
            s.settle()
            s.step(dve.tensor_tensor(a[:], a[:], kk[:], ALU.mult))
            for c in range(8):
                s.step(dve.scalar_tensor_tensor(scratch[:, c, :], r[:, c, :], col(k, "r_k", c), kv[:, c, :],
                                                ALU.mult, ALU.mult))
            s.settle()

        @block.tensor
        def _(pe):
            for c in range(8):
                for t in range(TT):
                    pe.matmul(bank(k, c)[:, t * T:(t + 1) * T], sig[:, t, c * P:(c + 1) * P],
                              k.mixer_consts[:, CONST["g_incl"][0] - N_KEPT:CONST["g_incl"][0] - N_KEPT + T], start=True, stop=True)
    with nc.Block(no_gpsimd_drain=True) as block:
        @block.scalar
        def _(act):
            for c in range(8):
                ps = bank(k, c).rearrange("p (t a n) -> p t a n", t=TT, a=2)
                act.activation(AR[:, c, :, 0, :], ps[:, :, 1, :], ACT.Exp, scale=-HALF_E)
                act.activation(AR[:, c, :, 1, :], ps[:, :, 0, :], ACT.Exp, scale=-HALF_E)
                act.activation(neg[:, c, :].rearrange("p (t n) -> p t n", t=TT), ps[:, :, 0, :], ACT.Exp, scale=HALF_E)
    with nc.Block(no_gpsimd_drain=True) as block:
        @block.tensor
        def _(pe):
            for b in range(4):
                pe.matmul(bank(k, b), const(k, "head_ones"),
                          scratch[:, 2 * b:2 * b + 2, :].rearrange("p c t -> p (c t)"), start=True, stop=True)
            for c in range(8):
                pe.matmul(bank(k, 4)[:, c:c + 1], sig[:, 0, c * P:(c + 1) * P], const(k, "g_post"),
                          start=True, stop=False)
                pe.matmul(bank(k, 4)[:, c:c + 1], sig[:, 1, c * P:(c + 1) * P], const(k, "g_pre"),
                          start=False, stop=True)

        @block.vector
        def _(dve):
            s.eng = dve
            def cut(x):
                return x.rearrange("p c (t n) -> p c t n", t=TT)
            for t in range(TT):
                s.step(dve.tensor_tensor(AR[:, :, t, 0, :], AR[:, :, t, 0, :], cut(kk)[:, :, t, :], ALU.mult))
                s.step(dve.tensor_tensor(AR[:, :, t, 1, :], AR[:, :, t, 1, :], cut(r)[:, :, t, :], ALU.mult))
            s.step(dve.tensor_tensor(a[:], a[:], neg[:], ALU.mult))
            s.step(dve.tensor_tensor(kv, kv, neg[:], ALU.mult))
            s.settle()
    with nc.Block(no_gpsimd_drain=True) as block:
        @block.scalar
        def _(act):
            act.activation(k.carry[:], bank(k, 4)[:, 0:8], ACT.Exp, scale=-HALF_E)

        @block.vector
        def _(dve):
            s.eng = dve
            for b in range(4):
                s.step(dve.tensor_tensor(out[:, 2 * b:2 * b + 2, :].rearrange("p c t -> p (c t)"), bank(k, b),
                                         v[:, 2 * b:2 * b + 2, :].rearrange("p c t -> p (c t)"), ALU.mult))
            s.settle()
            for c in range(8):
                s.step(dve.scalar_tensor_tensor(out[:, c, :], out[:, c, :], col(k, "ln_b", c), gate[:, c, :],
                                                ALU.add, ALU.mult))
            s.settle()
            for c in range(8):
                s.step(dve.tensor_scalar(gate[:, c, :], gate[:, c, :], col(k, "ln_w", c), None, ALU.mult))
            s.settle()


def rwkv_batch(nc, k, t, half, X, Y, AR, B, K, v_tm, b_tm, k_tm, R, U, y, tmp, state, gate, out):
    s = k.dve_steps
    c0 = 4 * half

    def rows(h):
        return slice(RW_DIM * (h % 2), RW_DIM * (h % 2) + RW_DIM)
    ts = slice(t * P, (t + 1) * P)
    if not t:
        turn_blocks(nc, k, [([B[:, c0 + c, ts] for c in range(4)], b_tm.rearrange("p (h n) -> p h n", n=P)),
                            ([K[:, c0 + c, ts] for c in range(4)], k_tm.rearrange("p (h n) -> p h n", n=P))])
    with nc.Block(no_gpsimd_drain=True) as block:
        @block.tensor
        def _(pe):
            for n, src in enumerate((B, K)):
                for h in range(8):
                    pe.matmul(bank(k, 4 * n + 2 * (h // 4) + h % 2)[:, (h // 2 % 2) * T:(h // 2 % 2) * T + T],
                              src[rows(h), c0 + h // 2, ts],
                              AR[rows(h), c0 + h // 2, t].rearrange("p a n -> p (a n)"), start=True, stop=True)
    with nc.Block(no_gpsimd_drain=True) as block:
        @block.vector
        def _(dve):
            s.eng = dve
            mask = const(k, "strict_incl").unsqueeze(1).broadcast_to([P, 2, 2 * P])
            for n, dst in enumerate((X, Y)):
                for b in range(4):
                    h = 4 * (b // 2) + b % 2
                    s.step(dve.tensor_tensor(dst[:, h:h + 3:2].rearrange("p h a n -> p h (a n)"),
                                             bank(k, 4 * n + b).rearrange("p (h n) -> p h n", h=2), mask, ALU.mult))
            s.settle()
    invert(nc, k, X)
    with nc.Block(no_gpsimd_drain=True) as block:
        @block.tensor
        def _(pe):
            for h in range(8):
                ps = bank(k, 5 * (h % 2))[:, (h // 2) * RW_DIM:(h // 2 + 1) * RW_DIM]
                pe.matmul(ps, Y[:, h, 0, :], v_tm[:, t, (8 * half + h) * RW_DIM:(8 * half + h + 1) * RW_DIM],
                          start=True, stop=not t)
                if t:
                    pe.matmul(ps, AR[rows(h), c0 + h // 2, t, 0, :], state[rows(h), c0 + h // 2, :],
                              start=False, stop=True)
    with nc.Block(no_gpsimd_drain=True) as block:
        @block.scalar
        def _(act):
            for b in range(2):
                act.activation(R.rearrange("p (h b n) -> p h b n", b=2, n=RW_DIM)[:, :, b, :],
                               bank(k, 5 * b)[:, 0:4 * RW_DIM].rearrange("p (h n) -> p h n", n=RW_DIM),
                               ACT.Copy, scale=-1.0)
    with nc.Block(no_gpsimd_drain=True) as block:
        @block.tensor
        def _(pe):
            for h in range(8):
                pe.matmul(bank(k, 1)[:, h * RW_DIM:(h + 1) * RW_DIM], k.inv_u[:, h, :],
                          R[:, h * RW_DIM:(h + 1) * RW_DIM], start=True, stop=True)
    with nc.Block(no_gpsimd_drain=True) as block:
        @block.scalar
        def _(act):
            act.activation(U, bank(k, 1), ACT.Copy)
    with nc.Block(no_gpsimd_drain=True) as block:
        @block.tensor
        def _(pe):
            for h in range(8):
                ps = bank(k, 2 + 4 * (h % 2))[:, (h // 2) * RW_DIM:(h // 2 + 1) * RW_DIM]
                v = v_tm[:, t, (8 * half + h) * RW_DIM:(8 * half + h + 1) * RW_DIM]
                own = slice(h * RW_DIM, (h + 1) * RW_DIM)
                pe.matmul(ps, X[:, h, 1, :], U[:, own], start=True, stop=False)
                pe.matmul(ps, Y[:, h, 1, :], v, start=False, stop=not t)
                if t:
                    pe.matmul(ps, AR[rows(h), c0 + h // 2, t, 1, :], state[rows(h), c0 + h // 2, :],
                              start=False, stop=True)
            if not t:
                for h in range(8):
                    ps = bank(k, 3 + h % 2)[rows(h), (h // 2) * RW_DIM:(h // 2 + 1) * RW_DIM]
                    v = v_tm[:, t, (8 * half + h) * RW_DIM:(8 * half + h + 1) * RW_DIM]
                    own = slice(h * RW_DIM, (h + 1) * RW_DIM)
                    pe.matmul(ps, b_tm[:, own], U[:, own], start=True, stop=False)
                    pe.matmul(ps, k_tm[:, own], v, start=False, stop=True)
    y3 = y.rearrange("p (h n) -> p h n", n=RW_DIM)
    tmp3 = tmp.rearrange("p (h n) -> p h n", n=RW_DIM)

    def over(x):
        return x.unsqueeze(2).broadcast_to([P, 8, RW_DIM])
    with nc.Block(no_gpsimd_drain=True) as block:
        @block.vector
        def _(dve):
            s.eng = dve
            for b in range(2):
                s.step(dve.tensor_copy(y.rearrange("p (h b n) -> p h b n", b=2, n=RW_DIM)[:, :, b, :],
                                       bank(k, 2 + 4 * b)[:, 0:4 * RW_DIM].rearrange("p (h n) -> p h n", n=RW_DIM)))
            s.settle()
            s.step(dve.tensor_reduce(k.y_mean[:], y3, AX.X, ALU.add))
            s.settle()
            s.step(dve.tensor_scalar(k.y_mean[:], k.y_mean[:], 1.0 / RW_DIM, None, ALU.mult))
            s.settle()
            s.step(dve.tensor_tensor(y3, y3, over(k.y_mean[:]), ALU.subtract))
            s.settle()
            s.step(dve.tensor_tensor(tmp, y, y, ALU.mult))
            s.settle()
            s.step(dve.tensor_reduce(k.y_ssq[:], tmp3, AX.X, ALU.add))
            if not t:
                for c in range(4):
                    for b in range(2):
                        own = slice(RW_DIM * b, RW_DIM * (b + 1))
                        s.step(dve.tensor_scalar(state[own, c0 + c, :], bank(k, 3 + b)[own, c * RW_DIM:(c + 1) * RW_DIM],
                                                 k.carry[own, c0 + c:c0 + c + 1], None, ALU.mult))
            s.settle()
    with nc.Block(no_gpsimd_drain=True) as block:
        @block.scalar
        def _(act):
            act.activation(k.y_ssq[:], k.y_ssq[:], ACT.Sqrt, bias=k.gn_eps[:, 0:1], scale=1.0 / RW_DIM)
    with nc.Block(no_gpsimd_drain=True) as block:
        @block.vector
        def _(dve):
            s.eng = dve
            s.step(dve.reciprocal(k.y_ssq[:], k.y_ssq[:]))
            s.settle()
            s.step(dve.tensor_tensor(y3, y3, over(k.y_ssq[:]), ALU.mult))
            s.settle()
    with nc.Block(no_gpsimd_drain=True) as block:
        @block.tensor
        def _(pe):
            for c in range(4):
                pe.transpose(bank(k, 0)[:, c * P:(c + 1) * P], y[:, c * P:(c + 1) * P], const(k, "ident"))
    with nc.Block(no_gpsimd_drain=True) as block:
        @block.vector
        def _(dve):
            s.eng = dve
            at = out[:, c0:c0 + 4, ts]
            turned = tmp.rearrange("p (c n) -> p c n", n=P)
            s.step(dve.tensor_tensor(turned, bank(k, 0).rearrange("p (c n) -> p c n", n=P), gate[:, c0:c0 + 4, ts],
                                     ALU.mult))
            s.settle()
            s.step(dve.tensor_tensor(at, at, turned, ALU.add))
            s.settle()


def unit_rows(first, chunks, per_unit=UNIT_KC, rows_per_chunk=1, at_col=0):
    return [(first + c // per_unit, (c % per_unit) * rows_per_chunk, at_col) for c in range(chunks)]


def mixer_out(nc, k, mixed, x):
    first, _ = STREAM["w_out"]
    t0 = k.tt
    with nc.Block(no_gpsimd_drain=True) as block:
        @block.sync
        def _(sp):
            with sp.Fori(0, 2) as i:
                for j in range(4):
                    sp.wait_ge(k.tt_done, i * 4 + t0 + 2 * (j // 2 + 1))
                    load_unit(k, sp, i * 4 + first + SLOTS + j, (first + j) % SLOTS)

        @block.tensor
        def _(pe):
            with pe.Fori(0, 2) as i:
                for g in range(2):
                    token_group(k, pe, unit_rows(first + 2 * g, KC), mixed, range(KC), t0 + 2 * g,
                                turn=i, rounds=1, per_turn=4)

        @block.vector
        def _(dve):
            with dve.Fori(0, 2) as i:
                for n in range(4):
                    dve.wait_ge(k.tt_done, i * 4 + t0 + n + 1)
                    at = x[:, n % 2, bass.ds(i * 1024 + (n // 2) * COLS, COLS)]
                    dve.tensor_tensor(at, at, bank(k, 4 + (t0 + n) % 4), ALU.add).then_inc(k.tt_free, 1)
    k.tt += 8


def cross_attention(nc, k, x, scope_sb, mem, h_t, mem_t, mem_in):
    s = k.dve_steps
    k_t, q_t, v_m = scope_sb("xa_k", [P, 4, T]), scope_sb("xa_q", [P, 4, T]), scope_sb("xa_v", [P, TT, 512])
    probs, probs_t, o_t = (scope_sb("xa_probs", [P, XA_HEADS, TT, T]), scope_sb("xa_probs_t", [P, XA_HEADS, TT, T]),
                           scope_sb("xa_o", [P, XA_HEADS, T]))
    top, total = scope_sb("xa_top", [P, XA_HEADS, TT]), scope_sb("xa_total", [P, XA_HEADS, TT])
    norm_turn(nc, k, x, h_t, lambda c: col(k, "xa_norm", c))
    norm_turn(nc, k, mem, mem_t, lambda c: col(k, "mem_norm", c), await_src=mem_in)
    f0, t0 = k.ft, k.tt
    with nc.Block(no_gpsimd_drain=True) as block:
        @block.sync
        def _(sp):
            for part, sem, value in (("xk", k.ft_done, f0 + 4), ("xv", k.tt_done, t0 + 2), ("xq", k.ft_done, f0 + 8)):
                for j in range(2):
                    load_next(k, sp, STREAM[part][0] + j, sem, value)

        @block.tensor
        def _(pe):
            feature_group(k, pe, STREAM["xk"][0], mem_t, f0)
            token_group(k, pe, unit_rows(STREAM["xv"][0], KC), mem_t, range(KC), t0)
            feature_group(k, pe, STREAM["xq"][0], h_t, f0 + 4)

        @block.scalar
        def _(act):
            for n in range(8):
                act.wait_ge(k.ft_done, f0 + n + 1)
                act.activation((k_t, q_t)[n // 4][:, n % 4, :], bank(k, n % 4)[:, 0:T], ACT.Copy).then_inc(k.ft_free, 1)

        @block.vector
        def _(dve):
            for n in range(2):
                dve.wait_ge(k.tt_done, t0 + n + 1)
                dve.tensor_copy(v_m[:, n, :], bank(k, 4 + (t0 + n) % 4)).then_inc(k.tt_free, 1)
    k.ft += 8
    k.tt += 2
    scores = k.psum[:, 0:4, :].rearrange("p h (t m) -> p h t m", t=TT)
    with nc.Block(no_gpsimd_drain=True) as block:
        @block.tensor
        def _(pe):
            for h in range(XA_HEADS):
                for t in range(TT):
                    mm = pe.matmul(scores[:, h, t, :], q_t[:, h, t * P:(t + 1) * P], k_t[:, h, :], start=True, stop=True)
            mm.then_inc(k.pe_sem, 1)

        @block.vector
        def _(dve):
            s.eng = dve
            dve.wait_ge(k.pe_sem, k.pe_n + 1)
            s.step(dve.tensor_reduce(top[:], scores, AX.X, ALU.max))
            s.settle()
            s.step(dve.tensor_scalar(top[:], top[:], -P ** -0.5, None, ALU.mult))

        @block.scalar
        def _(act):
            act.wait_ge(k.dve_sem, k.dve_steps_before + 2)
            for h in range(XA_HEADS):
                for t in range(TT):
                    act.activation(probs[:, h, t, :], scores[:, h, t, :], ACT.Exp, scale=P ** -0.5,
                                   bias=top[:, h, t:t + 1], accum_out=total[:, h, t:t + 1])
    k.pe_n += 1
    with nc.Block(no_gpsimd_drain=True) as block:
        @block.vector
        def _(dve):
            s.eng = dve
            s.step(dve.reciprocal(total[:], total[:]))
            s.settle()
            s.step(dve.tensor_tensor(probs[:], probs[:], total[:].unsqueeze(3).broadcast_to([P, XA_HEADS, TT, T]),
                                     ALU.mult))
            s.settle()
    turn_blocks(nc, k, [([probs[:, h, t, m * P:(m + 1) * P] for m in range(2) for t in range(TT)],
                         probs_t[:, h].rearrange("p m (t n) -> p (m t) n", n=P)) for h in range(XA_HEADS)])
    with nc.Block(no_gpsimd_drain=True) as block:
        @block.tensor
        def _(pe):
            for h in range(XA_HEADS):
                for m in range(2):
                    pe.matmul(bank(k, h)[:, 0:T], v_m[:, m, h * P:(h + 1) * P], probs_t[:, h, m, :],
                              start=(m == 0), stop=(m == 1))
    with nc.Block(no_gpsimd_drain=True) as block:
        @block.scalar
        def _(act):
            act.activation(o_t[:], k.psum[:, 0:4, 0:T], ACT.Copy)
    first, t0 = STREAM["xo"][0], k.tt
    with nc.Block(no_gpsimd_drain=True) as block:
        @block.sync
        def _(sp):
            for j in range(2):
                load_next(k, sp, first + j, k.tt_done, t0 + 8)

        @block.tensor
        def _(pe):
            for n in range(4):
                token_group(k, pe, unit_rows(first, 4, per_unit=2, rows_per_chunk=4, at_col=n * COLS), o_t, range(4),
                            t0 + 2 * n)

        @block.vector
        def _(dve):
            for n in range(8):
                dve.wait_ge(k.tt_done, t0 + n + 1)
                at = x[:, n % 2, (n // 2) * COLS:(n // 2 + 1) * COLS]
                dve.tensor_tensor(at, at, bank(k, 4 + (t0 + n) % 4), ALU.add).then_inc(k.tt_free, 1)
    k.tt += 8


class TwoLayers:

    def __init__(self, weights, blocks, downs, raws, parts, sb, sem, name):
        self.weights, self.blocks, self.downs, self.raws, self.parts = weights, blocks, downs, raws, parts
        self.per = 4 + downs
        self.unroll = 2
        assert self.per % raws == 0 and self.per % parts == 0 and (blocks - 2) % self.unroll == 0
        self.chunks = downs
        self.trips = (blocks - 2) // self.unroll
        self.raw = sb(name + "_raw", [P, raws, HALF])
        self.raw_in = [sem(f"{name}_raw_in{n}") for n in range(raws)]
        self.hi_done, self.lo_done = sem(name + "_hi_done"), sem(name + "_lo_done")
        self.up_used = sem(name + "_up_used")
        self.hid_act, self.hid_high, self.hid_ready = (sem(f"{name}_{n}") for n in ("hid_act", "hid_high", "hid_ready"))

    def buffers(self, sb, name):
        self.w_hi, self.w_lo = (sb(f"{name}_w_{n}", [P, self.parts, HALF], dtype=F32R) for n in ("hi", "lo"))
        self.hid_hi, self.hid_lo = (sb(f"{name}_hid_{n}", [P, 2, self.chunks, T], dtype=F32R) for n in ("hi", "lo"))
        self.hid = sb(name + "_hid", [P, self.chunks, T])

    def at(self, e, per, c=0):
        i, n = e
        return n * per + c if i is None else i * (self.unroll * per) + (n * per + c)

    def number(self, e, j):
        return self.at(e, self.per, j - self.downs)

    def slots(self, j):
        return (j - self.downs) % self.raws, (j - self.downs) % self.parts

    def load(self, sp, e, j):
        number, slot = self.number(e, j), self.slots(j)[0]
        src = self.weights[number] if e[0] is None else \
            self.weights[bass.ds(number, 1)].rearrange("a p n -> (a p) n")
        sp.dma_start(self.raw[:, slot], src).then_inc(self.raw_in[slot], 16)

    def first_loads(self, sp):
        for q in range(self.raws):
            self.load(sp, (None, 0), self.downs + q)

    def is_first(self, e):
        return e[0] is None and e[1] == 0

    def is_last(self, e):
        return e[0] is None and e[1] == self.blocks


def run_steps(two, eng, first, step, last):
    first((None, 0))
    with eng.Fori(0, two.trips) as i:
        for r in range(two.unroll):
            step((i, 1 + r))
    step((None, two.blocks - 1))
    last((None, two.blocks))


def load_weights(two, sp, beside=None):
    def step(e, halves):
        for j in halves:
            sp.wait_ge(two.lo_done, two.at(e, two.per, j - two.downs - two.raws + 1))
            two.load(sp, e, j)
            if beside is not None:
                beside(e, j)
    per, downs = two.per, two.downs
    run_steps(two, sp, lambda e: step(e, range(downs + two.raws, per + 2)), lambda e: step(e, range(2, per + 2)),
              lambda e: step(e, range(2, downs)))


def high_part(two, k, act, t0, e, j):
    raw, part = two.slots(j)
    per, downs, before = two.per, two.downs, j - two.parts
    tiles = 8 // downs
    act.wait_ge(two.raw_in[raw], two.at(e, 16 * per // two.raws, 16 * ((j - downs) // two.raws + 1)))
    if two.is_first(e):
        if before >= downs:
            act.wait_ge(two.up_used, before - downs + 1)
    elif before < 0:
        act.wait_ge(two.up_used, two.at(e, 4))
        act.wait_ge(k.tt_done, two.at(e, 8, t0 - 16 + tiles * (per + before - 3)))
    elif two.is_last(e):
        act.wait_ge(k.tt_done, two.at(e, 8, t0 - 8 + tiles * (before + 1)))
    elif before < 4:
        act.wait_ge(two.up_used, two.at(e, 4, before + 1))
    else:
        act.wait_ge(k.tt_done, two.at(e, 8, t0 - 8 + tiles * (before - 3)))
    act.activation(two.w_hi[:, part], two.raw[:, raw], ACT.Copy).then_inc(two.hi_done, 1)


def low_part(two, dve, e, j):
    raw, part = two.slots(j)
    dve.wait_ge(two.hi_done, two.at(e, two.per, j - two.downs + 1))
    dve.tensor_tensor(two.w_lo[:, part], two.raw[:, raw], two.w_hi[:, part].bitcast(F32), ALU.subtract)\
       .then_inc(two.lo_done, 1)


def two_layer_products(two, k, pe, x_hi, x_lo):
    f0, t0, at = k.ft, k.tt, two.at

    def product(out, lhs, rhs, start, stop):
        pe.matmul(out, lhs[0], rhs[0], start=start, stop=False)
        pe.matmul(out, lhs[0], rhs[1], start=False, stop=False)
        return pe.matmul(out, lhs[1], rhs[0], start=False, stop=stop)

    def up(e):
        pe.wait_ge(k.ft_free, at(e, 4, f0 + 4))
        for half in range(4):
            j = half + two.downs if two.is_first(e) else half
            part = two.slots(j)[1]
            hi, lo = (w[:, part].rearrange("p (c n) -> p c n", c=4) for w in (two.w_hi, two.w_lo))
            pe.wait_ge(two.lo_done, at(e, two.per, j - two.downs + 1))
            for m in range(4):
                for c in range(4):
                    cols, chunk = slice(m * P, (m + 1) * P), 4 * half + c
                    mm = product(bank(k, m)[:, 0:T], (hi[:, c, cols], lo[:, c, cols]),
                                 (x_hi[:, chunk, :], x_lo[:, chunk, :]), chunk == 0, chunk == KC - 1)
            mm.then_inc(two.up_used, 1)

    def down(e):
        b, chunks = (e[1] - 1) % 2, two.chunks
        pe.wait_ge(two.hid_ready, at(e, 1))
        for half in range(two.downs):
            j = half if two.is_last(e) else 4 + half
            part = two.slots(j)[1]
            pe.wait_ge(two.lo_done, at(e, two.per, j - two.downs + 1))
            hi, lo = (w[:, part].rearrange("p (c n) -> p c n", c=chunks) for w in (two.w_hi, two.w_lo))
            for tile in range(8 // two.downs * half, 8 // two.downs * (half + 1)):
                n, t = tile // 2 % (4 // two.downs), tile % 2
                pe.wait_ge(k.tt_free, at(e, 8, t0 - 8 + tile + 1))
                for c in range(chunks):
                    rows, cols = slice(t * P, (t + 1) * P), slice(n * COLS, (n + 1) * COLS)
                    mm = product(bank(k, 4 + (t0 + tile) % 4), (two.hid_hi[:, b, c, rows], two.hid_lo[:, b, c, rows]),
                                 (hi[:, c, cols], lo[:, c, cols]), c == 0, c == chunks - 1)
                mm.then_inc(k.tt_done, 1)

    def both(e):
        up(e)
        down(e)
    run_steps(two, pe, up, both, down)


def hidden_low(two, dve, e):
    b = e[1] % 2
    dve.wait_ge(two.hid_high, two.at(e, 1, 1))
    dve.tensor_tensor(two.hid_lo[:, b], two.hid[:], two.hid_hi[:, b].bitcast(F32), ALU.subtract)\
       .then_inc(two.hid_ready, 1)


def mlp_and_modulation(nc, k, io, two, x, u, u_hi, u_lo, acc, w_mod, part, spare, c_silu, mod_scaled,
                       mod_summed):
    f0, t0, at = k.ft, k.tt, two.at
    MOD_GROUPS = MOD_COLS // COLS
    assert MOD_GROUPS * 8 == FFN_BLOCKS * 12
    with nc.Block(no_gpsimd_drain=True) as block:
        @block.sync
        def _(sp):
            sp.wait_ge(k.pool_sem, 1)
            sp.dma_start(acc[0:2].rearrange("p g n -> p (g n)"), io["b_mod"]).then_inc(k.small_in, 16)
            sp.wait_ge(k.small_in, 48)

        @block.gpsimd
        def _(pool):
            pool.memset(acc[:], 0.0).then_inc(k.pool_sem, 1)

        @block.scalar
        def _(act):
            act.activation(c_silu[:], cols_of(k, "c"), ACT.Silu)
            act.activation(u_hi[:], u[:], ACT.Copy).then_inc(k.act_sem, 1)

        @block.vector
        def _(dve):
            dve.wait_ge(k.act_sem, k.act_n + 1)
            dve.tensor_tensor(u_lo[:], u[:], u_hi[:].bitcast(F32), ALU.subtract)
    k.act_n += 1
    with nc.Block() as block:
        @block.sync
        def _(sp):
            def load_piece(e, n):
                unit, slot = at(e, 6, n // 2), n % MOD_SLOTS
                src = io["w_mod"][unit] if e[0] is None else \
                    io["w_mod"][bass.ds(unit, 1)].rearrange("a p n -> (a p) n")
                sp.dma_start(w_mod[:, slot].rearrange("p k n -> p (k n)"),
                             src[:, n % 2 * 2 * COLS:(n % 2 + 1) * 2 * COLS]).then_inc(k.mod_in[slot], 16)

            def pieces(e, j):
                if two.is_first(e):
                    loads = [(e, n) for n in ((4, 5) if j == 8 else (6, 7))]
                elif j < 4:
                    loads = [((e[0], e[1] - 1), 2 * j + n) for n in (4, 5)]
                else:
                    loads = [(e, 2 * (j - 4) + n) for n in (0, 1)] if j < 8 else []
                for of, n in loads:
                    sp.wait_ge(mod_summed, at(of, 12, n - MOD_SLOTS + 1))
                    load_piece(of, n)
            for n in range(MOD_SLOTS):
                load_piece((None, 0), n)
            load_weights(two, sp, beside=pieces)

        @block.tensor
        def _(pe):
            two_layer_products(two, k, pe, u_hi, u_lo)

        @block.scalar
        def _(act):
            def hidden(e):
                act.wait_ge(two.up_used, at(e, 4, 4))
                if not two.is_first(e):
                    act.wait_ge(two.hid_ready, at(e, 1))
                act.activation(two.hid[:], k.psum[:, 0:4, 0:T], ACT.Relu).then_inc(k.ft_free, 4)
                act.wait_ge(k.ft_free, at(e, 4, f0 + 8))
                act.activation(two.hid[:], two.hid[:], ACT.Square).then_inc(two.hid_act, 1)
                act.wait_ge(two.hid_act, at(e, 1, 1))
                act.activation(two.hid_hi[:, e[1] % 2], two.hid[:], ACT.Copy).then_inc(two.hid_high, 1)

            def scale_rows(e, ns):
                for n in ns:
                    slot, pair = n % MOD_SLOTS, (4 * (e[1] % 2) + n) % 8
                    act.wait_ge(k.mod_in[slot], at(e, 48, 16 * (n // MOD_SLOTS + 1)))
                    for c in range(2):
                        ins = act.activation(w_mod[:, slot, c, :], w_mod[:, slot, c, :], ACT.Copy,
                                             scale=c_silu[:, 2 * pair + c:2 * pair + c + 1])
                    ins.then_inc(mod_scaled, 1)

            def step(e):
                for j in range(2, 10):
                    high_part(two, k, act, t0, e, j)
                    if j == 5:
                        hidden(e)
                    elif j != 6:
                        n = 2 * (j - 2 if j < 5 else j - 4)
                        scale_rows(e, (n, n + 1))

            def first(e):
                for j in range(4, 10):
                    high_part(two, k, act, t0, e, j)
                    if j < 8:
                        scale_rows(e, range(3 * (j - 4), 3 * (j - 3)))
                hidden(e)
            run_steps(two, act, first, step, lambda e: [high_part(two, k, act, t0, e, j) for j in (2, 3)])

        @block.vector
        def _(dve):
            def gather(e, half):
                for n in (2 * half, 2 * half + 1):
                    dve.wait_ge(k.tt_done, at(e, 8, t0 - 8 + n + 1))
                    out = x[:, n % 2, half * COLS:(half + 1) * COLS]
                    dve.tensor_tensor(out, out, bank(k, 4 + (t0 + n) % 4), ALU.add).then_inc(k.tt_free, 1)

            def step(e):
                for j in (2, 3, 4, 5):
                    low_part(two, dve, e, j)
                hidden_low(two, dve, e)
                for half in range(4):
                    low_part(two, dve, e, 6 + half)
                    gather(e, half)

            def first(e):
                for j in range(4, 10):
                    low_part(two, dve, e, j)
                hidden_low(two, dve, e)

            def last(e):
                for half in range(4):
                    if half < 2:
                        low_part(two, dve, e, 2 + half)
                    gather(e, half)
            run_steps(two, dve, first, step, last)

        @block.gpsimd
        def _(pool):
            steps = Steps(pool, k.pool_sem)
            steps.n = 1
            sums = acc[:].rearrange("p g n -> p (g n)")

            def group(g):
                for j in range(8):
                    w = w_mod[:, j % MOD_SLOTS]
                    pool.wait_ge(mod_scaled, g * 8 + (j + 1))
                    if j:
                        steps.step(pool.tensor_tensor(w[:, 0, :], w[:, 0, :], w[:, 1, :], ALU.add))
                        steps.settle()
                        pool.tensor_tensor(part[:], part[:], w[:, 0, :], ALU.add).then_inc(mod_summed, 1)
                    else:
                        pool.tensor_tensor(part[:], w[:, 0, :], w[:, 1, :], ALU.add).then_inc(mod_summed, 1)
                    pool.wait_ge(mod_summed, g * 8 + (j + 1))
                steps.step(pool.tensor_tensor(spare[:], part[:, 0:1], part[:, 1:2], ALU.mult))
                out = sums[:, g * COLS:(g + 1) * COLS] if isinstance(g, int) else sums[:, bass.ds(g * COLS, COLS)]
                steps.step(pool.tensor_tensor(out, out, part[:], ALU.add))
                steps.settle()
            with pool.Fori(0, MOD_GROUPS) as g:
                steps.loop(g, 9)
                group(g)
            steps.end(MOD_GROUPS)
    k.ft += 4 * FFN_BLOCKS
    k.tt += 8 * FFN_BLOCKS


def modulation(nc, k, acc, gates, mod_cols, scale1, scale2):
    ones = const(k, "ones")
    s = k.dve_steps
    with nc.Block(no_gpsimd_drain=True) as block:
        @block.tensor
        def _(pe):
            for n, section in enumerate((0, 1, 3, 4)):
                for c in range(KC):
                    pe.matmul(bank(k, 0)[:, n * KC + c:n * KC + c + 1],
                              acc[:, section * 4 + c // 4, (c % 4) * P:(c % 4 + 1) * P], ones[:, 0:1],
                              start=True, stop=True)
            for n in range(4):
                pe.matmul(bank(k, 4 + n), ones, acc[:, 8 + n, :], start=True, stop=True)
    for gate in range(2):
        with nc.Block(no_gpsimd_drain=True) as block:
            @block.scalar
            def _(act):
                act.activation(gates[:, gate, :], k.psum[:, 4:8, :].rearrange("p b n -> p (b n)"), ACT.Copy)

            @block.vector
            def _(dve):
                s.eng = dve
                if not gate:
                    s.step(dve.tensor_copy(mod_cols[:], bank(k, 0)[:, 0:64]))
                    s.settle()
                    for dst, at, norm in ((scale1, 16, "norm1"), (scale2, 48, "norm2")):
                        s.step(dve.scalar_tensor_tensor(dst[:], mod_cols[:, at:at + 16], 1.0, cols_of(k, norm),
                                                        ALU.add, ALU.mult))
                    s.settle()
        if not gate:
            with nc.Block(no_gpsimd_drain=True) as block:
                @block.tensor
                def _(pe):
                    for n in range(4):
                        pe.matmul(bank(k, 4 + n), ones, acc[:, 20 + n, :], start=True, stop=True)


def final_norm(nc, k, io, x, weight, squares):
    s = k.dve_steps
    with nc.Block(no_gpsimd_drain=True) as block:
        @block.sync
        def _(sp):
            sp.dma_start(weight[:], io["final_norm"]).then_inc(k.small_in, 16)

        @block.scalar
        def _(act):
            for t in range(TT):
                act.activation(squares, x[:, t, :], ACT.Square, accum_out=k.ssq[:, t:t + 1]).then_inc(k.act_sem, 1)
                act.wait_ge(k.act_sem, k.act_n + t + 1)
            act.activation(k.rms[:], k.ssq[:], ACT.Sqrt, bias=k.eps[:, 0:1], scale=1.0 / D).then_inc(k.act_sem, 1)

        @block.vector
        def _(dve):
            s.eng = dve
            dve.wait_ge(k.act_sem, k.act_n + 3)
            dve.wait_ge(k.small_in, 64)
            s.step(dve.reciprocal(k.rstd[:], k.rms[:]))
            s.settle()
            for t in range(TT):
                s.step(dve.scalar_tensor_tensor(x[:, t, :], x[:, t, :], k.rstd[:, t:t + 1], weight[:],
                                                ALU.mult, ALU.mult))
            s.settle()
    k.act_n += 3


def second_mixer(nc, k, io, x, h_t, gate, scope_sb):
    s = k.dve_steps
    first, _ = STREAM["w_in_2"]
    proj = scope_sb("proj", [P, TT, 5 * COLS])
    ws, gm_norm = scope_sb("gm_ws", [P, GMLP_GROUPS, P]), scope_sb("gm_norm", [P, COLS])
    ssq = scope_sb("proj_ssq", [P, TT, 12])
    squares = scope_sb("squares", [P, TT, 3 * COLS])
    t0 = k.tt
    with nc.Block(no_gpsimd_drain=True) as block:
        @block.sync
        def _(sp):
            sp.dma_start(ws[:], io["gm_ws"]).then_inc(k.small_in, 16)
            sp.dma_start(gm_norm[:], io["gm_norm"]).then_inc(k.small_in, 16)
            for j in range(10):
                load_next(k, sp, first + j, k.tt_done, t0 + 2 * (j // 2 + 1))
            sp.wait_ge(k.small_in, 96)

        @block.tensor
        def _(pe):
            for g in range(5):
                token_group(k, pe, unit_rows(first + 2 * g, KC), h_t, range(KC), t0 + 2 * g)

        @block.scalar
        def _(act):
            for n in range(10):
                act.wait_ge(k.tt_done, t0 + n + 1)
                act.activation(proj[:, n % 2, (n // 2) * COLS:(n // 2 + 1) * COLS], bank(k, 4 + (t0 + n) % 4),
                               ACT.Gelu if n < 4 else ACT.Copy).then_inc(k.tt_free, 1)
    k.tt += 10
    with nc.Block(no_gpsimd_drain=True) as block:
        @block.vector
        def _(dve):
            s.eng = dve
            s.step(dve.tensor_tensor(squares[:], proj[:, :, COLS:4 * COLS], proj[:, :, COLS:4 * COLS], ALU.mult))
            s.step(dve.tensor_tensor(ws[:], ws[:], const(k, "tri_le").unsqueeze(1).broadcast_to([P, GMLP_GROUPS, P]),
                                     ALU.mult))
            s.settle()
            s.step(dve.tensor_reduce(ssq[:], squares[:].rearrange("p t (g n) -> p t g n", n=P), AX.X, ALU.add))
            s.settle()
    with nc.Block(no_gpsimd_drain=True) as block:
        @block.scalar
        def _(act):
            act.activation(ssq[:], ssq[:], ACT.Sqrt, bias=k.eps[:, 0:1], scale=1.0 / P)
    with nc.Block(no_gpsimd_drain=True) as block:
        @block.vector
        def _(dve):
            s.eng = dve
            s.step(dve.reciprocal(ssq[:], ssq[:]))
            s.settle()
            for t in range(TT):
                at = proj[:, t, COLS:4 * COLS].rearrange("p (g n) -> p g n", n=P)
                s.step(dve.tensor_tensor(at, at, ssq[:, t, :].unsqueeze(2).broadcast_to([P, 12, P]), ALU.mult))
            s.settle()
    qk_t = squares[:].rearrange("p t n -> p (t n)")[:, 0:2048].rearrange("p (a h n) -> p a h n", a=2, h=SB_HEADS)
    turn_blocks(nc, k, [([proj[:, t, (2 + a) * COLS + h * P:(2 + a) * COLS + (h + 1) * P] for h in range(SB_HEADS)],
                         qk_t[:, a, :, t * P:(t + 1) * P]) for a in range(2) for t in range(TT)])
    y = scope_sb("y", [P, TT, MIX_GROUPS, P])
    z, sp_, e = (scope_sb(n, [P, SB_HEADS, TT, T]) for n in ("sb_z", "sb_softplus", "sb_exp"))
    with nc.Block(no_gpsimd_drain=True) as block:
        @block.vector
        def _(dve):
            s.eng = dve
            s.step(dve.tensor_scalar(qk_t[:, 0], qk_t[:, 0], col(k, "q_norm"), P ** -0.5, ALU.mult, ALU.mult))
            s.step(dve.tensor_scalar(qk_t[:, 1], qk_t[:, 1], col(k, "k_norm"), None, ALU.mult))
            s.settle()

        @block.tensor
        def _(pe):
            for t in range(TT):
                for g in range(GMLP_GROUPS):
                    pe.matmul(bank(k, 4 + t)[:, g * P:(g + 1) * P], ws[:, g, :],
                              proj[:, t, COLS + g * P:COLS + (g + 1) * P], start=True, stop=True)
    with nc.Block(no_gpsimd_drain=True) as block:
        @block.tensor
        def _(pe):
            for h in range(SB_HEADS):
                for b in range(TT):
                    pe.matmul(bank(k, h)[:, b * T:(b + 1) * T], qk_t[:, 1, h, b * P:(b + 1) * P], qk_t[:, 0, h, :],
                              start=True, stop=True)

        @block.vector
        def _(dve):
            s.eng = dve
            for t in range(TT):
                s.step(dve.tensor_tensor(y[:, t, 0:4, :].rearrange("p g n -> p (g n)"), bank(k, 4 + t), gm_norm[:],
                                         ALU.mult))
            s.settle()
            for g in range(GMLP_GROUPS):
                s.step(dve.scalar_tensor_tensor(y[:, :, g, :], y[:, :, g, :], col(k, "gm_bs", g),
                                                proj[:, :, g * P:(g + 1) * P], ALU.add, ALU.mult))
            s.settle()
    zf, sf, ef = (a[:].rearrange("p h b q -> p (h b q)") for a in (z, sp_, e))
    before = const(k, "before").unsqueeze(1).broadcast_to([P, SB_HEADS, TT * T])

    def heads(a):
        return a[:].rearrange("p h b q -> p h (b q)")
    with nc.Block(no_gpsimd_drain=True) as block:
        @block.vector
        def _(dve):
            s.eng = dve
            ps = k.psum[:, 0:4, :].rearrange("p b n -> p (b n)")
            s.step(dve.tensor_copy(zf, ps))
            s.settle()
            s.step(dve.tensor_scalar(sf, zf, 0.0, None, ALU.max))
            s.settle()
            s.step(dve.scalar_tensor_tensor(ef, sf, -2.0, zf, ALU.mult, ALU.add))
            s.settle()
    with nc.Block(no_gpsimd_drain=True) as block:
        @block.scalar
        def _(act):
            act.activation(ef, ef, ACT.Exp).then_inc(k.act_sem, 1)
            act.wait_ge(k.act_sem, k.act_n + 1)
            act.activation(ef, ef, ACT.Ln, bias=k.one[:, 0:1])
    k.act_n += 1
    with nc.Block(no_gpsimd_drain=True) as block:
        @block.vector
        def _(dve):
            s.eng = dve
            s.step(dve.tensor_tensor(sf, sf, ef, ALU.add))
            s.settle()
            s.step(dve.tensor_tensor(zf, zf, sf, ALU.subtract))
            s.step(dve.tensor_tensor(heads(e), heads(sp_), before, ALU.mult))
            s.settle()
    with nc.Block(no_gpsimd_drain=True) as block:
        @block.tensor
        def _(pe):
            for h in range(SB_HEADS):
                pe.matmul(bank(k, h)[:, 0:T], const(k, "tri_gt"), e[:, h, 0, :], start=True, stop=False)
                pe.matmul(bank(k, h)[:, 0:T], const(k, "ones"), e[:, h, 1, :], start=False, stop=True)
                pe.matmul(bank(k, h)[:, T:2 * T], const(k, "tri_gt"), e[:, h, 1, :], start=True, stop=True)
    with nc.Block(no_gpsimd_drain=True) as block:
        @block.vector
        def _(dve):
            s.eng = dve
            s.step(dve.tensor_tensor(zf, zf, k.psum[:, 0:4, :].rearrange("p b n -> p (b n)"), ALU.subtract))
            s.settle()
    with nc.Block(no_gpsimd_drain=True) as block:
        @block.scalar
        def _(act):
            act.activation(zf, zf, ACT.Exp)
    with nc.Block(no_gpsimd_drain=True) as block:
        @block.vector
        def _(dve):
            s.eng = dve
            s.step(dve.tensor_tensor(heads(z), heads(z), before, ALU.mult))
            s.settle()
    with nc.Block(no_gpsimd_drain=True) as block:
        @block.tensor
        def _(pe):
            for t in range(TT):
                for h in range(SB_HEADS):
                    for b in range(t + 1):
                        pe.matmul(bank(k, t)[:, h * P:(h + 1) * P], z[:, h, b, t * P:(t + 1) * P],
                                  proj[:, b, 4 * COLS + h * P:4 * COLS + (h + 1) * P], start=(b == 0), stop=(b == t))
    y_ssq = scope_sb("y_ssq", [P, TT, MIX_GROUPS])
    y_sq = squares[:].rearrange("p t n -> p (t n)")[:, 0:2048].rearrange("p (t g n) -> p t g n", t=TT, n=P)
    with nc.Block(no_gpsimd_drain=True) as block:
        @block.vector
        def _(dve):
            s.eng = dve
            for t in range(TT):
                s.step(dve.tensor_copy(y[:, t, 4:8, :].rearrange("p g n -> p (g n)"), bank(k, t)))
            s.settle()
            s.step(dve.tensor_tensor(y_sq, y[:], y[:], ALU.mult))
            s.settle()
            s.step(dve.tensor_reduce(y_ssq[:], y_sq, AX.X, ALU.add))
            s.settle()
    with nc.Block(no_gpsimd_drain=True) as block:
        @block.scalar
        def _(act):
            act.activation(y_ssq[:], y_ssq[:], ACT.Sqrt, bias=k.eps[:, 0:1], scale=1.0 / P)
    with nc.Block(no_gpsimd_drain=True) as block:
        @block.vector
        def _(dve):
            s.eng = dve
            s.step(dve.reciprocal(y_ssq[:], y_ssq[:]))
            s.settle()
            s.step(dve.tensor_tensor(y[:], y[:], y_ssq[:].unsqueeze(3).broadcast_to([P, TT, MIX_GROUPS, P]), ALU.mult))
            s.settle()
    y_t = sf.rearrange("p (g t) -> p g t", t=T)
    turn_blocks(nc, k, [([y[:, t, 4 * g + c, :] for c in range(4)], y_t[:, 4 * g:4 * g + 4, t * P:(t + 1) * P])
                        for t in range(TT) for g in range(2)])
    with nc.Block(no_gpsimd_drain=True) as block:
        @block.vector
        def _(dve):
            s.eng = dve
            for g in range(MIX_GROUPS):
                s.step(dve.tensor_scalar(y_t[:, g, :], y_t[:, g, :], col(k, "out_norm", g), None, ALU.mult))
            s.settle()
    first, t0 = STREAM["w_out_2"][0], k.tt
    gated = ef.rearrange("p (n c) -> p n c", c=COLS)
    with nc.Block(no_gpsimd_drain=True) as block:
        @block.sync
        def _(sp):
            for j in range(4):
                load_next(k, sp, first + j, k.tt_done, t0 + 2 * (j + 1))

        @block.tensor
        def _(pe):
            for n in range(4):
                token_group(k, pe, unit_rows(first + n, MIX_GROUPS), y_t, range(MIX_GROUPS), t0 + 2 * n)

        @block.vector
        def _(dve):
            s.eng = dve
            for n in range(8):
                dve.wait_ge(k.tt_done, t0 + n + 1)
                own = slice((n // 2) * COLS, (n // 2 + 1) * COLS)
                dve.tensor_tensor(gated[:, n % 4, :], bank(k, 4 + (t0 + n) % 4), gate[:, own], ALU.mult)\
                   .then_inc(k.tt_free, 1)
                dve.wait_ge(k.tt_free, 4 + t0 + n + 1)
                s.step(dve.tensor_tensor(x[:, n % 2, own], x[:, n % 2, own], gated[:, n % 4, :], ALU.add))
            s.settle()
    k.tt += 8


def route(nc, k, io, h_t, comb, scope_sb):
    s = k.dve_steps
    w, b = scope_sb("w_route", [P, KC, 36]), scope_sb("b_route", [1, 36])
    logits = scope_sb("logits", [P, TT, 36])
    e4, m4 = scope_sb("group_exp", [P, TT, GROUPS]), scope_sb("group_mask", [P, TT, GROUPS])
    one, p_group = scope_sb("route_one", [P, TT, 1]), scope_sb("p_group", [P, TT])
    total = scope_sb("group_total", [P, TT])
    pick = scope_sb("pick", [P, TT, GROUPS, PER_GROUP])
    chosen, rest = scope_sb("chosen", [P, TT, PER_GROUP]), scope_sb("rest", [P, TT, PER_GROUP])
    tmp = scope_sb("route_tmp", [P, TT, PER_GROUP])
    hot = [scope_sb(f"hot{n}", [P, TT, PER_GROUP]) for n in range(2)]
    v = [scope_sb(f"top{n}", [P, TT, 1]) for n in range(2)]
    w1 = scope_sb("weight1", [P, TT, 1])
    with nc.Block(no_gpsimd_drain=True) as block:
        @block.sync
        def _(sp):
            sp.dma_start(w[:], io["w_route"]).then_inc(k.small_in, 16)
            sp.dma_start(b[:], io["b_route"]).then_inc(k.small_in, 16)

        @block.tensor
        def _(pe):
            pe.wait_ge(k.small_in, 128)
            for t in range(TT):
                ps = bank(k, t)[:, 0:36]
                for c in range(KC):
                    pe.matmul(ps, h_t[:, c, t * P:(t + 1) * P], w[:, c, :], start=(c == 0), stop=False)
                pe.matmul(ps, const(k, "ones")[0:1, :], b[:], start=False, stop=True)

    def first_hot(dve, dst, src, top, n, work):
        index = const(k, "index")[:, 0:n].unsqueeze(1).broadcast_to([P, TT, n])
        s.step(dve.tensor_tensor(dst, src, top.broadcast_to([P, TT, n]), ALU.is_ge))
        s.settle()
        s.step(dve.tensor_tensor(work, dst, index, ALU.mult))
        s.settle()
        s.step(dve.tensor_reduce(one[:], work, AX.X, ALU.min))
        s.settle()
        s.step(dve.tensor_tensor(dst, index, one[:].broadcast_to([P, TT, n]), ALU.is_equal))
        s.settle()
    with nc.Block(no_gpsimd_drain=True) as block:
        @block.vector
        def _(dve):
            s.eng = dve
            for t in range(TT):
                s.step(dve.tensor_copy(logits[:, t, :], bank(k, t)[:, 0:36]))
            s.settle()
            g = logits[:, :, 0:GROUPS]
            s.step(dve.tensor_reduce(v[0][:], g, AX.X, ALU.max))
            s.settle()
            s.step(dve.tensor_tensor(e4[:], g, v[0][:].broadcast_to([P, TT, GROUPS]), ALU.subtract))
            first_hot(dve, m4[:], g, v[0][:], GROUPS, tmp[:, :, 0:GROUPS])
            for t in range(TT):
                s.step(dve.tensor_tensor(pick[:, t], logits[:, t, GROUPS:].rearrange("p (g j) -> p g j", g=GROUPS),
                                         m4[:, t, :].unsqueeze(2).broadcast_to([P, GROUPS, PER_GROUP]), ALU.mult))
            s.settle()
            s.step(dve.tensor_reduce(chosen[:], pick[:].rearrange("p t g j -> p t j g"), AX.X, ALU.add))
            s.settle()
            s.step(dve.tensor_reduce(v[0][:], chosen[:], AX.X, ALU.max))
            s.settle()
            first_hot(dve, hot[0][:], chosen[:], v[0][:], PER_GROUP, tmp[:])
            s.step(dve.scalar_tensor_tensor(rest[:], hot[0][:], -3.0e38, chosen[:], ALU.mult, ALU.add))
            s.settle()
            s.step(dve.tensor_reduce(v[1][:], rest[:], AX.X, ALU.max))
            s.settle()
            first_hot(dve, hot[1][:], rest[:], v[1][:], PER_GROUP, tmp[:])
            s.step(dve.tensor_tensor(w1[:], v[1][:], v[0][:], ALU.subtract))
            s.settle()
    with nc.Block(no_gpsimd_drain=True) as block:
        @block.scalar
        def _(act):
            act.activation(w1[:], w1[:], ACT.Exp)
            for t in range(TT):
                act.activation(e4[:, t, :], e4[:, t, :], ACT.Exp, accum_out=total[:, t:t + 1])
    with nc.Block(no_gpsimd_drain=True) as block:
        @block.vector
        def _(dve):
            s.eng = dve
            s.step(dve.scalar_tensor_tensor(p_group[:], w1[:].rearrange("p t a -> p (t a)"), 1.0, total[:],
                                            ALU.add, ALU.mult))
            s.settle()
            s.step(dve.reciprocal(p_group[:], p_group[:]))
            for n in range(2):
                if n:
                    s.step(dve.tensor_tensor(hot[1][:], hot[1][:], w1[:].broadcast_to([P, TT, PER_GROUP]), ALU.mult))
            s.settle()
            s.step(dve.tensor_tensor(hot[0][:], hot[0][:], hot[1][:], ALU.add))
            s.settle()
            s.step(dve.tensor_tensor(hot[0][:], hot[0][:],
                                     p_group[:].unsqueeze(2).broadcast_to([P, TT, PER_GROUP]), ALU.mult))
            s.settle()
            for t in range(TT):
                s.step(dve.tensor_tensor(comb[:, t, :].rearrange("p (g j) -> p g j", g=GROUPS),
                                         hot[0][:, t, :].unsqueeze(1).broadcast_to([P, GROUPS, PER_GROUP]),
                                         m4[:, t, :].unsqueeze(2).broadcast_to([P, GROUPS, PER_GROUP]), ALU.mult))
            s.settle()


def experts(nc, k, two, h_hi, h_lo, comb, acc, silu):
    f0, t0, at = k.ft, k.tt, two.at
    with nc.Block(no_gpsimd_drain=True) as block:
        @block.sync
        def _(sp):
            load_weights(two, sp)

        @block.scalar
        def _(act):
            def gate(e):
                act.wait_ge(two.up_used, at(e, 4, 4))
                if not two.is_first(e):
                    act.wait_ge(two.hid_ready, at(e, 1))
                act.activation(silu[:], k.psum[:, 0:4:2, 0:T], ACT.Silu).then_inc(two.hid_act, 1)

            def step(e):
                for j in (2, 3, 4, 5):
                    high_part(two, k, act, t0, e, j)
                gate(e)
                for j in (6, 7):
                    high_part(two, k, act, t0, e, j)

            def first(e):
                for j in range(2, 8):
                    high_part(two, k, act, t0, e, j)
                gate(e)
            run_steps(two, act, first, step, lambda e: None)

        @block.vector
        def _(dve):
            def hidden(e):
                dve.wait_ge(two.hid_act, at(e, 1, 1))
                if not two.is_first(e):
                    dve.wait_ge(two.hid_ready, at(e, 1))
                dve.tensor_tensor(two.hid[:], silu[:], k.psum[:, 1:4:2, 0:T], ALU.mult).then_inc(k.ft_free, 4)
                dve.wait_ge(k.ft_free, at(e, 4, f0 + 8))
                dve.tensor_copy(two.hid_hi[:, e[1] % 2], two.hid[:]).then_inc(two.hid_high, 1)
                hidden_low(two, dve, e)

            def gather(e, tiles):
                for n in tiles:
                    dve.wait_ge(k.tt_done, at(e, 8, t0 - 8 + n + 1))
                    out = acc[:, n % 2, (n // 2) * COLS:(n // 2 + 1) * COLS]
                    expert = slice(e[1] - 1, e[1]) if e[0] is None else bass.ds(at(e, 1, -1), 1)
                    dve.scalar_tensor_tensor(out, bank(k, 4 + (t0 + n) % 4), comb[:, n % 2, expert],
                                             out, ALU.mult, ALU.add).then_inc(k.tt_free, 1)

            def step(e):
                for j in (2, 3, 4, 5):
                    low_part(two, dve, e, j)
                hidden(e)
                for h in range(2):
                    low_part(two, dve, e, 6 + h)
                    gather(e, range(4 * h, 4 * h + 4))

            def first(e):
                for j in range(2, 8):
                    low_part(two, dve, e, j)
                hidden(e)
            run_steps(two, dve, first, step, lambda e: gather(e, range(8)))

        @block.tensor
        def _(pe):
            two_layer_products(two, k, pe, h_hi, h_lo)
    k.ft += 4 * EXPERTS
    k.tt += 8 * EXPERTS


def finish(nc, k, io, x, acc, gate):
    s = k.dve_steps
    with nc.Block(no_gpsimd_drain=True) as block:
        @block.vector
        def _(dve):
            s.eng = dve
            for t in range(TT):
                s.step(dve.tensor_tensor(acc[:, t, :], acc[:, t, :], gate, ALU.mult))
                s.settle()
                dve.tensor_tensor(x[:, t, :], x[:, t, :], acc[:, t, :], ALU.add).then_inc(k.out_ready, 1)

        @block.sync
        def _(sp):
            for t in range(TT):
                sp.wait_ge(k.out_ready, t + 1)
                sp.dma_start(io["out"][t * P:(t + 1) * P, :], x[:, t, :]).then_inc(k.out_written, 16)
            sp.wait_ge(k.out_written, 16 * TT)


def program(nc, io):
    k = Kit(io["stream"])
    with ExitStack() as ctx:
        def sb(name, shape, scope=ctx, dtype=F32, side=None):
            return scope.enter_context(nc.sbuf_tensor(name, shape, dtype, side=side))

        def kept(name, shape, dtype=F32):
            return sb(name, shape, dtype=dtype, side="right")

        def sem(name):
            return ctx.enter_context(nc.semaphore(name))
        k.norm_ssq, k.norm_rms, k.norm_diag, k.norm_mm = \
            sem("norm_ssq"), sem("norm_rms"), sem("norm_diag"), sem("norm_mm")
        k.ft_done, k.ft_free, k.tt_done, k.tt_free = \
            sem("ft_done"), sem("ft_free"), sem("tt_done"), sem("tt_free")
        k.turned, k.turn_taken, k.gates_ready, k.inv_masked = \
            sem("turned"), sem("turn_taken"), sem("gates_ready"), sem("inv_masked")
        k.inv_first, k.inv_second, k.inv_taken, k.dve_sem = \
            sem("inv_first"), sem("inv_second"), sem("inv_taken"), sem("dve_sem")
        k.act_sem, k.pe_sem, k.pool_sem, k.consts_in = \
            sem("act_sem"), sem("pe_sem"), sem("pool_sem"), sem("consts_in")
        k.out_ready, k.out_written, k.small_in = \
            sem("out_ready"), sem("out_written"), sem("small_in")
        k.piece_high, k.piece_low, k.piece_used = sem("piece_high"), sem("piece_low"), sem("piece_used")
        k.loaded = [sem(f"loaded{n}") for n in range(SLOTS)]
        k.x_in, k.mem_in = ([sem(f"{what}{n}") for n in range(2)] for what in ("x_in", "mem_in"))
        k.mod_in = [sem(f"mod_in{n}") for n in range(MOD_SLOTS)]
        k.dve_steps = Steps(None, k.dve_sem)
        k.psum = ctx.enter_context(nc.psum_tensor("psum", [P, 8, 512], F32))
        k.consts = kept("consts", [P, N_KEPT])
        k.cols = kept("cols", [P, N_COLS])
        x = kept("x", [P, TT, D])
        k.diag = kept("diag", [P, TT, P])
        k.ssq, k.rms, k.rstd = kept("ssq", [P, TT]), kept("rms", [P, TT]), kept("rstd", [P, TT])
        k.eps, k.one = kept("eps", [P, 1]), kept("one", [P, 1])
        ring = ctx.enter_context(ExitStack())
        k.ring = sb("ring", [P, SLOTS, UNIT_KC, COLS], ring)
        k.stream_end = STREAM["w_in_2"][0]

        def begin(sp):
            sp.dma_start(k.consts[:], io["consts"][:, 0:N_KEPT]).then_inc(k.consts_in, 16)
            sp.dma_start(k.mixer_consts[:], io["consts"][:, N_KEPT:]).then_inc(k.consts_in, 16)
            sp.dma_start(k.cols[:], io["cols"]).then_inc(k.consts_in, 16)
            for t in range(TT):
                sp.dma_start(x[:, t, :], io["x"][t * P:(t + 1) * P, :]).then_inc(k.x_in[t], 16)
            for u in range(SLOTS):
                load_unit(k, sp, u, u)
            sp.wait_ge(k.consts_in, 48)
        with nc.Block(no_gpsimd_drain=True) as block:
            @block.vector
            def _(dve):
                dve.memset(k.eps[:], EPS)
                dve.memset(k.one[:], 1.0)

            @block.tensor
            def _(pe):
                pe.sem_inc(k.ft_free, 8)
                pe.sem_inc(k.ft_done, 4)
                pe.sem_inc(k.piece_used, 1)
                pe.sem_inc(k.tt_free, 4)
        with ExitStack() as mixer:
            k.mixer_consts = sb("mixer_consts", [P, N_CONST - N_KEPT], mixer, side="right")
            mixed = sb("mixed", [P, 16, T], mixer)
            u = sb("u", [P, KC, T], mixer)
            norm_turn(nc, k, x, u, lambda c: col(k, "mix_norm", c), sync=begin, await_src=k.x_in)
            with ExitStack() as dn:
                qkvz = sb("qkvz", [P, 32, T], dn)
                w_gate = sb("w_gate", [P, KC, 16], dn)
                with nc.Block(no_gpsimd_drain=True) as block:
                    @block.sync
                    def _(sp):
                        sp.dma_start(w_gate[:], io["w_gate"]).then_inc(k.small_in, 16)
                        sp.wait_ge(k.small_in, 16)
                with ExitStack() as split:
                    tiles = SplitTiles(k, STREAM["dn"][0], lambda n, shape, dtype: sb(n, shape, split, dtype), "dn")
                    tiles.split_input(nc, u)
                    deltanet_project(nc, k, tiles, qkvz)
                bufs = [sb(f"dn{n}", [P, TT, 8, P], dn) for n in range(4)]
                q_tm, k_tm, v_tm, kb_tm = bufs
                X = sb("dn_x", [P, 8, 2, P], dn)
                state = sb("dn_state", [P, 8, P], dn)
                k.beta, k.g, k.sp_pos = (sb(n, [P, TT, 8], dn) for n in ("beta", "g", "sp_pos"))
                k.a_exp, k.egc, k.o_ssq = sb("a_exp", [P, 8], dn), sb("egc", [P, 16], dn), sb("o_ssq", [P, 8], dn)
                k.qk_ssq = sb("qk_ssq", [P, 2, TT, 8], dn)
                k.scratch8 = X[:].rearrange("p h a n -> p (h a n)")
                k.inv_u, k.inv_w = q_tm[:, 0], q_tm[:, 1]
                k.inv_m, k.inv_p = kb_tm[:, 0], kb_tm[:, 1]
                KQ = qkvz[:, 0:16, :].rearrange("p (h t) (a n) -> p h t a n", t=TT, n=P)
                kT = qkvz[:, 16:24, :].rearrange("p h (t n) -> p h t n", n=P)
                deltanet_prepare(nc, k, u, qkvz, w_gate, q_tm, k_tm, v_tm, kb_tm, KQ, kT)
                for t in range(TT):
                    deltanet_tile(nc, k, t, v_tm, k_tm, KQ, kT, X, k.inv_m, k.inv_p, state, qkvz[:, 24:32, :], mixed)
            with ExitStack() as rw:
                mix = sb("rw_mix", [P, 26, T], rw)
                k.one_less_mu, k.one_less_ka = sb("one_less_mu", [P, 26], rw), sb("one_less_ka", [P, 8], rw)
                with ExitStack() as split:
                    tiles = SplitTiles(k, STREAM["rw"][0], lambda n, shape, dtype: sb(n, shape, split, dtype), "rw")
                    tiles.split_input(nc, u)
                    rwkv_project(nc, k, tiles, u, mix)
                AR = sb("rw_ar", [P, RW_TILES, TT, 2, P], rw)
                sig = sb("rw_sig", [P, TT, 1024], rw)
                neg, a_b, gate = (sb(n, [P, RW_TILES, T], rw) for n in ("rw_neg", "rw_ab", "rw_gate"))
                k.tanh = sb("rw_tanh", [P, T], rw)
                k.carry, k.y_mean, k.y_ssq = (sb(n, [P, 8], rw) for n in ("rw_carry", "rw_mean", "rw_ssq"))
                k.gn_eps = sb("gn_eps", [P, 1], rw)
                state = sb("rw_state", [P, RW_TILES, RW_DIM], rw)
                lora = AR[:].rearrange("p c t a n -> p (c t a n)")[:, 0:3072].rearrange("p (a n) -> p a n", a=3)
                with nc.Block(no_gpsimd_drain=True) as block:
                    @block.sync
                    def _(sp):
                        sp.dma_start(lora, io["lora"]).then_inc(k.small_in, 16)

                    @block.vector
                    def _(dve):
                        dve.memset(k.gn_eps[:], RW_GN_EPS)
                kk, scratch = u[:, 0:8, :], u[:, 8:16, :]
                rwkv_prepare(nc, k, mix, lora, AR, sig, neg, a_b, gate, kk, scratch, mixed[:, 8:16, :])
                X = mix[:, 0:8, :].rearrange("p h (a n) -> p h a n", a=2)
                v_tm = sig
                turn_blocks(nc, k, [([mix[:, 16 + 4 * g + c, t * P:(t + 1) * P] for c in range(4)],
                                     v_tm[:, t, 512 * g:512 * g + 512].rearrange("p (c n) -> p c n", n=P))
                                    for t in range(TT) for g in range(2)])
                Y = mix[:, 16:24, :].rearrange("p h (a n) -> p h a n", a=2)
                k.inv_u, k.inv_w, k.inv_m, k.inv_p = (u[:, 4 * n:4 * n + 4, :].rearrange("p a (b n) -> p (a b) n", n=P)
                                                      for n in range(4))
                flat = neg[:].rearrange("p c t -> p (c t)")
                b_tm, k_tm, R, U = (flat[:, 512 * n:512 * n + 512] for n in range(4))
                y, tmp = mix[:, 24:26, :].rearrange("p c t -> p (c t)"), sb("rw_tmp", [P, 512], rw)[:]
                for t in range(TT):
                    for half in range(2):
                        rwkv_batch(nc, k, t, half, X, Y, AR, a_b, mix[:, 8:16, :], v_tm, b_tm, k_tm, R, U, y, tmp,
                                   state, gate, mixed[:, 8:16, :])
            mixer_out(nc, k, mixed, x)
        with ExitStack() as xa:
            mem, h_t, mem_t = (sb(n, [P, TT, D], xa) for n in ("mem", "xa_h", "mem_t"))
            with nc.Block(no_gpsimd_drain=True) as block:
                @block.sync
                def _(sp):
                    for t in range(TT):
                        sp.dma_start(mem[:, t, :], io["mem"][t * P:(t + 1) * P, :]).then_inc(k.mem_in[t], 16)
            k.dve_steps_before = k.dve_steps.n
            cross_attention(nc, k, x, lambda n, shape: sb(n, shape, xa), mem, features(h_t), features(mem_t), k.mem_in)
        shared = kept("shared", [P, TT, D])
        mod_cols, scale1, scale2 = kept("mod_cols", [P, 64]), kept("scale1", [P, 16]), kept("scale2", [P, 16])
        ring.close()
        with ExitStack() as ffn:
            def ffn_sb(name, shape, dtype=F32):
                return sb(name, shape, ffn, dtype)
            two = TwoLayers(io["ffn"], FFN_BLOCKS, 4, 4, 2, ffn_sb, sem, "ffn")
            norm_turn(nc, k, x, features(shared), lambda c: col(k, "ffn_norm", c), sync=two.first_loads)
            two.buffers(ffn_sb, "ffn")
            u_hi, u_lo = (ffn_sb(n, [P, KC, T], F32R) for n in ("u_hi", "u_lo"))
            acc = ffn_sb("mod_acc", [P, MOD_COLS // COLS, COLS])
            part, spare, c_silu = ffn_sb("mod_part", [P, COLS]), ffn_sb("mod_spare", [P, 1]), ffn_sb("c_silu", [P, KC])
            w_mod = shared[:].rearrange("p t (s c n) -> p (t s) c n", c=2, n=COLS)
            mlp_and_modulation(nc, k, io, two, x, features(shared), u_hi, u_lo, acc, w_mod, part, spare, c_silu,
                               sem("mod_scaled"), sem("mod_summed"))
            modulation(nc, k, acc, shared, mod_cols, scale1, scale2)
            final_norm(nc, k, io, x, two.raw[:, 0], two.raw[:, 1])
        ring = ctx.enter_context(ExitStack())
        k.ring = sb("ring_2", [P, SLOTS, UNIT_KC, COLS], ring)
        k.stream_end = UNITS

        def refill(sp):
            for unit in range(STREAM["w_in_2"][0], STREAM["w_in_2"][0] + SLOTS):
                load_unit(k, sp, unit, unit % SLOTS)
        with ExitStack() as second:
            h_t = sb("h_t", [P, KC, T], second)
            norm_turn(nc, k, x, h_t, lambda c: scale1[:, c:c + 1], lambda c: mod_cols[:, c:c + 1], sync=refill)
            with ExitStack() as mixer:
                second_mixer(nc, k, io, x, h_t, shared[:, 0, :], lambda n, shape: sb(n, shape, mixer))
        ring.close()
        h_hi, h_lo = (kept(n, [P, KC, T], F32R) for n in ("h_hi", "h_lo"))
        comb, acc = kept("comb", [P, TT, EXPERTS]), kept("moe_acc", [P, TT, D])
        two = TwoLayers(io["moe"], EXPERTS, 2, 6, 3, sb, sem, "moe")
        with ExitStack() as routing:
            h_t = sb("h2_t", [P, KC, T], routing)
            norm_turn(nc, k, x, h_t, lambda c: scale2[:, c:c + 1], lambda c: mod_cols[:, 32 + c:33 + c],
                      sync=two.first_loads)
            with nc.Block(no_gpsimd_drain=True) as block:
                @block.scalar
                def _(act):
                    act.activation(h_hi[:], h_t[:], ACT.Copy)

                @block.vector
                def _(dve):
                    dve.memset(acc[:], 0.0)
            with nc.Block(no_gpsimd_drain=True) as block:
                @block.vector
                def _(dve):
                    dve.tensor_tensor(h_lo[:], h_t[:], h_hi[:].bitcast(F32), ALU.subtract)
            route(nc, k, io, h_t, comb, lambda n, shape: sb(n, shape, routing))
        two.buffers(lambda name, shape, dtype=F32: sb(name, shape, dtype=dtype), "moe")
        silu = sb("moe_silu", [P, 2, T])
        experts(nc, k, two, h_hi, h_lo, comb, acc, silu)
        finish(nc, k, io, x, acc, shared[:, 1, :])




def lay_out(a):
    def units(w, order):
        w = w.reshape(-1, UNIT_KC, P, w.shape[1] // COLS, COLS)
        w = w.transpose(3, 0, 2, 1, 4) if order == "columns" else w.transpose(0, 3, 2, 1, 4)
        return w.reshape(-1, P, UNIT)

    w_in = a["w_in"][0]
    dn_cols = 4 * 1024
    rw = w_in[:, dn_cols + 16:]
    parts = [units(w_in[:, :dn_cols], "columns"), units(rw[:, :3072], "columns"),
             rw[:, 3072:].reshape(KC, P, 256).transpose(1, 0, 2).reshape(1, P, UNIT),
             units(a["w_out"][0], "columns"), units(a["xa_wk"][0], "columns"), units(a["xa_wv"][0], "columns"),
             units(a["xa_wq"][0], "columns"),
             a["xa_wo"][0].reshape(2, 2, P, D).transpose(0, 2, 1, 3).reshape(2, P, UNIT)]
    parts += [units(a["w_in_2"][0], "columns"), units(a["w_out_2"][0], "columns")]
    stream = np.concatenate(parts)
    assert stream.shape == (UNITS, P, UNIT), stream.shape

    def two_layers(ups, downs):
        n, pieces = len(downs), D * downs.shape[1] // (P * HALF)
        ups = ups.reshape(n, 4, 4, P, COLS).transpose(0, 1, 3, 2, 4).reshape(n, 4, P, HALF)
        downs = downs.reshape(n, -1, P, pieces, D // pieces).transpose(0, 3, 2, 1, 4).reshape(n, pieces, P, HALF)
        return np.concatenate([ups[0]] + [h for e in range(1, n) for h in (ups[e], downs[e - 1])] + [downs[-1]])

    def tiles(v):
        return np.ascontiguousarray(v).reshape(-1, P).T
    cols = {
        "mix_norm": tiles(a["mix_norm_w"][0]),
        "conv": a["dn_conv_w"][0].reshape(4, DN_TILES, P).transpose(2, 1, 0).reshape(P, -1),
        "dn_norm": tiles(a["dn_norm_w"][0]), "mu": tiles(a["rw_mu"][0]), "a0": tiles(a["rw_a0"][0]),
        "k_k": tiles(a["rw_k_k"][0]), "k_a": tiles(a["rw_k_a"][0]), "r_k": tiles(a["rw_r_k"][0]),
        "ln_w": tiles(a["rw_ln_w"][0]), "ln_b": tiles(a["rw_ln_b"][0]), "xa_norm": tiles(a["xa_norm_w"][0]),
        "mem_norm": tiles(a["mem_norm_w"][0]), "ffn_norm": tiles(a["ffn_norm_w"][0]),
        "norm1": tiles(a["norm1_g_2"][0]), "norm2": tiles(a["norm2_g_2"][0]), "out_norm": tiles(a["out_norm_g_2"][0]),
        "q_norm": tiles(a["q_norm_g_2"][0]), "k_norm": tiles(a["k_norm_g_2"][0]), "gm_bs": a["gm_bs_2"][0].T,
        "c": tiles(a["c_2"][0]),
        "dn_gate": np.concatenate([np.broadcast_to(a["dn_a_log"][0], (P, 8)),
                                   np.broadcast_to(a["dn_dt_bias"][0], (P, 8))], 1),
    }
    cols = np.concatenate([cols[n] for n in COL], 1)
    m, j = np.arange(P)[:, None], np.arange(P)[None, :]
    levels = []
    for level in range(7):
        s = 1 << level
        levels.append((j // s % 2 == 1) & (m // s % 2 == 0) & (m // (2 * s) == j // (2 * s)))
    mid = m < P // 2
    consts = {
        "ident": m == j, "ones": m >= 0 * j, "tri_le": m <= j, "tri_gt": m > j, "levels": np.concatenate(levels, 1),
        "strict_incl": np.concatenate([m < j, m <= j], 1), "head_ones": m // RW_DIM == j // RW_DIM,
        "g_incl": (m <= j) * 1.0 - mid, "g_excl": (m < j) * 1.0 - mid, "g_pre": mid, "g_post": ~mid,
        "before": np.concatenate([m + P * b < np.arange(T)[None, :] for b in range(TT)], 1),
        "index": np.broadcast_to(np.arange(PER_GROUP) - 99.0, (P, PER_GROUP)),
    }
    consts = np.concatenate([np.asarray(consts[n], np.float32) for n in CONST], 1)
    lora = np.zeros((P, 3, 1024), np.float32)
    lora[0:64, 0], lora[64, 0] = a["rw_w2"][0], a["rw_w0"][0]
    lora[64:128, 1], lora[:, 2] = a["rw_a2"][0], a["rw_g2"][0]
    gate_up = np.stack([a["w_gate_2"][0].reshape(EXPERTS, D, 2, P), a["w_up_2"][0].reshape(EXPERTS, D, 2, P)], 3)
    moe = two_layers(gate_up.reshape(EXPERTS, D, COLS), a["w_down_2"][0])
    ffn = two_layers(a["ffn_w1"][0].reshape(D, FFN_BLOCKS, COLS).transpose(1, 0, 2),
                     a["ffn_w2"][0].reshape(FFN_BLOCKS, COLS, D))
    w_route = np.concatenate([a["w_group_2"][0], a["w_route_2"][0]], 1)
    return {
        "stream": stream, "ffn": ffn, "moe": moe, "cols": cols, "consts": consts, "x": a["x"][0], "mem": a["mem"][0],
        "w_gate": w_in[:, dn_cols:dn_cols + 16].reshape(KC, P, 16).transpose(1, 0, 2),
        "lora": lora,
        "w_mod": a["w_mod_2"].reshape(KC // 4, 4, P, MOD_COLS // COLS, COLS).transpose(3, 0, 2, 1, 4)
                              .reshape(-1, P, 4 * COLS),
        "b_mod": np.stack([a["b_mod_2"], a["mod_layer_2"][0]]),
        "final_norm": np.broadcast_to(a["final_norm_w"], (P, D)),
        "gm_norm": np.broadcast_to(a["gm_norm_g_2"][0], (P, 512)),
        "gm_ws": a["gm_ws_2"][0].transpose(2, 0, 1),
        "w_route": w_route.reshape(KC, P, 36).transpose(1, 0, 2),
        "b_route": np.concatenate([a["b_group_2"][0], a["b_route_2"][0]])[None],
    }


def kernel(**inputs):
    import concourse.bacc as bacc
    from concourse.bass_utils import run_bass_kernel_spmd

    nc = bacc.Bacc("TRN2", target_bir_lowering=False, num_devices=1)
    arrays = lay_out({n: np.asarray(v) for n, v in inputs.items()})
    arrays = {n: np.ascontiguousarray(v) for n, v in arrays.items()}
    io = {n: nc.dram_tensor("in_" + n, v.shape, mybir.dt.from_np(v.dtype), kind="ExternalInput").ap()
          for n, v in arrays.items()}
    io["out"] = nc.dram_tensor("out", (T, D), F32, kind="ExternalOutput").ap()
    program(nc, io)
    got = run_bass_kernel_spmd(nc, [{"in_" + n: v for n, v in arrays.items()}], core_ids=[0])
    return got.results[0]["out"].reshape(1, T, D)
```
